# Optimizing a Trainium2 kernel written in Bass

```python
import jax, jax.numpy as jnp
from jax import lax
import numpy as np

D_MODEL = 1024
BATCH = 1
SEQ = 2048
DEPTH = 2
DEC_BATCH = 8
DEC_SEQ = 16
PAST_LEN = 128

CHUNK = 64
N_PAST_CHUNKS = 8
PAST_BAND = N_PAST_CHUNKS * CHUNK
BAND = (N_PAST_CHUNKS + 1) * CHUNK
MIX_WIDTH = 3 * D_MODEL // 4
X_WIDTH = D_MODEL // 4
D_INNER = MIX_WIDTH + X_WIDTH
HD_A = 64
H_A = MIX_WIDTH // HD_A
REL_CLIP = 128
DK_B = 128
DV_B = 128
H_B = MIX_WIDTH // DK_B
H_X = 4
HD_X = X_WIDTH // H_X
N_MEM = 256
N_MIXERS = 2
N_A = (DEPTH + 1) // 2
N_B = DEPTH // 2
D_PROJ = 3 * MIX_WIDTH + X_WIDTH + D_INNER
EPS = 1e-6
NEG = -1e30
F32 = jnp.float32

kernel_name = 'hybrid_streaming_encoder_step'

def rmsnorm(x, g):
    x32 = x.astype(F32)
    y = x32 * lax.rsqrt(jnp.mean(x32 * x32, axis=-1, keepdims=True) + EPS)
    return (y * g.astype(F32)).astype(x.dtype)

def heads(t, h, d):
    return t.reshape(*t.shape[:-1], h, d)

def rel_bias_lookup(table, dist):
    idx = jnp.clip(dist, -REL_CLIP, REL_CLIP) + REL_CLIP
    return table[:, idx].astype(F32)

def band_attn_prompt(q, k, v, table):
    b, t = q.shape[:2]
    nc = t // CHUNK
    qc = q.reshape(b, nc, CHUNK, H_A, HD_A)
    pad = ((0, 0), (N_PAST_CHUNKS, 0), (0, 0), (0, 0), (0, 0))
    kp = jnp.pad(k.reshape(b, nc, CHUNK, H_A, HD_A), pad)
    vp = jnp.pad(v.reshape(b, nc, CHUNK, H_A, HD_A), pad)
    kb = jnp.concatenate([kp[:, j:j + nc] for j in range(N_PAST_CHUNKS + 1)], axis=2)
    vb = jnp.concatenate([vp[:, j:j + nc] for j in range(N_PAST_CHUNKS + 1)], axis=2)
    s = jnp.einsum('bcqhd,bckhd->bchqk', qc, kb).astype(F32) * (HD_A ** -0.5)
    dist = PAST_BAND + jnp.arange(CHUNK)[:, None] - jnp.arange(BAND)[None, :]
    s = s + rel_bias_lookup(table, dist)
    valid = (jnp.arange(BAND) // CHUNK)[None, :] >= (N_PAST_CHUNKS - jnp.arange(nc))[:, None]
    s = jnp.where(valid[None, :, None, None, :], s, NEG)
    p = jax.nn.softmax(s, axis=-1).astype(v.dtype)
    o = jnp.einsum('bchqk,bckhd->bcqhd', p, vb)
    return o.reshape(b, t, MIX_WIDTH)

def band_attn_sample(q, k, v, k_cache, v_cache, table):
    b, s_len = q.shape[:2]
    L = k_cache.shape[1]
    kk = jnp.concatenate([k_cache.astype(k.dtype), k], axis=1)
    vv = jnp.concatenate([v_cache.astype(v.dtype), v], axis=1)
    s = jnp.einsum('bqhd,bkhd->bhqk', q, kk).astype(F32) * (HD_A ** -0.5)
    dist = L + jnp.arange(s_len)[:, None] - jnp.arange(L + s_len)[None, :]
    s = s + rel_bias_lookup(table, dist)
    p = jax.nn.softmax(s, axis=-1).astype(v.dtype)
    o = jnp.einsum('bhqk,bkhd->bqhd', p, vv)
    return o.reshape(b, s_len, MIX_WIDTH)

def hgrn2_inputs(a, b, c, lb):
    q = heads(a, H_B, DK_B).astype(F32)
    z = heads(b, H_B, DK_B).astype(F32)
    i = heads(c, H_B, DV_B).astype(F32)
    lbh = lb.reshape(H_B, DK_B)
    log_f = jnp.logaddexp(jnp.log(lbh), jnp.log1p(-lbh) + jax.nn.log_sigmoid(z))
    k = (1.0 - lbh) * jax.nn.sigmoid(-z)
    return q, k, i, log_f

def hgrn2_block(S, q, k, i, log_f):
    t = q.shape[1]
    A = jnp.cumsum(log_f, axis=1)
    causal = jnp.tril(jnp.ones((t, t), dtype=bool))
    diff = A[:, :, None] - A[:, None, :]
    decay = jnp.exp(jnp.where(causal[None, :, :, None, None], diff, -jnp.inf))
    attn = jnp.einsum('bthk,btshk,bshk->bhts', q, decay, k)
    o = jnp.einsum('bhts,bshv->bthv', attn, i) + jnp.einsum('bthk,bhkv->bthv', q * jnp.exp(A), S)
    a_last = A[:, -1]
    S_new = jnp.exp(a_last)[..., None] * S + jnp.einsum('bshk,bshv->bhkv', k * jnp.exp(a_last[:, None] - A), i)
    return S_new, o

def hgrn2_prompt(q, k, i, log_f):
    b, t = q.shape[:2]
    nb = t // CHUNK

    def to_blocks(u):
        return u.reshape(b, nb, CHUNK, *u.shape[2:]).swapaxes(0, 1)

    S0 = jnp.zeros((b, H_B, DK_B, DV_B), F32)
    S, o = lax.scan(lambda S, xs: hgrn2_block(S, *xs), S0,
                    (to_blocks(q), to_blocks(k), to_blocks(i), to_blocks(log_f)))
    return S, o.swapaxes(0, 1).reshape(b, t, H_B, DV_B)

def hgrn2_out(o, g, dtype):
    o = rmsnorm(o, g.reshape(H_B, DV_B))
    return o.reshape(*o.shape[:-2], MIX_WIDTH).astype(dtype)

def mem_kv(mem, g, w):
    kv = rmsnorm(mem, g) @ w
    return heads(kv[..., :X_WIDTH], H_X, HD_X), heads(kv[..., X_WIDTH:], H_X, HD_X)

def cross_attn(q, mk, mv):
    s = jnp.einsum('bthd,bmhd->bhtm', q, mk.astype(q.dtype)).astype(F32) * (HD_X ** -0.5)
    p = jax.nn.softmax(s, axis=-1).astype(q.dtype)
    o = jnp.einsum('bhtm,bmhd->bthd', p, mv.astype(q.dtype))
    return o.reshape(*o.shape[:-2], X_WIDTH)

def in_proj(x, g, w):
    p = rmsnorm(x, g) @ w
    m = MIX_WIDTH
    return (p[..., :m], p[..., m:2 * m], p[..., 2 * m:3 * m],
            heads(p[..., 3 * m:3 * m + X_WIDTH], H_X, HD_X), p[..., 3 * m + X_WIDTH:])

def out_proj(x, mix_o, xq, mk, mv, gate, w):
    y = jnp.concatenate([mix_o, cross_attn(xq, mk, mv)], axis=-1) * jax.nn.silu(gate)
    return x + y @ w

def setup_inputs(seed: int = 0) -> dict:
    key = jax.random.key(seed)
    ks = jax.random.split(key, 18)
    band_len = min(PAST_BAND, PAST_LEN)

    def nrm(k, shape, s=1.0):
        return s * jax.random.normal(k, shape, F32)

    return {
        'x_prompt': nrm(ks[0], (BATCH, SEQ, D_MODEL)),
        'x_sample': nrm(ks[1], (DEC_BATCH, DEC_SEQ, D_MODEL)),
        'cache_a_k': nrm(ks[2], (N_A, DEC_BATCH, band_len, H_A, HD_A)),
        'cache_a_v': nrm(ks[3], (N_A, DEC_BATCH, band_len, H_A, HD_A)),
        'state_b': nrm(ks[4], (N_B, DEC_BATCH, H_B, DK_B, DV_B), 0.3),
        'cache_mem_k': nrm(ks[5], (DEPTH, DEC_BATCH, N_MEM, H_X, HD_X)),
        'cache_mem_v': nrm(ks[6], (DEPTH, DEC_BATCH, N_MEM, H_X, HD_X)),
        'mem_prompt': nrm(ks[7], (BATCH, N_MEM, D_MODEL)),
        'ln_g': 1.0 + nrm(ks[8], (DEPTH, D_MODEL), 0.02),
        'w_in': nrm(ks[9], (DEPTH, D_MODEL, D_PROJ), D_MODEL ** -0.5),
        'w_out': nrm(ks[10], (DEPTH, D_INNER, D_MODEL), D_INNER ** -0.5),
        'rel_bias_table': nrm(ks[11], (N_A, H_A, 2 * REL_CLIP + 1), 0.5),
        'lower_bounds': nrm(ks[12], (N_B, MIX_WIDTH)),
        'hgrn_norm_g': 1.0 + nrm(ks[13], (N_B, MIX_WIDTH), 0.02),
        'mem_norm_g': 1.0 + nrm(ks[14], (DEPTH, D_MODEL), 0.02),
        'w_mem_kv': nrm(ks[15], (DEPTH, D_MODEL, 2 * X_WIDTH), D_MODEL ** -0.5),
        'final_g': 1.0 + nrm(ks[16], (D_MODEL,), 0.02),
    }

def reference(x_prompt, x_sample, cache_a_k, cache_a_v, state_b, cache_mem_k, cache_mem_v, mem_prompt,
              ln_g, w_in, w_out, rel_bias_table, lower_bounds, hgrn_norm_g, mem_norm_g, w_mem_kv, final_g):
    lb_all = jnp.cumsum(jax.nn.softmax(lower_bounds.astype(F32), axis=0), axis=0)
    lb_all = lb_all - lb_all[:1]
    xp, xs = x_prompt, x_sample
    ak_p, av_p, sb_p, mk_pl, mv_pl, ak_s, av_s, sb_s = [], [], [], [], [], [], [], []
    for l in range(DEPTH):
        j = l // N_MIXERS
        mk_p, mv_p = mem_kv(mem_prompt, mem_norm_g[l], w_mem_kv[l])
        a_p, b_p, c_p, xq_p, g_p = in_proj(xp, ln_g[l], w_in[l])
        a_s, b_s, c_s, xq_s, g_s = in_proj(xs, ln_g[l], w_in[l])
        if l % N_MIXERS == 0:
            k_p, v_p = heads(b_p, H_A, HD_A), heads(c_p, H_A, HD_A)
            o_p = band_attn_prompt(heads(a_p, H_A, HD_A), k_p, v_p, rel_bias_table[j])
            k_s, v_s = heads(b_s, H_A, HD_A), heads(c_s, H_A, HD_A)
            o_s = band_attn_sample(heads(a_s, H_A, HD_A), k_s, v_s, cache_a_k[j], cache_a_v[j], rel_bias_table[j])
            keep = min(PAST_BAND, k_p.shape[1])
            ak_p.append(k_p[:, -keep:])
            av_p.append(v_p[:, -keep:])
            ak_s.append(k_s)
            av_s.append(v_s)
        else:
            S_p, o = hgrn2_prompt(*hgrn2_inputs(a_p, b_p, c_p, lb_all[j]))
            o_p = hgrn2_out(o, hgrn_norm_g[j], xp.dtype)
            S_s, o = hgrn2_block(state_b[j].astype(F32), *hgrn2_inputs(a_s, b_s, c_s, lb_all[j]))
            o_s = hgrn2_out(o, hgrn_norm_g[j], xs.dtype)
            sb_p.append(S_p.astype(xp.dtype))
            sb_s.append(S_s.astype(state_b.dtype))
        xp = out_proj(xp, o_p, xq_p, mk_p, mv_p, g_p, w_out[l])
        xs = out_proj(xs, o_s, xq_s, cache_mem_k[l], cache_mem_v[l], g_s, w_out[l])
        mk_pl.append(mk_p)
        mv_pl.append(mv_p)
    y_prompt = rmsnorm(xp, final_g)
    y_sample = rmsnorm(xs, final_g)
    return (y_prompt, y_sample, jnp.stack(ak_p), jnp.stack(av_p), jnp.stack(sb_p), jnp.stack(mk_pl), jnp.stack(mv_pl),
            jnp.stack(ak_s), jnp.stack(av_s), jnp.stack(sb_s))


_drawn_inputs = setup_inputs


def setup_inputs(seed=0):
    import zlib

    import numpy as np

    out = dict(_drawn_inputs(seed))
    spreads = {}
    factors = {'hgrn_norm_g': 6.024, 'mem_norm_g': 2.773, 'final_g': 2.858}
    for name, (base, spread) in spreads.items():
        noise = np.random.default_rng([zlib.crc32(name.encode()), seed]).standard_normal(out[name].shape)
        drawn = base * np.exp(spread * noise) if base else spread * noise
        out[name] = __import__('jax').numpy.asarray(drawn.astype(out[name].dtype))
    for name, factor in factors.items():
        out[name] = (out[name] * factor).astype(out[name].dtype)
    return out
```

```python
from contextlib import ExitStack

import concourse.bass as bass
from concourse import mybir

F32 = mybir.dt.float32
F32R = mybir.dt.float32r
U32 = mybir.dt.uint32
ALU = mybir.AluOpType
ACT = mybir.ActivationFunctionType
AX_X = mybir.AxisListType.X

P = 128
D = 1024
KD = D // P
SEQ = 2048
NT = SEQ // P
TS = NT
NTOK = SEQ + P
SB, SL = 8, 16
MIX = 768
MG = MIX // P
HA, HD = 12, 64
HX = 4
NMEM = 256
XW = HX * HD
NG = (3 * MIX + XW + D) // P
CHUNK = 64
BAND = 640
CLIP = 128
EPS = 1e-6
DEPTH = 2
BIG = 1e30
GQ, GK, GV, GX, GG = 0, MG, 2 * MG, 3 * MG, 3 * MG + 2
BLOCKS = [(0, 512), (512, 512), (1024, 384), (1408, 384), (1792, 384)]
NBLK = len(BLOCKS)


def wait(eng, sem, value):
    if not (isinstance(value, int) and value <= 0):
        eng.wait_ge(sem, value)


def counted(eng, value):
    return value if isinstance(value, int) else eng.to_reg(value)


def sweep(eng, first, last, per, body):
    n = (last - first) // per
    for r in range(min(per, last - first)):
        body(first + r, r)
    if n > 1:
        with eng.Fori(1, n) as i:
            for r in range(per):
                body(i * per + (first + r), r)
    for r in range(n * per if n else last - first, last - first):
        body(first + r, r % per)


class Semaphores:

    def __init__(self, nc, software):
        self.nc, self.held, self.ctx, self._software = nc, [], ExitStack(), software

    def __enter__(self):
        return self

    def __call__(self, name):
        self.held.append(self.ctx.enter_context(self.nc.semaphore(name)))
        return self.held[-1]

    def software(self, name):
        return self._software.enter_context(self.nc.semaphore(name))

    def __exit__(self, *error):
        if error[0] is None:
            with self.nc.Block() as block:
                @block.gpsimd
                def _(pool):
                    for s in self.held:
                        pool.sem_clear(s)
        self.ctx.close()


class Chain:

    def __init__(self, eng, sem):
        self.eng, self.sem, self.n = eng, sem, 0

    def __call__(self, ins):
        self.n += 1
        ins.then_inc(self.sem, 1)
        self.eng.wait_ge(self.sem, self.n)


def hybrid_encoder(nc, x_prompt, x_sample, cache_a_k, cache_a_v, state_b, cache_mem_k, cache_mem_v, mem_prompt,
                   ln_g, w_in, w_out, rel_bias_table, lower_bounds, hgrn_norm_g, mem_norm_g, w_mem_kv, final_g,
                   y_prompt, y_sample, a_k_prompt, a_v_prompt, b_state_prompt, mem_k_prompt, mem_v_prompt,
                   a_k_sample, a_v_sample, b_state_sample):
    top = ExitStack()
    with top, nc.allow_non_contiguous_dma(reason="channel vectors onto partitions, and the small bias table"):
        def dram(name, shape):
            return nc.dram_tensor(name, shape, F32, kind="Internal").ap()

        def sb_in(ctx):
            return lambda name, shape, dt=F32: ctx.enter_context(nc.sbuf_tensor(name, shape, dt))

        def ps_in(ctx):
            return lambda name, shape, dt=F32: ctx.enter_context(nc.psum_tensor(name, shape, dt))

        software = top.enter_context(ExitStack())
        sb = sb_in(top)
        proj = dram("proj", (NG, P, NTOK))
        kgate = dram("kgate", (MG, P, NTOK))
        x_mid = dram("x_mid", (NT + 1, P, D))
        ext = dram("ext", (HA, P, 768))

        ident = sb("ident", [P, P])
        g_ln = sb("g_ln", [P, 2, KD])
        g_mem = sb("g_mem", [P, 2, KD])
        g_hgrn = sb("g_hgrn", [P, MG])
        lb = sb("lb", [P, MG])
        lb1 = sb("lb1", [P, MG])
        neg_half = sb("neg_half", [P, 16])
        seqmask = sb("seqmask", [P, SB])
        mem_kT = sb("mem_kT", [P, 2, 2, NMEM])
        mem_v = sb("mem_v", [P, 2, 2, XW])

        xp_t = x_prompt.rearrange("b (t p) d -> (b t) p d", p=P)
        xs_t = x_sample.rearrange("b s d -> (b s) d")

        with Semaphores(nc, software) as sem:
            setup(nc, sem, sb_in, ps_in, locals())
        for l in range(DEPTH):
            def x_of(t):
                if l:
                    return x_mid[t]
                return xs_t if isinstance(t, int) and t == TS else xp_t[t]
            with ExitStack() as ctx:
                xh = sb_in(ctx)(f"xh{l}", [P, KD, NTOK], F32R)
                xl = sb_in(ctx)(f"xl{l}", [P, KD, NTOK], F32R)
                with Semaphores(nc, software) as sem:
                    norm_transpose(nc, l, sem, sb_in, ps_in, x_of, ident, neg_half, xh, xl)
                    project(nc, l, sem, sb_in, ps_in, xh, xl, w_in, g_ln, lb, lb1, proj, kgate)
            if l == 0:
                with Semaphores(nc, software) as sem:
                    keys_out(nc, sem, sb_in, ps_in, ident, proj, a_k_prompt, a_v_prompt, a_k_sample, a_v_sample)
            mix(nc, l, software, sb_in, ps_in, locals())


def setup(nc, sem, sb_in, ps_in, v):
    ident, g_ln, g_mem, g_hgrn, lb, lb1 = (v[n] for n in ("ident", "g_ln", "g_mem", "g_hgrn", "lb", "lb1"))
    neg_half, seqmask, mem_kT, mem_v, ext = (v[n] for n in ("neg_half", "seqmask", "mem_kT", "mem_v", "ext"))
    mem_k_prompt, mem_v_prompt = v["mem_k_prompt"], v["mem_v_prompt"]
    s_cols, s_tab, s_mem, s_ext, s_out = (sem(f"su_{n}") for n in ("cols", "tab", "mem", "ext", "out"))
    s_wkv = [sem(f"su_wkv{i}") for i in range(2)]
    c_pool, c_dve, s_const, s_extv = (sem(f"su_{n}") for n in ("cpool", "cdve", "const", "extv"))
    s_sq, s_ms, s_rs, s_xn, s_tp, s_ev, s_wg, s_kv, s_kvev, s_kt, s_ktev, s_lbx, s_lbe = (
        sem(f"su_{n}") for n in ("sq", "ms", "rs", "xn", "tp", "ev", "wg", "kv", "kvev", "kt", "ktev", "lbx", "lbe"))
    with ExitStack() as ctx:
        sb, ps = sb_in(ctx), ps_in(ctx)
        tab = sb("tab", [HA, 2 * CLIP + 1])
        extv = sb("extv", [HA, 768])
        xm = sb("xm", [P, 2, D])
        sq = sb("sq", [P, D])
        ss = sb("ss", [P, 2])
        ms = sb("ms", [P, 2])
        rs = sb("rs", [P, 2])
        xn = sb("xn", [P, 2, D])
        xT = sb("xT", [P, KD, NMEM])
        wkv = sb("wkv", [P, 2, KD, 2 * XW])
        kv = sb("kv", [P, 4, 2 * XW])
        lbraw = sb("lbraw", [P, MG])
        lbd = sb("lbd", [P, MG])
        lbe = sb("lbe", [P, MG])
        lbr = sb("lbr", [P, MG])
        TP = [ps(f"suTP{i}", [P, 512]) for i in range(4)]
        KV = [ps(f"suKV{i}", [P, 512]) for i in range(4)]
        with nc.Block() as block:
            @block.sync
            def _(sp):
                sp.dma_start(xm[:], v["mem_prompt"].rearrange("b (t p) d -> p (b t) d", p=P)).then_inc(s_mem, 16)
                for l in range(2):
                    sp.dma_start(wkv[:, l], v["w_mem_kv"][l].rearrange("(k p) n -> p k n", p=P)).then_inc(s_wkv[l], 16)
                sp.wait_ge(s_extv, 1)
                sp.dma_start(ext, extv[:].unsqueeze(1).to_broadcast([HA, P, 768])).then_inc(s_ext, 16)
                for i in range(4):
                    l, t = divmod(i, 2)
                    sp.wait_ge(s_kvev, i + 1)
                    rows = slice(t * P, (t + 1) * P)
                    for out, cols in ((mem_k_prompt, slice(0, XW)), (mem_v_prompt, slice(XW, 2 * XW))):
                        sp.dma_start(out[l, 0, rows].rearrange("p h d -> p (h d)"), kv[:, i, cols]).then_inc(s_out, 16)
                sp.wait_ge(s_out, 128)
                sp.wait_ge(s_ext, 16)

            @block.scalar
            def _(act):
                act.dma_start(tab[:], v["rel_bias_table"][0]).then_inc(s_tab, 16)
                for l in range(2):
                    act.dma_start(g_ln[:, l], v["ln_g"][l].rearrange("(k p) -> p k", p=P)).then_inc(s_cols, 16)
                    act.dma_start(g_mem[:, l], v["mem_norm_g"][l].rearrange("(k p) -> p k", p=P)).then_inc(s_cols, 16)
                act.dma_start(g_hgrn[:], v["hgrn_norm_g"][0].rearrange("(k p) -> p k", p=P)).then_inc(s_cols, 16)
                act.dma_start(lbraw[:], v["lower_bounds"][0].rearrange("(k p) -> p k", p=P)).then_inc(s_cols, 16)
                act.wait_ge(s_mem, 16)
                for t in range(2):
                    nc.scalar.activation(sq[:], xm[:, t], ACT.Square, accum_out=ss[:, t:t + 1]).then_inc(s_sq, 1)
                    if t == 0:
                        act.wait_ge(s_sq, 1)
                act.wait_ge(s_lbx, 1)
                nc.scalar.activation(lbe[:], lbd[:], ACT.Exp).then_inc(s_lbe, 1)
                for i in range(4):
                    act.wait_ge(s_tp, i + 1)
                    t, half = divmod(i, 2)
                    nc.scalar.copy(xT[:, half * 4:half * 4 + 4, t * P:(t + 1) * P],
                                   TP[i][:].rearrange("p (k n) -> p k n", n=P)).then_inc(s_ev, 1)
                for i in range(4):
                    l, t = divmod(i, 2)
                    act.wait_ge(s_kv, i + 1)
                    nc.scalar.copy(kv[:, i], KV[i][:]).then_inc(s_kvev, 1)
                for i in range(4):
                    l, t = divmod(i, 2)
                    act.wait_ge(s_kt, i + 1)
                    nc.scalar.copy(mem_kT[:, l, :, t * P:(t + 1) * P],
                                   TP[i][:, 0:2 * P].rearrange("p (g n) -> p g n", n=P)).then_inc(s_ktev, 1)

            @block.gpsimd
            def _(pool):
                link = Chain(pool, c_pool)
                link(nc.gpsimd.memset(ident[:], 0.0))
                link(nc.gpsimd.affine_select(out=ident[:], in_=ident[:], compare_op=ALU.not_equal, fill=1.0,
                                             base=0, pattern=[[-1, P]], channel_multiplier=1))
                link(nc.gpsimd.memset(seqmask[:], 1.0))
                link(nc.gpsimd.affine_select(out=seqmask[:], in_=seqmask[:], compare_op=ALU.is_ge, fill=0.0,
                                             base=0, pattern=[[-SL, SB]], channel_multiplier=1))
                link(nc.gpsimd.affine_select(out=seqmask[:], in_=seqmask[:], compare_op=ALU.is_ge, fill=0.0,
                                             base=SL - 1, pattern=[[SL, SB]], channel_multiplier=-1))
                nc.gpsimd.memset(neg_half[:], -0.5).then_inc(s_const, 1)
                pool.wait_ge(s_const, 1)
                pool.wait_ge(s_ms, 1)
                nc.gpsimd.tensor_tensor(rs[:], ms[:], neg_half[:, 0:2], ALU.pow).then_inc(s_rs, 1)

            @block.vector
            def _(dve):
                link = Chain(dve, c_dve)
                dve.wait_ge(s_cols, 96)
                nc.vector.tensor_tensor(lbd[:], lbraw[:], lbraw[:], ALU.subtract).then_inc(s_lbx, 1)
                dve.wait_ge(s_tab, 16)
                link(nc.vector.memset(extv[:], 0.0))
                link(nc.vector.tensor_scalar(extv[:, 0:511], extv[:, 0:511], tab[:, 2 * CLIP:2 * CLIP + 1], None, ALU.subtract))
                back = bass.AP(tab[:].tensor, 2 * CLIP, [[2 * CLIP + 1, HA], [-1, 2 * CLIP]])
                nc.vector.tensor_scalar(extv[:, 511:511 + 2 * CLIP], back, -1.0, None, ALU.mult).then_inc(s_extv, 1)
                dve.wait_ge(s_lbe, 1)
                link(nc.vector.reciprocal(lbr[:], lbe[:]))
                link(nc.vector.tensor_tensor(lb[:], lbe[:], lbr[:], ALU.mult))
                link(nc.vector.tensor_tensor(lb[:], lb[:], lb[:], ALU.subtract))
                link(nc.vector.tensor_scalar(lb1[:], lb[:], -1.0, 1.0, ALU.mult, ALU.add))
                dve.wait_ge(s_sq, 2)
                nc.vector.tensor_scalar(ms[:], ss[:], 1.0 / D, EPS, ALU.mult, ALU.add).then_inc(s_ms, 1)
                dve.wait_ge(s_rs, 1)
                for t in range(2):
                    nc.vector.tensor_scalar(xn[:, t], xm[:, t], rs[:, t:t + 1], None, ALU.mult).then_inc(s_xn, 1)
                for l in range(2):
                    dve.wait_ge(s_wkv[l], 16)
                    nc.vector.tensor_tensor(wkv[:, l], wkv[:, l],
                                            g_mem[:, l].unsqueeze(2).to_broadcast([P, KD, 2 * XW]),
                                            ALU.mult).then_inc(s_wg, 1)
                for i in range(4):
                    l, t = divmod(i, 2)
                    dve.wait_ge(s_kvev, i + 1)
                    nc.vector.tensor_copy(mem_v[:, l, t], kv[:, i, XW:2 * XW]).then_inc(c_dve, 1)

            @block.tensor
            def _(pe):
                pe.wait_ge(c_pool, 2)
                for t in range(2):
                    pe.wait_ge(s_xn, t + 1)
                    for k in range(KD):
                        ins = nc.tensor.transpose(TP[2 * t + k // 4][:, (k % 4) * P:(k % 4 + 1) * P],
                                                  xn[:, t, k * P:(k + 1) * P], ident[:])
                        if k % 4 == 3:
                            ins.then_inc(s_tp, 1)
                pe.wait_ge(s_ev, 4)
                for i in range(4):
                    l, t = divmod(i, 2)
                    pe.wait_ge(s_wg, l + 1)
                    for k in range(KD):
                        ins = nc.tensor.matmul(KV[i][:], xT[:, k, t * P:(t + 1) * P], wkv[:, l, k],
                                               start=(k == 0), stop=(k == KD - 1))
                    ins.then_inc(s_kv, 1)
                for i in range(4):
                    pe.wait_ge(s_kvev, i + 1)
                    for g in range(2):
                        ins = nc.tensor.transpose(TP[i][:, g * P:(g + 1) * P], kv[:, i, g * P:(g + 1) * P], ident[:])
                    ins.then_inc(s_kt, 1)


def norm_transpose(nc, l, sem, sb_in, ps_in, x_of, ident, neg_half, xh, xl):
    s_in = [sem(f"nt{l}_in{i}") for i in range(2)]
    s_sq, s_ms, s_rs, s_xn, s_tp, s_hi, s_lo = (sem(f"nt{l}_{n}") for n in ("sq", "ms", "rs", "xn", "tp", "hi", "lo"))
    with ExitStack() as ctx:
        sb, ps = sb_in(ctx), ps_in(ctx)
        xt = [sb(f"nt{l}_x{i}", [P, D]) for i in range(2)]
        xn = [sb(f"nt{l}_xn{i}", [P, D]) for i in range(2)]
        sq = sb(f"nt{l}_sq", [P, D])
        ss = sb(f"nt{l}_ss", [P, 2])
        ms = sb(f"nt{l}_ms", [P, 2])
        rs = sb(f"nt{l}_rs", [P, 2])
        TP = [[ps(f"nt{l}_tp{i}{h}", [P, 512]) for h in range(2)] for i in range(2)]
        with nc.Block() as block:
            @block.sync
            def _(sp):
                def body(t, p):
                    wait(sp, s_xn, t - 1)
                    sp.dma_start(xt[p][:], x_of(t)).then_inc(s_in[p], 16)
                sweep(sp, 0, NT, 2, body)
                body(TS, TS % 2)

            def square(act, t, p):
                act.wait_ge(s_in[p], in_count(t, p))
                wait(act, s_ms, t - 1)
                wait(act, s_sq, t)
                nc.scalar.activation(sq[:], xt[p][:], ACT.Square, accum_out=ss[:, p:p + 1]).then_inc(s_sq, 1)

            def in_count(t, p):
                return (t - p) * 8 + 16

            @block.scalar
            def _(act):
                square(act, 0, 0)

                def body(t, p, last=False):
                    if not last:
                        square(act, t + 1, 1 - p)
                    for h in range(2):
                        act.wait_ge(s_tp, t * 2 + (h + 1))
                        nc.scalar.copy(xh[:, 4 * h:4 * h + 4, bass.ds(t * P, P)],
                                       TP[p][h][:].rearrange("p (k n) -> p k n", n=P)).then_inc(s_hi, 1)
                sweep(act, 0, NT, 2, body)
                body(TS, TS % 2, last=True)

            @block.gpsimd
            def _(pool):
                def body(t, p):
                    pool.wait_ge(s_ms, t + 1)
                    wait(pool, s_xn, t - 1)
                    nc.gpsimd.tensor_tensor(rs[:, p:p + 1], ms[:, p:p + 1], neg_half[:, 0:1], ALU.pow).then_inc(s_rs, 1)
                sweep(pool, 0, NT, 2, body)
                body(TS, TS % 2)

            @block.vector
            def _(dve):
                def norm(t, p):
                    dve.wait_ge(s_sq, t + 1)
                    wait(dve, s_rs, t - 1)
                    nc.vector.tensor_scalar(ms[:, p:p + 1], ss[:, p:p + 1], 1.0 / D, EPS, ALU.mult, ALU.add).then_inc(s_ms, 1)
                    dve.wait_ge(s_rs, t + 1)
                    wait(dve, s_tp, t * 2 - 2)
                    nc.vector.tensor_scalar(xn[p][:], xt[p][:], rs[:, p:p + 1], None, ALU.mult).then_inc(s_xn, 1)
                norm(0, 0)

                def body(t, p, last=False):
                    if not last:
                        norm(t + 1, 1 - p)
                    for h in range(2):
                        dve.wait_ge(s_hi, t * 2 + (h + 1))
                        nc.vector.tensor_tensor(xl[:, 4 * h:4 * h + 4, bass.ds(t * P, P)],
                                                TP[p][h][:].rearrange("p (k n) -> p k n", n=P),
                                                xh[:, 4 * h:4 * h + 4, bass.ds(t * P, P)].bitcast(F32),
                                                ALU.subtract).then_inc(s_lo, 1)
                sweep(dve, 0, NT, 2, body)
                body(TS, TS % 2, last=True)

            @block.tensor
            def _(pe):
                def body(t, p):
                    pe.wait_ge(s_xn, t + 1)
                    wait(pe, s_lo, t * 2 - 2)
                    for k in range(KD):
                        ins = nc.tensor.transpose(TP[p][k // 4][:, (k % 4) * P:(k % 4 + 1) * P],
                                                  xn[p][:, k * P:(k + 1) * P], ident[:])
                        if k % 4 == 3:
                            ins.then_inc(s_tp, 1)
                sweep(pe, 0, NT, 2, body)
                body(TS, TS % 2)


def project(nc, l, sem, sb_in, ps_in, xh, xl, w_in, g_ln, lb, lb1, proj, kgate):
    s_w = sem.software(f"pj{l}_w")
    s_wg, s_wh, s_wl, s_mm, s_free, s_stage, s_sig, s_act = (
        sem(f"pj{l}_{n}") for n in ("wg", "wh", "wl", "mm", "free", "stage", "sig", "act"))
    s_st = [sem(f"pj{l}_st{b}") for b in range(NBLK)]
    s_st2 = [sem(f"pj{l}_st2{b}") for b in range(NBLK)]
    plain, gate, forget = "plain", "gate", "forget"
    if l == 0:
        parts = [(GQ, GK, plain, -HD ** -0.5), (GK, GX, plain, 1.0), (GX, GG, plain, -HD ** -0.5), (GG, NG, gate, 1.0)]
    else:
        parts = [(GQ, GK, plain, 1.0), (GK, GV, forget, 1.0), (GV, GX, plain, 1.0), (GX, GG, plain, -HD ** -0.5),
                 (GG, NG, gate, 1.0)]
    with ExitStack() as ctx:
        sb, ps = sb_in(ctx), ps_in(ctx)
        wraw = sb(f"pj{l}_wraw", [P, KD, 2 * P])
        wg = sb(f"pj{l}_wg", [P, KD, P])
        wh = [sb(f"pj{l}_wh{i}", [P, KD, P], F32R) for i in range(2)]
        wl = [sb(f"pj{l}_wl{i}", [P, KD, P], F32R) for i in range(2)]
        stage = [sb(f"pj{l}_stg{b}", [P, BLOCKS[b][1]]) for b in range(NBLK)]
        stage2 = [sb(f"pj{l}_stg2{b}", [P, BLOCKS[b][1]]) for b in range(NBLK)]
        acc = [ps(f"pj{l}_acc{b}", [P, 512]) for b in range(NBLK)]
        w_pairs = w_in[l].rearrange("(k p) (c n) -> c p k n", p=P, n=2 * P)
        with nc.Block() as block:
            @block.gpsimd
            def _(pool):
                def body(i, _):
                    wait(pool, s_wg, i * 2)
                    pool.dma_start(wraw[:], w_pairs[i]).then_inc(s_w, 16)
                sweep(pool, 0, NG // 2, 1, body)

            @block.sync
            def _(sp):
                for lo, hi, kind, _ in parts:
                    def body(c, _):
                        for b, (at, n) in enumerate(BLOCKS):
                            sp.wait_ge(s_stage, c * NBLK + (b + 1))
                            sp.dma_start(proj[c][:, at:at + n], stage[b][:]).then_inc(s_st[b], 16)
                            if kind == forget:
                                sp.dma_start(kgate[c - GK][:, at:at + n], stage2[b][:]).then_inc(s_st2[b], 16)
                    sweep(sp, lo, hi, 1, body)
                for b in range(NBLK):
                    sp.wait_ge(s_st[b], 16 * NG)
                    if l == 1:
                        sp.wait_ge(s_st2[b], 16 * MG)

            @block.scalar
            def _(act):
                def high(c, p):
                    act.wait_ge(s_wg, c + 1)
                    wait(act, s_mm, (c - 1) * NBLK)
                    nc.scalar.copy(wh[p][:], wg[:]).then_inc(s_wh, 1)
                high(0, 0)
                for lo, hi, kind, scale in parts:
                    def body(c, p):
                        if not (isinstance(c, int) and c == NG - 1):
                            high(c + 1, 1 - p)
                        for b, (at, n) in enumerate(BLOCKS):
                            act.wait_ge(s_mm, c * NBLK + (b + 1))
                            wait(act, s_st[b], c * 16)
                            if kind == plain:
                                nc.scalar.mul(stage[b][:], acc[b][:, 0:n], scale).then_inc(s_stage, 1)
                            elif kind == gate:
                                nc.scalar.activation(stage[b][:], acc[b][:, 0:n], ACT.Sigmoid).then_inc(s_sig, 1)
                            else:
                                if not (isinstance(c, int) and c == GK):
                                    act.wait_ge(s_st2[b], (c - GK) * 16)
                                nc.scalar.activation(stage[b][:], acc[b][:, 0:n], ACT.Sigmoid)
                                nc.scalar.activation(stage2[b][:], acc[b][:, 0:n], ACT.Sigmoid, scale=-1.0).then_inc(s_sig, 1)
                    if hi == NG:
                        sweep(act, lo, hi - 2, 2, body)
                        body(hi - 2, 0)
                        body(hi - 1, 1)
                    else:
                        sweep(act, lo, hi, 2, body)

            @block.vector
            def _(dve):
                def low(c, p):
                    wait(dve, s_w, (c - p) * 8 + 16)
                    wait(dve, s_wl, c)
                    nc.vector.tensor_tensor(wg[:], wraw[:, :, p * P:(p + 1) * P],
                                            g_ln[:, l].unsqueeze(2).to_broadcast([P, KD, P]), ALU.mult).then_inc(s_wg, 1)
                    dve.wait_ge(s_wh, c + 1)
                    nc.vector.tensor_tensor(wl[p][:], wg[:], wh[p][:].bitcast(F32), ALU.subtract).then_inc(s_wl, 1)
                low(0, 0)
                seen = 0
                for lo, hi, kind, _ in parts:
                    def body(c, p):
                        if not (isinstance(c, int) and c == NG - 1):
                            low(c + 1, 1 - p)
                        if kind == plain:
                            return
                        for b, (at, n) in enumerate(BLOCKS):
                            dve.wait_ge(s_sig, (c - lo + seen) * NBLK + (b + 1))
                            if kind == gate:
                                nc.vector.tensor_tensor(stage[b][:], acc[b][:, 0:n], stage[b][:], ALU.mult).then_inc(s_stage, 1)
                            else:
                                g = bass.ds(c - GK, 1)
                                nc.vector.tensor_scalar(stage2[b][:], stage2[b][:], lb1[:, g], None, ALU.mult)
                                nc.vector.tensor_scalar(stage[b][:], stage[b][:], lb1[:, g], lb[:, g],
                                                        ALU.mult, ALU.add).then_inc(s_stage, 1)
                    if hi == NG:
                        sweep(dve, lo, hi - 2, 2, body)
                        body(hi - 2, 0)
                        body(hi - 1, 1)
                    else:
                        sweep(dve, lo, hi, 2, body)
                    if kind != plain:
                        seen += hi - lo

            @block.tensor
            def _(pe):
                def body(c, p):
                    pe.wait_ge(s_wl, c + 1)
                    for b, (at, n) in enumerate(BLOCKS):
                        wait(pe, s_stage, c * NBLK - NBLK + (b + 1))
                        for k in range(KD):
                            for w, x in ((wh, xh), (wl, xh), (wh, xl)):
                                ins = nc.tensor.matmul(acc[b][:, 0:n], w[p][:, k], x[:, k, at:at + n],
                                                       start=(k == 0 and x is xh and w is wh),
                                                       stop=(k == KD - 1 and x is xl))
                        ins.then_inc(s_mm, 1)
                sweep(pe, 0, NG, 2, body)


def keys_out(nc, sem, sb_in, ps_in, ident, proj, a_k_prompt, a_v_prompt, a_k_sample, a_v_sample):
    s_in = [sem(f"ko_in{i}") for i in range(2)]
    s_out = [sem.software(f"ko_out{i}") for i in range(2)]
    s_tp, s_ev = sem("ko_tp"), sem("ko_ev")
    jobs = [(g, t) for t in range(NT - 4, NT + 1) for g in (GK, GV)]
    with ExitStack() as ctx:
        sb, ps = sb_in(ctx), ps_in(ctx)
        src = [sb(f"ko_src{i}", [P, MG, P]) for i in range(2)]
        dst = [sb(f"ko_dst{i}", [P, MIX]) for i in range(2)]
        TP = [[ps(f"ko_tp{i}{h}", [P, 512]) for h in range(2)] for i in range(2)]
        with nc.Block() as block:
            @block.sync
            def _(sp):
                for n, (g, t) in enumerate(jobs):
                    wait(sp, s_tp, n - 1)
                    sp.dma_start(src[n % 2][:], proj[g:g + MG, :, t * P:(t + 1) * P].rearrange("g p n -> p g n")
                                 ).then_inc(s_in[n % 2], 16)

            @block.gpsimd
            def _(pool):
                for n, (g, t) in enumerate(jobs):
                    pool.wait_ge(s_ev, 2 * n + 2)
                    if t == TS:
                        out = (a_k_sample if g == GK else a_v_sample)[0].rearrange("b s h d -> (b s) (h d)")
                    else:
                        r = (t - (NT - 4)) * P
                        out = (a_k_prompt if g == GK else a_v_prompt)[0, 0, r:r + P].rearrange("p h d -> p (h d)")
                    pool.dma_start(out, dst[n % 2][:]).then_inc(s_out[n % 2], 16)
                for i in range(2):
                    pool.wait_ge(s_out[i], 16 * (len(jobs) // 2))

            @block.tensor
            def _(pe):
                for n in range(len(jobs)):
                    pe.wait_ge(s_in[n % 2], 16 * (n // 2 + 1))
                    wait(pe, s_ev, 2 * n - 2)
                    for g in range(MG):
                        ins = nc.tensor.transpose(TP[n % 2][g // 3][:, (g % 3) * P:(g % 3 + 1) * P], src[n % 2][:, g], ident[:])
                    ins.then_inc(s_tp, 1)

            @block.vector
            def _(dve):
                for n in range(len(jobs)):
                    dve.wait_ge(s_tp, n + 1)
                    wait(dve, s_out[n % 2], 16 * (n // 2))
                    for h in range(2):
                        nc.vector.tensor_copy(dst[n % 2][:, h * 384:(h + 1) * 384], TP[n % 2][h][:, 0:384]).then_inc(s_ev, 1)


class Unit:

    def __init__(self, col, tiles, split, score, bias, pv):
        self.col, self.tiles, self.split, self.score, self.bias, self.pv = col, tiles, split, score, bias, pv
        self.width = tiles * P


def tp_cols(unit, i):
    return i * P if i < unit.split else 512 + (i - unit.split) * P


def unit_scores(nc, unit, sc):
    for cols, rows, q, k in unit.score:
        ins = nc.tensor.matmul(sc[rows, cols], q, k, start=True, stop=True)
    return ins


def unit_min(nc, unit, sc, se, minimum):
    n = unit.width
    if unit.bias is None:
        return nc.vector.tensor_reduce(minimum, sc[:, 0:n], AX_X, ALU.min)
    return nc.vector.tensor_tensor_reduce(se[:, 0:n], sc[:, 0:n], unit.bias, 1.0, 3e38, ALU.add, ALU.min, minimum)


def unit_exp(nc, unit, sc, se, minimum, total):
    src = sc if unit.bias is None else se
    return nc.scalar.activation(se[:, 0:unit.width], src[:, 0:unit.width], ACT.Exp, bias=minimum, scale=-1.0,
                                accum_out=total)


def unit_transposes(nc, unit, se, tp, ident):
    for i in range(unit.tiles):
        at = tp_cols(unit, i)
        ins = nc.tensor.transpose(tp[:, at:at + P], se[:, i * P:(i + 1) * P], ident[:])
    return ins


def unit_evac_low(unit, copy, pt, tp):
    if unit.tiles == 1:
        return copy(pt[0:64, 0:P], tp[0:64, 0:P])
    return copy(pt[:, 0:unit.split * P], tp[:, 0:unit.split * P])


def unit_evac_high(unit, copy, pt, tp):
    if unit.tiles == 1:
        return copy(pt[64:P, 0:P], tp[64:P, 0:P])
    n = (unit.tiles - unit.split) * P
    return copy(pt[:, unit.split * P:unit.width], tp[:, 512:512 + n])


def unit_pv(nc, unit, pt, ob):
    first = {}
    last = {}
    for n, (rows, *_) in enumerate(unit.pv):
        first.setdefault(rows.start, n)
        last[rows.start] = n
    for n, (rows, i, cols, val) in enumerate(unit.pv):
        ins = nc.tensor.matmul(ob[rows, unit.col:unit.col + HD], pt[:, i * P + cols.start:i * P + cols.stop], val,
                               start=first[rows.start] == n, stop=last[rows.start] == n)
    return ins


ALL = slice(0, P)


def cross_unit(col, h, q, keys, vals):
    g, po = h // 2, HD * (h % 2)
    return Unit(col, 2, 1, [(slice(0, NMEM), ALL, q[po:po + HD, g], keys[po:po + HD, g])], None,
                [(ALL, i, ALL, vals[:, i, h * HD:(h + 1) * HD]) for i in range(2)])


def sample_attention(nc, name, sem, sb_in, ps_in, ident, units_of, loads, o_s, bias_width, extra=None):
    s_ld, s_tp, s_eva, s_evd, s_sc, s_min, s_exp, s_pv, s_rs, s_bias = (
        sem(f"{name}_{n}") for n in ("ld", "tp", "eva", "evd", "sc", "min", "exp", "pv", "rs", "bias"))
    with ExitStack() as ctx:
        sb, ps = sb_in(ctx), ps_in(ctx)
        bufs, dmas, turns = loads(sb)
        se = [sb(f"{name}_se{i}", [P, bias_width]) for i in range(2)]
        pt = [sb(f"{name}_pt{i}", [P, bias_width]) for i in range(2)]
        mn = sb(f"{name}_mn", [P, 16])
        tot = sb(f"{name}_tot", [P, 16])
        rs = sb(f"{name}_rs", [P, 16])
        SC = [ps(f"{name}_SC{i}", [P, 1024]) for i in range(2)]
        TP = ps(f"{name}_TP", [P, 1024])
        OB = ps(f"{name}_OB", [P, 1024])
        units = units_of(bufs)
        U, NR = len(units), len(turns)
        o_cols = slice(units[0].col, units[-1].col + HD)
        with nc.Block() as block:
            @block.sync
            def _(sp):
                for out, src in dmas:
                    sp.dma_start(out, src).then_inc(s_ld, 16)

            @block.gpsimd
            def _(pool):
                pool.wait_ge(s_ld, 16 * len(dmas))
                if extra:
                    extra(bufs, pool, s_bias)

            @block.tensor
            def _(pe):
                pe.wait_ge(s_ld, 16 * len(dmas))
                for n, (srcs, _) in enumerate(turns):
                    wait(pe, s_eva, n)
                    wait(pe, s_evd, n)
                    for i, src in enumerate(srcs):
                        at = i % (len(srcs) // 2) * P + 512 * (i // (len(srcs) // 2))
                        ins = nc.tensor.transpose(TP[:, at:at + P], src, ident[:])
                    ins.then_inc(s_tp, 1)

                def scores(u):
                    wait(pe, s_exp, u - 1)
                    unit_scores(nc, units[u], SC[u % 2]).then_inc(s_sc, 1)

                def values(u):
                    pe.wait_ge(s_eva, NR + u + 1)
                    pe.wait_ge(s_evd, NR + u + 1)
                    unit_pv(nc, units[u], pt[u % 2], OB).then_inc(s_pv, 1)
                pe.wait_ge(s_eva, NR)
                pe.wait_ge(s_evd, NR)
                scores(0)
                scores(1)
                for u in range(U):
                    pe.wait_ge(s_exp, u + 1)
                    wait(pe, s_eva, NR + u)
                    wait(pe, s_evd, NR + u)
                    unit_transposes(nc, units[u], se[u % 2], TP, ident).then_inc(s_tp, 1)
                    if u:
                        values(u - 1)
                    if u + 2 < U:
                        scores(u + 2)
                values(U - 1)

            @block.vector
            def _(dve):
                def low_min(u):
                    dve.wait_ge(s_sc, u + 1)
                    unit_min(nc, units[u], SC[u % 2], se[u % 2], mn[:, u:u + 1]).then_inc(s_min, 1)
                for n, (srcs, dst) in enumerate(turns):
                    dve.wait_ge(s_tp, n + 1)
                    half = len(srcs) // 2
                    nc.vector.tensor_copy(dst[1], TP[:, 512:512 + half * P].rearrange("p (g n) -> p g n", n=P)
                                          ).then_inc(s_evd, 1)
                if extra:
                    dve.wait_ge(s_bias, 1)
                low_min(0)
                low_min(1)
                for u in range(U):
                    dve.wait_ge(s_tp, NR + u + 1)
                    unit_evac_high(units[u], nc.vector.tensor_copy, pt[u % 2], TP).then_inc(s_evd, 1)
                    if u + 2 < U:
                        low_min(u + 2)
                dve.wait_ge(s_pv, U)
                nc.vector.reciprocal(rs[:, 0:U], tot[:, 0:U]).then_inc(s_rs, 1)
                dve.wait_ge(s_rs, 1)
                for c in range(o_cols.start, o_cols.stop, 256):
                    u0 = (c - o_cols.start) // HD
                    nc.vector.tensor_tensor(o_s[:, c:c + 256].rearrange("p (h d) -> p h d", d=HD),
                                            OB[:, c:c + 256].rearrange("p (h d) -> p h d", d=HD),
                                            rs[:, u0:u0 + 4].unsqueeze(2).to_broadcast([P, 4, HD]), ALU.mult)

            @block.scalar
            def _(act):
                def exp(u):
                    act.wait_ge(s_min, u + 1)
                    unit_exp(nc, units[u], SC[u % 2], se[u % 2], mn[:, u:u + 1], tot[:, u:u + 1]).then_inc(s_exp, 1)
                for n, (srcs, dst) in enumerate(turns):
                    act.wait_ge(s_tp, n + 1)
                    half = len(srcs) // 2
                    nc.scalar.copy(dst[0], TP[:, 0:half * P].rearrange("p (g n) -> p g n", n=P)).then_inc(s_eva, 1)
                exp(0)
                exp(1)
                for u in range(U):
                    act.wait_ge(s_tp, NR + u + 1)
                    unit_evac_low(units[u], nc.scalar.copy, pt[u % 2], TP).then_inc(s_eva, 1)
                    if u + 2 < U:
                        exp(u + 2)


def halves(h, po, g, q, keys, new, vals, vnew, tiles, split, bias, col):
    score, pv = [], []
    n = tiles - (1 if new is not None else 0)
    for half in range(2):
        rows = slice(64 * half, 64 * half + 64)
        for at in range(0, n * P, 512):
            score.append((slice(at, at + 512), rows, q[po:po + HD, g, rows], keys[po:po + HD, g, n * P * half + at:n * P * half + at + 512]))
    if new is not None:
        score.append((slice(n * P, n * P + P), ALL, q[po:po + HD, g], new[po:po + HD, g]))
    for half in range(2):
        rows = slice(64 * half, 64 * half + 64)
        for i in range(tiles):
            v = vals[:, n * half + i, h * HD:(h + 1) * HD] if i < n else vnew[:, h * HD:(h + 1) * HD]
            pv.append((rows, i, rows, v))
    return Unit(col, tiles, split, score, bias, pv)


def sample_band(nc, sem, sb_in, ps_in, v, o_s):
    ident, proj, ext, seqmask = v["ident"], v["proj"], v["ext"], v["seqmask"]
    ck = v["cache_a_k"][0].rearrange("b s h d -> s b (h d)")
    cv = v["cache_a_v"][0].rearrange("b s h d -> s b (h d)")
    vn = v["a_v_sample"][0].rearrange("b s h d -> (b s) (h d)")
    tok = slice(SEQ, NTOK)

    def loads(sb):
        raw = sb("sa_raw", [P, SB, MIX])
        kT = sb("sa_kT", [P, MG, SB * P])
        vals = sb("sa_v", [P, SB, MIX])
        knew = sb("sa_knew", [P, MG, P])
        vnew = sb("sa_vnew", [P, MIX])
        q = sb("sa_q", [P, MG, P])
        tb = sb("sa_tb", [P, HA, P])
        tn = sb("sa_tn", [P, HA, SL])
        bias = sb("sa_bias", [P, HA, 5 * P])
        off = sb("sa_off", [P, 4])
        offn = sb("sa_offn", [P, SB])
        dmas = [(raw[:], ck), (vals[:], cv),
                (q[:], proj[GQ:GQ + MG, :, tok].rearrange("g p n -> p g n")),
                (knew[:], proj[GK:GK + MG, :, tok].rearrange("g p n -> p g n")), (vnew[:], vn)]
        for b in range(SB):
            rows = slice(b * SL, (b + 1) * SL)
            dmas.append((tb[rows], bass.AP(ext.tensor, 511, [[767, SL], [P * 768, HA], [1, P]])))
            dmas.append((tn[rows], bass.AP(ext.tensor, 639, [[767, SL], [P * 768, HA], [1, SL]])))
        turns = [([raw[:, b, g * P:(g + 1) * P] for g in range(MG)],
                  (kT[:, 0:3, b * P:(b + 1) * P], kT[:, 3:6, b * P:(b + 1) * P])) for b in range(SB)]
        return (kT, vals, knew, vnew, q, tb, tn, bias, off, offn), dmas, turns

    def units_of(bufs):
        kT, vals, knew, vnew, q, tb, tn, bias, off, offn = bufs
        return [halves(h, HD * (h % 2), h // 2, q, kT, knew, vals, vnew, 5, 3, bias[:, h], h * HD) for h in range(HA)]

    def extra(bufs, pool, s_bias):
        kT, vals, knew, vnew, q, tb, tn, bias, off, offn = bufs
        link = Chain(pool, sem("sa_cpool"))
        link(nc.gpsimd.tensor_tensor(off[:], seqmask[:, 0:4], seqmask[:, 4:8], ALU.add))
        link(nc.gpsimd.tensor_scalar(off[:], off[:], -BIG, BIG, ALU.mult, ALU.add))
        link(nc.gpsimd.tensor_scalar(offn[:], seqmask[:], -BIG, BIG, ALU.mult, ALU.add))
        for i in range(4):
            nc.gpsimd.tensor_scalar(bias[:, :, i * P:(i + 1) * P], tb[:], off[:, i:i + 1], None, ALU.add)
        for b in range(SB):
            ins = nc.gpsimd.tensor_scalar(bias[:, :, 4 * P + b * SL:4 * P + (b + 1) * SL], tn[:], offn[:, b:b + 1], None,
                                          ALU.add)
        ins.then_inc(s_bias, 1)

    sample_attention(nc, "sa", sem, sb_in, ps_in, ident, units_of, loads, o_s, 5 * P, extra)


def sample_cross(nc, l, sem, sb_in, ps_in, v, o_s):
    ident, proj, seqmask = v["ident"], v["proj"], v["seqmask"]
    ck = v["cache_mem_k"][l].rearrange("b (t p) h d -> p (b t) (h d)", p=P)
    cv = v["cache_mem_v"][l].rearrange("b (t p) h d -> p (b t) (h d)", p=P)
    name = f"sx{l}"

    def loads(sb):
        raw = sb(f"{name}_raw", [P, 2 * SB, XW])
        kT = sb(f"{name}_kT", [P, 2, 2 * SB * P])
        vals = sb(f"{name}_v", [P, 2 * SB, XW])
        q = sb(f"{name}_q", [P, 2, P])
        off = sb(f"{name}_off", [P, 4])
        bias = sb(f"{name}_bias", [P, 4, 2 * P])
        dmas = [(raw[:], ck), (vals[:], cv), (q[:], proj[GX:GX + 2, :, SEQ:NTOK].rearrange("g p n -> p g n"))]
        turns = [([raw[:, 2 * b + t, g * P:(g + 1) * P] for g in range(2) for t in range(2)],
                  (kT[:, 0, b * 2 * P:(b + 1) * 2 * P].rearrange("p (t n) -> p t n", n=P),
                   kT[:, 1, b * 2 * P:(b + 1) * 2 * P].rearrange("p (t n) -> p t n", n=P))) for b in range(SB)]
        return (kT, vals, q, off, bias), dmas, turns

    def units_of(bufs):
        kT, vals, q, off, bias = bufs
        flat = bias[:].rearrange("p b n -> p (b n)")
        return [halves(h, HD * (h % 2), h // 2, q, kT, None, vals, None, 8, 4, flat, MIX + h * HD) for h in range(HX)]

    def extra(bufs, pool, s_bias):
        kT, vals, q, off, bias = bufs
        link = Chain(pool, sem(f"{name}_cpool"))
        link(nc.gpsimd.tensor_tensor(off[:], seqmask[:, 0:4], seqmask[:, 4:8], ALU.add))
        link(nc.gpsimd.tensor_scalar(off[:], off[:], -BIG, BIG, ALU.mult, ALU.add))
        nc.gpsimd.tensor_copy(bias[:], off[:].unsqueeze(2).to_broadcast([P, 4, 2 * P])).then_inc(s_bias, 1)

    sample_attention(nc, name, sem, sb_in, ps_in, ident, units_of, loads, o_s, 8 * P, extra)


def sample_hgrn(nc, sem, sb_in, ps_in, v, o_s):
    ident, proj, seqmask, neg_half = v["ident"], v["proj"], v["seqmask"], v["neg_half"]
    tok = slice(SEQ, NTOK)
    LEVELS = 5
    s_ld, s_st, s_tp, s_ev, s_lv, s_cp, s_qz, s_o, s_kz, s_kv, s_s, s_oc, s_sq, s_ms, s_rs, s_out, c_pool, c_dve = (
        sem(f"sh_{n}") for n in ("ld", "st", "tp", "ev", "lv", "cp", "qz", "o", "kz", "kv", "s", "oc", "sq", "ms", "rs",
                                 "out", "cpool", "cdve"))
    with ExitStack() as ctx:
        sb, ps = sb_in(ctx), ps_in(ctx)
        q, f, k, iT = (sb(f"sh_{n}", [P, MIX]) for n in ("q", "f", "k", "iT"))
        qm = {m: sb(f"sh_q{m}", [P, MIX]) for m in (1, 2, 4, 8, 16)}
        km = {m: sb(f"sh_k{m}", [P, MIX]) for m in (2, 4, 8, 16)}
        tm = {m: sb(f"sh_t{m}", [P, MIX // m]) for m in (2, 4, 8, 16)}
        qm[0], km[0], km[1], tm[1] = q, k, k, f
        am, inat, knat = (sb(f"sh_{n}", [P, MIX]) for n in ("a", "inat", "knat"))
        masks = sb("sh_masks", [P, LEVELS, P])
        st = sb("sh_state", [P, SB, MG, P])
        qz = [sb(f"sh_qz{i}", [P, SB * P]) for i in range(2)]
        kz = [sb(f"sh_kz{i}", [P, SB, P]) for i in range(2)]
        sq = sb("sh_sq", [P, MIX])
        ssq, ms, rs = (sb(f"sh_{n}", [P, MG]) for n in ("ssq", "ms", "rs"))
        SC = [ps(f"sh_SC{i}", [P, 1024]) for i in range(2)]
        TP = ps("sh_TP", [P, 1024])
        OB = ps("sh_OB", [P, 1024])
        with nc.Block() as block:
            @block.sync
            def _(sp):
                for buf, src in ((q, proj[GQ:GQ + MG, :, tok]), (f, proj[GK:GK + MG, :, tok]), (k, v["kgate"][:, :, tok]),
                                 (iT, proj[GV:GV + MG, :, tok])):
                    sp.dma_start(buf[:].rearrange("p (g n) -> p g n", n=P), src.rearrange("g p n -> p g n")).then_inc(s_ld, 16)
                for h in range(MG):
                    sp.dma_start(st[:, :, h], v["state_b"][0, :, h].rearrange("b k v -> k b v")).then_inc(s_st, 16)
                for h in range(MG):
                    sp.wait_ge(s_s, h + 1)
                    sp.dma_start(v["b_state_sample"][0, :, h].rearrange("b k v -> k b v"), st[:, :, h]).then_inc(s_out, 16)
                sp.wait_ge(s_out, 16 * MG)

            @block.gpsimd
            def _(pool):
                link = Chain(pool, c_pool)
                link(nc.gpsimd.memset(masks[:], 1.0))
                link(nc.gpsimd.affine_select(out=masks[:, 0], in_=masks[:, 0], compare_op=ALU.is_equal, fill=0.0,
                                             base=0, pattern=[[-1, P]], channel_multiplier=1))
                for i in range(1, LEVELS):
                    m = 1 << (i - 1)
                    nb = P // (2 * m)
                    view = masks[:, i].rearrange("p (b two m) -> p b two m", two=2, m=m)
                    link(nc.gpsimd.memset(view[:, :, 0, :], 0.0))
                    sel = view[:, :, 1, :]
                    link(nc.gpsimd.affine_select(out=sel, in_=sel, compare_op=ALU.is_ge, fill=0.0, base=0,
                                                 pattern=[[-2 * m, nb], [0, m]], channel_multiplier=1))
                    link(nc.gpsimd.affine_select(out=sel, in_=sel, compare_op=ALU.is_ge, fill=0.0, base=m - 1,
                                                 pattern=[[2 * m, nb], [0, m]], channel_multiplier=-1))
                for z in (am, qz[0], qz[1]):
                    link(nc.gpsimd.memset(z[:], 0.0))
                pool.wait_ge(s_ms, 1)
                nc.gpsimd.tensor_tensor(rs[:], ms[:], neg_half[:, 0:MG], ALU.pow).then_inc(s_rs, 1)
            N_POOL = 2 + 3 * (LEVELS - 1) + 3

            def update(h, dve, link):
                dve.wait_ge(s_o, h + 1)
                link(nc.vector.tensor_tensor(st[:, :, h], st[:, :, h],
                                             tm[16][:, h * SB:(h + 1) * SB].unsqueeze(2).to_broadcast([P, SB, P]), ALU.mult))
                dve.wait_ge(s_kv, h + 1)
                for c in range(2):
                    bs = slice(4 * c, 4 * c + 4)
                    ins = nc.vector.tensor_tensor(st[:, bs, h], st[:, bs, h],
                                                  SC[h % 2][:, 512 * c:512 * c + 512].rearrange("p (b v) -> p b v", v=P), ALU.add)
                ins.then_inc(s_s, 1)

            @block.scalar
            def _(act):
                act.wait_ge(s_oc, 1)
                nc.scalar.activation(sq[:], o_s[:, 0:MIX], ACT.Square).then_inc(s_sq, 1)

            @block.vector
            def _(dve):
                link = Chain(dve, c_dve)
                dve.wait_ge(s_ld, 64)
                dve.wait_ge(c_pool, N_POOL)
                link(nc.vector.tensor_tensor(qm[1][:], q[:], f[:], ALU.mult))
                for m in (1, 2, 4, 8):
                    n = MIX // (2 * m)

                    def two(a, width=m):
                        return a[:].rearrange("p (n two m) -> p n two m", two=2, m=width)
                    tot = two(tm[m], 1)
                    nc.vector.tensor_copy(two(qm[2 * m])[:, :, 0], two(qm[m])[:, :, 0])
                    nc.vector.tensor_copy(two(km[2 * m])[:, :, 1], two(km[m])[:, :, 1])
                    nc.vector.tensor_tensor(two(qm[2 * m])[:, :, 1], two(qm[m])[:, :, 1],
                                            tot[:, :, 0].to_broadcast([P, n, m]), ALU.mult)
                    nc.vector.tensor_tensor(two(km[2 * m])[:, :, 0], two(km[m])[:, :, 0],
                                            tot[:, :, 1].to_broadcast([P, n, m]), ALU.mult)
                    link(nc.vector.tensor_tensor(tm[2 * m][:].unsqueeze(2), tot[:, :, 0], tot[:, :, 1], ALU.mult))
                dve.wait_ge(s_tp, 1)
                nc.vector.tensor_copy(inat[:].rearrange("p (c n) -> p c n", n=384),
                                      TP[:].rearrange("p (c n) -> p c n", n=512)[:, :, 0:384]).then_inc(s_ev, 1)
                for i in range(LEVELS):
                    dve.wait_ge(s_lv, i + 1)
                    nc.vector.copy_predicated(am[:].rearrange("p (c n) -> p c n", n=P),
                                              masks[:, i:i + 1].bitcast(U32).to_broadcast([P, MG, P]),
                                              SC[i % 2][:, 0:MIX].rearrange("p (h n) -> p h n", n=P)).then_inc(s_cp, 1)
                    dve.wait_ge(s_cp, i + 1)
                dve.wait_ge(s_tp, 2)
                nc.vector.tensor_copy(knat[:].rearrange("p (c n) -> p c n", n=384),
                                      TP[:].rearrange("p (c n) -> p c n", n=512)[:, :, 0:384]).then_inc(s_ev, 1)
                dve.wait_ge(s_ev, 2)
                dve.wait_ge(s_st, 16 * MG)
                for h in range(MG):
                    hs = slice(h * P, (h + 1) * P)
                    wait(dve, s_o, h - 1)
                    nc.vector.tensor_copy(bass.AP(qz[h % 2][:].tensor, 0, [[SB * P, P], [P + SL, SB], [1, SL]]),
                                          qm[16][:, hs].rearrange("p (b n) -> p b n", n=SL)).then_inc(s_qz, 1)
                    wait(dve, s_kv, h - 1)
                    nc.vector.tensor_tensor(kz[h % 2][:], knat[:, hs].unsqueeze(1).to_broadcast([P, SB, P]),
                                            seqmask[:].unsqueeze(2).to_broadcast([P, SB, P]), ALU.mult).then_inc(s_kz, 1)
                    if h:
                        update(h - 1, dve, link)
                update(MG - 1, dve, link)
                nc.vector.tensor_copy(o_s[:, 0:512], OB[:, 0:512])
                nc.vector.tensor_copy(o_s[:, 512:MIX], OB[:, 512:MIX]).then_inc(s_oc, 1)
                dve.wait_ge(s_sq, 1)
                link(nc.vector.tensor_reduce(ssq[:], sq[:].rearrange("p (h d) -> p h d", d=P), AX_X, ALU.add))
                nc.vector.tensor_scalar(ms[:], ssq[:], 1.0 / P, EPS, ALU.mult, ALU.add).then_inc(s_ms, 1)
                dve.wait_ge(s_rs, 1)
                nc.vector.tensor_tensor(o_s[:, 0:MIX].rearrange("p (h d) -> p h d", d=P),
                                        o_s[:, 0:MIX].rearrange("p (h d) -> p h d", d=P),
                                        rs[:].unsqueeze(2).to_broadcast([P, MG, P]), ALU.mult)

            @block.tensor
            def _(pe):
                def turn(src):
                    for g in range(MG):
                        at = (g % 3) * P + 512 * (g // 3)
                        ins = nc.tensor.transpose(TP[:, at:at + P], src[:, g * P:(g + 1) * P], ident[:])
                    ins.then_inc(s_tp, 1)
                pe.wait_ge(s_ld, 64)
                pe.wait_ge(c_dve, 5)
                turn(iT)
                for i in range(LEVELS):
                    wait(pe, s_cp, i - 1)
                    m = 0 if i == 0 else 1 << (i - 1)
                    for h in range(MG):
                        hs = slice(h * P, (h + 1) * P)
                        ins = nc.tensor.matmul(SC[i % 2][:, hs], km[m][:, hs], qm[m][:, hs], start=True, stop=True)
                    ins.then_inc(s_lv, 1)
                pe.wait_ge(s_ev, 1)
                turn(km[16])
                pe.wait_ge(s_cp, LEVELS)
                pe.wait_ge(s_st, 16 * MG)
                for h in range(MG):
                    hs = slice(h * P, (h + 1) * P)
                    pe.wait_ge(s_qz, h + 1)
                    nc.tensor.matmul(OB[:, hs], am[:, hs], inat[:, hs], start=True, stop=False)
                    for b in range(SB):
                        ins = nc.tensor.matmul(OB[:, hs], qz[h % 2][:, b * P:(b + 1) * P], st[:, b, h], start=False,
                                               stop=(b == SB - 1))
                    ins.then_inc(s_o, 1)
                    pe.wait_ge(s_kz, h + 1)
                    wait(pe, s_s, h - 1)
                    for b in range(SB):
                        ins = nc.tensor.matmul(SC[h % 2][:, b * P:(b + 1) * P], kz[h % 2][:, b], inat[:, hs], start=True, stop=True)
                    ins.then_inc(s_kv, 1)


def load_w_out(nc, l, sem, sb_in, w_out, g_hgrn, woh, wol):
    s_in = [sem(f"wo{l}_in{i}") for i in range(2)]
    s_g, s_h, s_l = sem(f"wo{l}_g"), sem(f"wo{l}_h"), sem(f"wo{l}_l")
    with ExitStack() as ctx:
        raw = [sb_in(ctx)(f"wo{l}_raw{i}", [P, D]) for i in range(2)]
        with nc.Block() as block:
            @block.sync
            def _(sp):
                for k in range(KD):
                    wait(sp, s_l, k - 1)
                    sp.dma_start(raw[k % 2][:], w_out[l, k * P:(k + 1) * P]).then_inc(s_in[k % 2], 16)

            @block.vector
            def _(dve):
                for k in range(KD):
                    dve.wait_ge(s_in[k % 2], 16 * (k // 2 + 1))
                    g = g_hgrn[:, k:k + 1] if l == 1 and k < MG else 1.0
                    nc.vector.tensor_scalar(raw[k % 2][:], raw[k % 2][:], g, None, ALU.mult).then_inc(s_g, 1)
                    dve.wait_ge(s_h, k + 1)
                    nc.vector.tensor_tensor(wol[:, k], raw[k % 2][:], woh[:, k].bitcast(F32), ALU.subtract).then_inc(s_l, 1)

            @block.scalar
            def _(act):
                for k in range(KD):
                    act.wait_ge(s_g, k + 1)
                    nc.scalar.copy(woh[:, k], raw[k % 2][:]).then_inc(s_h, 1)


def mix(nc, l, software, sb_in, ps_in, v):
    with ExitStack() as ctx:
        sb = sb_in(ctx)
        o_s = sb(f"o_s{l}", [P, D])
        with Semaphores(nc, software) as sem:
            if l == 0:
                sample_band(nc, sem, sb_in, ps_in, v, o_s)
            else:
                sample_hgrn(nc, sem, sb_in, ps_in, v, o_s)
            sample_cross(nc, l, sem, sb_in, ps_in, v, o_s)
        woh = sb(f"woh{l}", [P, KD, D], F32R)
        wol = sb(f"wol{l}", [P, KD, D], F32R)
        with Semaphores(nc, software) as sem:
            load_w_out(nc, l, sem, sb_in, v["w_out"], v["g_hgrn"], woh, wol)
            prompt(nc, l, sem, sb_in, ps_in, v, o_s, woh, wol)


def prompt(nc, l, sem, sb_in, ps_in, v, o_s, woh, wol):
    ident, proj, mem_kT, mem_v, neg_half = (v[n] for n in ("ident", "proj", "mem_kT", "mem_v", "neg_half"))
    band = l == 0
    nm = f"pr{l}_"
    U = (HA if band else 0) + HX
    PRE, MID = 1, (0 if band else 1)
    PER_D, PER_A = PRE + 1 + MID + U, PRE + MID + U
    LEVELS = 8
    names = ["tp", "eva", "evd", "sc", "min", "exp", "pv", "rs", "o", "y", "yh", "yl", "op", "xadd", "out", "vc",
             "kp", "ldg", "ldf", "fsq", "fms", "frs", "ld_b", "bias",
             "hq", "hst", "hcp", "lv", "cp", "om", "kv", "s", "osq", "oms", "ors", "ocp", "init"]
    S = {n: sem(nm + n) for n in names if band or n not in ("vc", "kp", "ld_b", "bias")
         if not band or n not in ("ldf", "fsq", "fms", "frs", "hq", "hst", "hcp", "lv", "cp", "om", "kv", "s", "osq", "oms",
                                  "ors", "ocp", "init")}
    s_ld = [sem(nm + f"ld{i}") for i in range(2)]
    s_ldx = [sem(nm + f"ldx{i}") for i in range(2)]
    s_stx = [sem.software(nm + f"stx{i}") for i in range(2)]
    LOADS = 4 if band else 5
    with ExitStack() as ctx:
        sb, ps = sb_in(ctx), ps_in(ctx)
        xq = [sb(nm + f"xq{i}", [P, 2, P]) for i in range(2)]
        gt = sb(nm + "gate", [P, KD, P])
        xt = [sb(nm + f"x{i}", [P, D]) for i in range(2)]
        W = BAND if band else NMEM
        se = [sb(nm + f"se{i}", [P, W]) for i in range(2)]
        pt = [sb(nm + f"pt{i}", [P, W]) for i in range(2)]
        mn = sb(nm + "mn", [P, 16])
        tot = sb(nm + "tot", [P, 16])
        rs = sb(nm + "rs", [P, 16])
        o = sb(nm + "o", [P, D])
        y = sb(nm + "y", [P, D])
        yh = sb(nm + "yh", [P, KD, P], F32R)
        yl = sb(nm + "yl", [P, KD, P], F32R)
        SC = [ps(nm + f"SC{i}", [P, 1024]) for i in range(2)]
        TP = ps(nm + "TP", [P, 1024])
        OB = ps(nm + "OB", [P, 1024])
        tT = sb(nm + "vT", [P, MG, P])
        if band:
            q = [sb(nm + f"q{i}", [P, MG, P]) for i in range(2)]
            kcur, kprev = sb(nm + "kcur", [P, MG, 512]), sb(nm + "kprev", [P, MG, 512])
            vcur, vprev = sb(nm + "vcur", [P, 4, MIX]), sb(nm + "vprev", [P, 4, MIX])
            bias = sb(nm + "bias", [P, HA, BAND])
        else:
            qm = {m: sb(nm + f"q{m}", [P, MIX]) for m in (1, 2, 4, 8, 16, 32, 64, 128)}
            km = {m: sb(nm + f"k{m}", [P, MIX]) for m in (2, 4, 8, 16, 32, 64, 128)}
            tm = {m: sb(nm + f"t{m}", [P, MIX // m]) for m in (2, 4, 8, 16, 32, 64, 128)}
            q = [sb(nm + f"q0{i}", [P, MIX]) for i in range(2)]
            k1 = [sb(nm + f"k1{i}", [P, MIX]) for i in range(2)]
            t1 = [sb(nm + f"t1{i}", [P, MIX]) for i in range(2)]
            am = [sb(nm + f"a{i}", [P, MIX]) for i in range(2)]
            masks = sb(nm + "masks", [P, LEVELS, P])
            inat = sb(nm + "inat", [P, MIX])
            knat = sb(nm + "knat", [P, MIX])
            st = sb(nm + "state", [P, MIX])
            fg = sb(nm + "fg", [P, D])
            ssq = sb(nm + "ssq", [P, 16])
            ms6 = sb(nm + "ms6", [P, 16])
            rs6 = sb(nm + "rs6", [P, 16])
            fs = sb(nm + "fs", [P, 2])
            fm = sb(nm + "fm", [P, 2])
            fr = sb(nm + "fr", [P, 2])

        def units(j, first_block, p):
            out = []
            if band:
                n = j + 1 if first_block else 5
                keys = [(kcur, vcur, i) for i in range(j + 1)]
                if not first_block:
                    keys = [(kprev, vprev, i) for i in range(j, 4)] + keys
                for h in range(HA):
                    g, po = h // 2, HD * (h % 2)
                    score, at = [], 0
                    while at < n:
                        end = at + 1
                        while end < n and keys[end][0] is keys[at][0] and end != 4:
                            end += 1
                        slot = keys[at][2]
                        score.append((slice(at * P, end * P), ALL, q[p][po:po + HD, g],
                                      keys[at][0][po:po + HD, g, slot * P:(slot + end - at) * P]))
                        at = end
                    out.append(Unit(h * HD, n, (n + 1) // 2, score, bias[:, h, (5 - n) * P:],
                                    [(ALL, i, ALL, keys[i][1][:, keys[i][2], h * HD:(h + 1) * HD]) for i in range(n)]))
            for h in range(HX):
                out.append(cross_unit(MIX + h * HD, h, xq[p], mem_kT[:, l], mem_v[:, l]))
            return out

        def d_pre(t):
            return t * PER_D - 1 if not (isinstance(t, int) and t == 0) else 0

        def d_y(t):
            if isinstance(t, int) and t == NT:
                return NT * PER_D - 1
            return t * PER_D + (PRE - 1)

        def d_mid(t):
            return t * PER_D + PRE

        def d_unit(t, u):
            return t * PER_D + (PRE + MID + u)

        def a_pre(t):
            return t * PER_A

        def a_y(t):
            if isinstance(t, int) and t == NT:
                return NT * PER_A
            return t * PER_A + PRE

        def a_unit(t, u):
            return t * PER_A + (PRE + MID + u)

        def slot(t, u):
            return u % 2 if band else (u + 1) % 2

        def tiles(eng, body):
            for j in range(4):
                body(j, j, 0)
            with eng.Fori(1, NT // 4) as b:
                for j in range(4):
                    body(b * 4 + j, j, b)

        with nc.Block() as block:
            @block.sync
            def _(sp):
                if band:
                    sp.dma_start(bias[:], bass.AP(v["ext"].tensor, P - 1, [[767, P], [P * 768, HA], [1, BAND]])
                                 ).then_inc(S["ld_b"], 16)
                else:
                    sp.dma_start(fg[:], bass.AP(v["final_g"].tensor, 0, [[0, P], [1, D]])).then_inc(S["ldf"], 16)

                def cols(g, n, t):
                    return proj[g:g + n, :, bass.ds(t * P, P)].rearrange("g p n -> p g n")

                def body(t, j, b):
                    first = isinstance(b, int)
                    p = j % 2
                    if band:
                        wait(sp, S["sc"], (t - 1) * U)
                        sp.dma_start(q[p][:], cols(GQ, MG, t)).then_inc(s_ld[p], 16)
                        sp.dma_start(xq[p][:], cols(GX, 2, t)).then_inc(s_ld[p], 16)
                        if not first and j == 0:
                            sp.wait_ge(S["pv"], t)
                            sp.dma_start(kprev[:], proj[GK:GK + MG, :, bass.ds(t * P - 512, 512)].rearrange("g p n -> p g n")
                                         ).then_inc(S["kp"], 16)
                        sp.dma_start(kcur[:, :, j * P:(j + 1) * P], cols(GK, MG, t)).then_inc(s_ld[p], 16)
                    else:
                        wait(sp, S["pv"], t - 1)
                        for buf, src in ((q, cols(GQ, MG, t)), (t1, cols(GK, MG, t)),
                                         (k1, v["kgate"][:, :, bass.ds(t * P, P)].rearrange("g p n -> p g n"))):
                            sp.dma_start(buf[p][:].rearrange("p (g n) -> p g n", n=P), src).then_inc(s_ld[p], 16)
                        sp.dma_start(xq[p][:], cols(GX, 2, t)).then_inc(s_ld[p], 16)
                    if not (isinstance(t, int) and t == 0):
                        sp.wait_ge(S["tp"], d_pre(t - 1) + 1)
                    sp.dma_start(tT[:], cols(GV, MG, t)).then_inc(s_ld[p], 16)
                    load_x(t, p)
                    if not (isinstance(t, int) and t == 0):
                        sp.wait_ge(S["evd"], d_y(t) + 1)
                    sp.dma_start(gt[:], cols(GG, KD, t)).then_inc(S["ldg"], 16)

                def load_x(t, p):
                    if not (isinstance(t, int) and t < 2):
                        sp.wait_ge(s_stx[p], (t - p) * 8)
                    sp.dma_start(xt[p][:], v["x_of"](t)).then_inc(s_ldx[p], 16)
                tiles(sp, body)
                load_x(NT, 0)
                sp.wait_ge(S["evd"], d_y(NT) + 1)
                sp.dma_start(gt[:], cols(GG, KD, NT)).then_inc(S["ldg"], 16)

            def out_of(t):
                if band:
                    return v["x_mid"][t]
                if isinstance(t, int) and t == NT:
                    return v["y_sample"].rearrange("b s d -> (b s) d")
                return v["y_prompt"].rearrange("b (t p) d -> (b t) p d", p=P)[t]

            def level_masks(pool):
                link = Chain(pool, S["init"])
                link(nc.gpsimd.memset(masks[:], 1.0))
                link(nc.gpsimd.affine_select(out=masks[:, 0], in_=masks[:, 0], compare_op=ALU.is_equal, fill=0.0,
                                             base=0, pattern=[[-1, P]], channel_multiplier=1))
                for i in range(1, LEVELS):
                    m = 1 << (i - 1)
                    nb = P // (2 * m)
                    whole = masks[:, i]
                    view = whole.rearrange("p (b two m) -> p b two m", two=2, m=m)
                    link(nc.gpsimd.memset(view[:, :, 0, :], 0.0))
                    sel = view[:, :, 1, :]
                    link(nc.gpsimd.affine_select(out=sel, in_=sel, compare_op=ALU.is_ge, fill=0.0, base=0,
                                                 pattern=[[-2 * m, nb], [0, m]], channel_multiplier=1))
                    link(nc.gpsimd.affine_select(out=sel, in_=sel, compare_op=ALU.is_ge, fill=0.0, base=m - 1,
                                                 pattern=[[2 * m, nb], [0, m]], channel_multiplier=-1))
                link(nc.gpsimd.memset(am[0][:], 0.0))
                link(nc.gpsimd.memset(am[1][:], 0.0))
                link(nc.gpsimd.memset(st[:], 0.0))

            @block.gpsimd
            def _(pool):
                if band:
                    pool.wait_ge(S["ld_b"], 16)
                    nc.gpsimd.memset(bias[64:P, :, 0:CHUNK], BIG)
                    nc.gpsimd.memset(bias[0:64, :, BAND - CHUNK:], BIG).then_inc(S["bias"], 1)
                else:
                    level_masks(pool)

                def body(t, j, b):
                    first = isinstance(b, int)
                    p = j % 2
                    if not band:
                        powers(pool, t, p)
                    pool.wait_ge(S["xadd" if band else "out"], t + 1)
                    pool.dma_start(out_of(t), xt[p][:]).then_inc(s_stx[p], 16)

                def powers(pool, t, p, hgrn=True):
                    if hgrn:
                        pool.wait_ge(S["oms"], t + 1)
                        wait(pool, S["o"], t)
                        nc.gpsimd.tensor_tensor(rs6[:, 0:MG], ms6[:, 0:MG], neg_half[:, 0:MG], ALU.pow).then_inc(S["ors"], 1)
                    pool.wait_ge(S["fms"], t + 1)
                    nc.gpsimd.tensor_tensor(fr[:, 0:1], fm[:, 0:1], neg_half[:, 0:1], ALU.pow).then_inc(S["frs"], 1)
                tiles(pool, body)
                if not band:
                    powers(pool, NT, 0, hgrn=False)
                pool.wait_ge(S["xadd" if band else "out"], NT + 1)
                pool.dma_start(out_of(NT), xt[0][:]).then_inc(s_stx[0], 16)
                if not band:
                    pool.wait_ge(S["s"], NT)
                    pool.dma_start(v["b_state_prompt"][0, 0].rearrange("h k v -> k h v"),
                                   st[:].rearrange("k (h v) -> k h v", v=P)).then_inc(s_stx[1], 16)
                pool.wait_ge(s_stx[0], 16 * (NT // 2 + 1))
                pool.wait_ge(s_stx[1], 16 * (NT // 2 + (0 if band else 1)))

            N_INIT = 2 + 3 * (LEVELS - 1) + 3

            def q_of(m, p):
                return q[p] if m == 0 else qm[m]

            def k_of(m, p):
                return k1[p] if m <= 1 else km[m]

            def t_of(m, p):
                return t1[p] if m == 1 else tm[m]

            @block.tensor
            def _(pe):
                def gate_and_project(t, src, sample=False):
                    if not sample:
                        pe.wait_ge(S["o"], t)
                    pe.wait_ge(S["evd"], d_y(t) if not sample else d_y(t) + 1)
                    pe.wait_ge(S["eva"], a_y(t))
                    for k in range(KD):
                        ins = nc.tensor.transpose(TP[:, k * P:(k + 1) * P], src[:, k * P:(k + 1) * P], ident[:])
                    ins.then_inc(S["tp"], 1)
                    n = t + 1 if sample else t
                    pe.wait_ge(S["yl"], n)
                    if sample:
                        pe.wait_ge(S["xadd"], NT)
                    for half in range(2):
                        cols = slice(half * 512, half * 512 + 512)
                        for k in range(KD):
                            for a, w in ((yh, woh), (yh, wol), (yl, woh)):
                                ins = nc.tensor.matmul(OB[:, cols], a[:, k], w[:, k, cols], start=(k == 0 and a is yh and w is woh),
                                                       stop=(k == KD - 1 and a is yl))
                    ins.then_inc(S["op"], 1)

                def body(t, j, b):
                    first = isinstance(b, int)
                    p = j % 2
                    us = units(j, first, p)
                    has_prev = not (isinstance(t, int) and t == 0)

                    def scores(u):
                        if band:
                            wait(pe, S["exp"], t * U + (u - 1))
                        elif u == 0:
                            pe.wait_ge(S["cp"], t * 16 + 16)
                        elif u == 1:
                            pe.wait_ge(S["s"], t + 1)
                        else:
                            pe.wait_ge(S["exp"], t * U + (u - 1))
                        unit_scores(nc, us[u], SC[slot(t, u)]).then_inc(S["sc"], 1)

                    def values(u):
                        pe.wait_ge(S["eva"], a_unit(t, u) + 1)
                        pe.wait_ge(S["evd"], d_unit(t, u) + 1)
                        if u == 0 and has_prev:
                            pe.wait_ge(S["xadd"], t)
                        ins = unit_pv(nc, us[u], pt[u % 2], OB)
                        if u == U - 1:
                            ins.then_inc(S["pv"], 1)

                    def turn(srcs, n_d, n_a):
                        wait(pe, S["evd"], n_d)
                        wait(pe, S["eva"], n_a)
                        for g in range(MG):
                            at = (g % 3) * P + 512 * (g // 3)
                            ins = nc.tensor.transpose(TP[:, at:at + P], srcs(g), ident[:])
                        ins.then_inc(S["tp"], 1)

                    pe.wait_ge(s_ld[p], (t - p) * 8 * LOADS + 16 * LOADS)
                    turn(lambda g: tT[:, g], d_pre(t), a_pre(t))
                    if band:
                        if not first and j == 0:
                            pe.wait_ge(S["kp"], b * 16)
                        scores(0)
                        scores(1)
                    else:
                        def level(i):
                            m = 0 if i == 0 else 1 << (i - 1)
                            if i < 2:
                                wait(pe, S["exp"], t * U - i)
                            else:
                                pe.wait_ge(S["cp"], t * 16 + 2 * (i - 1))
                            if i:
                                pe.wait_ge(S["hst"], t * 8 + i)
                            if i > 1:
                                pe.wait_ge(S["hcp"], t * 7 + (i - 1))
                            for h in range(MG):
                                at = (h % 3) * P + 512 * (h // 3)
                                hs = slice(h * P, (h + 1) * P)
                                ins = nc.tensor.matmul(SC[i % 2][:, at:at + P], k_of(m, p)[:, hs], q_of(m, p)[:, hs],
                                                       start=True, stop=True)
                                if h % 3 == 2:
                                    ins.then_inc(S["lv"], 1)
                        level(0)
                        level(1)
                    if has_prev:
                        gate_and_project(t, o)
                    if not band:
                        for i in range(2, LEVELS):
                            level(i)
                        pe.wait_ge(S["hst"], t * 8 + 8)
                        pe.wait_ge(S["hcp"], t * 7 + 7)
                        turn(lambda g: km[128][:, g * P:(g + 1) * P], d_mid(t), t * PER_A + PRE)
                        pe.wait_ge(S["cp"], t * 16 + 16)
                        if has_prev:
                            pe.wait_ge(S["xadd"], t)
                            pe.wait_ge(S["s"], t)
                        for h in range(MG):
                            hs = slice(h * P, (h + 1) * P)
                            nc.tensor.matmul(OB[:, hs], am[p][:, hs], inat[:, hs], start=True, stop=False)
                            nc.tensor.matmul(OB[:, hs], qm[128][:, hs], st[:, hs], start=False, stop=True)
                        pe.wait_ge(S["evd"], d_mid(t) + 1)
                        pe.wait_ge(S["eva"], t * PER_A + (PRE + 1))
                        for h in range(MG):
                            at = (h % 3) * P + 512 * (h // 3)
                            hs = slice(h * P, (h + 1) * P)
                            ins = nc.tensor.matmul(SC[0][:, at:at + P], knat[:, hs], inat[:, hs], start=True, stop=True)
                        ins.then_inc(S["kv"], 1)
                        scores(0)
                        scores(1)
                    for u in range(U):
                        pe.wait_ge(S["exp"], t * U + (u + 1))
                        pe.wait_ge(S["eva"], a_unit(t, u))
                        pe.wait_ge(S["evd"], d_unit(t, u))
                        unit_transposes(nc, us[u], se[u % 2], TP, ident).then_inc(S["tp"], 1)
                        if u:
                            values(u - 1)
                        elif band and not first and j == 0:
                            pe.wait_ge(S["vc"], b)
                        if u + 2 < U:
                            scores(u + 2)
                    values(U - 1)

                if band:
                    pe.wait_ge(S["bias"], 1)
                else:
                    pe.wait_ge(S["init"], N_INIT)
                tiles(pe, body)
                gate_and_project(NT, o)
                gate_and_project(NT, o_s, sample=True)

            @block.vector
            def _(dve):
                def outputs(t):
                    dve.wait_ge(S["pv"], t)
                    nc.vector.reciprocal(rs[:, 0:U], tot[:, 0:U]).then_inc(S["rs"], 1)
                    dve.wait_ge(S["rs"], t)
                    if band:
                        for c in range(2):
                            ins = nc.vector.tensor_tensor(o[:, c * 512:(c + 1) * 512].rearrange("p (h d) -> p h d", d=HD),
                                                          OB[:, c * 512:(c + 1) * 512].rearrange("p (h d) -> p h d", d=HD),
                                                          rs[:, c * 8:c * 8 + 8].unsqueeze(2).to_broadcast([P, 8, HD]), ALU.mult)
                        ins.then_inc(S["o"], 1)
                        return
                    nc.vector.tensor_tensor(o[:, MIX:D].rearrange("p (h d) -> p h d", d=HD),
                                            OB[:, MIX:D].rearrange("p (h d) -> p h d", d=HD),
                                            rs[:, 0:HX].unsqueeze(2).to_broadcast([P, HX, HD]), ALU.mult)
                    nc.vector.tensor_copy(o[:, 0:512], OB[:, 0:512])
                    nc.vector.tensor_copy(o[:, 512:MIX], OB[:, 512:MIX]).then_inc(S["ocp"], 1)

                def outputs_norm(t):
                    dve.wait_ge(S["osq"], t)
                    nc.vector.tensor_reduce(ssq[:, 0:MG], y[:, 0:MIX].rearrange("p (h d) -> p h d", d=P), AX_X, ALU.add
                                            ).then_inc(S["hq"], 1)
                    dve.wait_ge(S["hq"], t)
                    nc.vector.tensor_scalar(ms6[:, 0:MG], ssq[:, 0:MG], 1.0 / P, EPS, ALU.mult, ALU.add).then_inc(S["oms"], 1)
                    dve.wait_ge(S["ors"], t)
                    nc.vector.tensor_tensor(o[:, 0:MIX].rearrange("p (h d) -> p h d", d=P),
                                            o[:, 0:MIX].rearrange("p (h d) -> p h d", d=P),
                                            rs6[:, 0:MG].unsqueeze(2).to_broadcast([P, MG, P]), ALU.mult).then_inc(S["o"], 1)

                def gate_and_add(t, p, sample=False):
                    n = t + 1 if sample else t
                    dve.wait_ge(S["tp"], d_y(t) + (2 if sample else 1))
                    dve.wait_ge(S["ldg"], n * 16)
                    for c in range(2):
                        ins = nc.vector.tensor_tensor(y[:, c * 512:(c + 1) * 512], TP[:, c * 512:(c + 1) * 512],
                                                      gt[:, 4 * c:4 * c + 4].rearrange("p k n -> p (k n)"), ALU.mult)
                    ins.then_inc(S["evd"], 1)
                    dve.wait_ge(S["yh"], n)
                    nc.vector.tensor_tensor(yl[:].rearrange("p k n -> p (k n)"), y[:], yh[:].bitcast(F32).rearrange("p k n -> p (k n)"),
                                            ALU.subtract).then_inc(S["yl"], 1)
                    dve.wait_ge(S["op"], n)
                    dve.wait_ge(s_ldx[p], (n - 1 - p) * 8 + 16)
                    for c in range(2):
                        ins = nc.vector.tensor_tensor(xt[p][:, c * 512:(c + 1) * 512], xt[p][:, c * 512:(c + 1) * 512],
                                                      OB[:, c * 512:(c + 1) * 512], ALU.add)
                    ins.then_inc(S["xadd"], 1)

                def final_mean(n):
                    dve.wait_ge(S["fsq"], n)
                    wait(dve, S["frs"], n - 1)
                    nc.vector.tensor_scalar(fm[:, 0:1], fs[:, 0:1], 1.0 / D, EPS, ALU.mult, ALU.add).then_inc(S["fms"], 1)

                def final_scale(n, p):
                    dve.wait_ge(S["frs"], n)
                    nc.vector.scalar_tensor_tensor(out=xt[p][:], in0=xt[p][:], scalar=fr[:, 0:1], in1=fg[:],
                                                   op0=ALU.mult, op1=ALU.mult).then_inc(S["out"], 1)

                def body(t, j, b):
                    first = isinstance(b, int)
                    p = j % 2
                    us = units(j, first, p)
                    has_prev = not (isinstance(t, int) and t == 0)

                    def low_min(u):
                        scored = counted(dve, t * U + (u + 1))
                        if band:
                            dve.wait_ge(S["bias"], 1)
                        dve.wait_ge(S["sc"], scored)
                        unit_min(nc, us[u], SC[slot(t, u)], se[u % 2], mn[:, u:u + 1]).then_inc(S["min"], 1)
                    if has_prev:
                        outputs(t)
                    if band and not first and j == 0:
                        nc.vector.tensor_copy(vprev[:], vcur[:]).then_inc(S["vc"], 1)
                        dve.wait_ge(S["vc"], b)
                    dve.wait_ge(S["tp"], d_pre(t) + 1)
                    dst = vcur[:, j] if band else inat[:]
                    nc.vector.tensor_copy(dst[:, 384:MIX], TP[:, 512:896]).then_inc(S["evd"], 1)
                    if band:
                        low_min(0)
                        low_min(1)
                        if has_prev:
                            gate_and_add(t, 1 - p)
                    else:
                        dve.wait_ge(s_ld[p], (t - p) * 8 * LOADS + 16 * LOADS)

                        def step(i):
                            if i == 0:
                                nc.vector.tensor_tensor(qm[1][:], q[p][:], t1[p][:], ALU.mult).then_inc(S["hst"], 1)
                                return
                            m = 1 << (i - 1)
                            dve.wait_ge(S["hst"], t * 8 + i)
                            wait(dve, S["hcp"], t * 7 + (i - 1))
                            n = MIX // (2 * m)

                            def two(a, width=m):
                                return a[:].rearrange("p (n two m) -> p n two m", two=2, m=width)
                            tot_m = two(t_of(m, p), 1)
                            nc.vector.tensor_tensor(two(qm[2 * m])[:, :, 1], two(q_of(m, p))[:, :, 1],
                                                    tot_m[:, :, 0].to_broadcast([P, n, m]), ALU.mult)
                            nc.vector.tensor_tensor(two(km[2 * m])[:, :, 0], two(k_of(m, p))[:, :, 0],
                                                    tot_m[:, :, 1].to_broadcast([P, n, m]), ALU.mult)
                            nc.vector.tensor_tensor(tm[2 * m][:].unsqueeze(2), tot_m[:, :, 0], tot_m[:, :, 1], ALU.mult
                                                    ).then_inc(S["hst"], 1)

                        def place(i):
                            for c in range(2):
                                made = counted(dve, t * 16 + (2 * i + c + 1))
                                placed = counted(dve, t * 16 + (2 * i + c - 1))
                                dve.wait_ge(S["init"], N_INIT)
                                dve.wait_ge(S["lv"], made)
                                if i:
                                    dve.wait_ge(S["cp"], placed)
                                hs = slice(c * 384, c * 384 + 384)
                                nc.vector.copy_predicated(am[p][:, hs].rearrange("p (h n) -> p h n", n=P),
                                                          masks[:, i:i + 1].bitcast(U32).to_broadcast([P, 3, P]),
                                                          SC[i % 2][:, 512 * c:512 * c + 384].rearrange("p (h n) -> p h n", n=P)
                                                          ).then_inc(S["cp"], 1)
                        step(0)
                        step(1)
                        if has_prev:
                            outputs_norm(t)
                        place(0)
                        step(2)
                        place(1)
                        step(3)
                        if has_prev:
                            gate_and_add(t, 1 - p)
                        for i in range(2, LEVELS):
                            place(i)
                            if i + 2 < LEVELS:
                                step(i + 2)
                            if i == 4 and has_prev:
                                final_mean(t)
                        dve.wait_ge(S["tp"], d_mid(t) + 1)
                        nc.vector.tensor_copy(knat[:, 384:MIX], TP[:, 512:896]).then_inc(S["evd"], 1)
                        if has_prev:
                            final_scale(t, 1 - p)
                        dve.wait_ge(S["kv"], t + 1)
                        for h in range(MG):
                            at = (h % 3) * P + 512 * (h // 3)
                            hs = slice(h * P, (h + 1) * P)
                            ins = nc.vector.scalar_tensor_tensor(out=st[:, hs], in0=st[:, hs], scalar=tm[128][:, h:h + 1],
                                                                 in1=SC[0][:, at:at + P], op0=ALU.mult, op1=ALU.add)
                        ins.then_inc(S["s"], 1)
                        low_min(0)
                        low_min(1)
                    for u in range(U):
                        dve.wait_ge(S["tp"], d_unit(t, u) + 1)
                        unit_evac_high(us[u], nc.vector.tensor_copy, pt[u % 2], TP).then_inc(S["evd"], 1)
                        if u + 2 < U:
                            low_min(u + 2)
                if not band:
                    dve.wait_ge(S["ldf"], 16)
                tiles(dve, body)
                outputs(NT)
                if not band:
                    outputs_norm(NT)
                gate_and_add(NT, 1)
                if not band:
                    final_mean(NT)
                    final_scale(NT, 1)
                gate_and_add(NT, 0, sample=True)
                if not band:
                    final_mean(NT + 1)
                    final_scale(NT + 1, 0)

            @block.scalar
            def _(act):
                def y_high(n, t=None):
                    act.wait_ge(S["evd"], d_y(n) + 1 if t is None else t)
                    nc.scalar.copy(yh[:].rearrange("p k n -> p (k n)"), y[:]).then_inc(S["yh"], 1)

                def final_square(n, p):
                    act.wait_ge(S["xadd"], n)
                    wait(act, S["fms"], n - 1)
                    nc.scalar.activation(y[:], xt[p][:], ACT.Square, accum_out=fs[:, 0:1]).then_inc(S["fsq"], 1)

                def out_square(t):
                    act.wait_ge(S["ocp"], t)
                    wait(act, S["fsq"], t - 1)
                    nc.scalar.activation(y[:, 0:MIX], o[:, 0:MIX], ACT.Square).then_inc(S["osq"], 1)

                def body(t, j, b):
                    first = isinstance(b, int)
                    p = j % 2
                    us = units(j, first, p)
                    has_prev = not (isinstance(t, int) and t == 0)

                    def exp(u):
                        act.wait_ge(S["min"], t * U + (u + 1))
                        unit_exp(nc, us[u], SC[slot(t, u)], se[u % 2], mn[:, u:u + 1], tot[:, u:u + 1]).then_inc(S["exp"], 1)
                    if not band and has_prev:
                        out_square(t)
                    act.wait_ge(S["tp"], d_pre(t) + 1)
                    if band and not first and j == 0:
                        act.wait_ge(S["vc"], b)
                    dst = vcur[:, j] if band else inat[:]
                    nc.scalar.copy(dst[:, 0:384], TP[:, 0:384]).then_inc(S["eva"], 1)
                    if band:
                        exp(0)
                        exp(1)
                        if has_prev:
                            y_high(t)
                    else:
                        act.wait_ge(s_ld[p], (t - p) * 8 * LOADS + 16 * LOADS)

                        def carry(i):
                            m = 1 << (i - 1)
                            act.wait_ge(S["hst"], t * 8 + i)
                            wait(act, S["hcp"], t * 7 + (i - 1))

                            def two(a):
                                return a[:].rearrange("p (n two m) -> p n two m", two=2, m=m)
                            nc.scalar.copy(two(qm[2 * m])[:, :, 0], two(q_of(m, p))[:, :, 0])
                            nc.scalar.copy(two(km[2 * m])[:, :, 1], two(k_of(m, p))[:, :, 1]).then_inc(S["hcp"], 1)
                        carry(1)
                        carry(2)
                        carry(3)
                        if has_prev:
                            y_high(t)
                        carry(4)
                        carry(5)
                        if has_prev:
                            final_square(t, 1 - p)
                        carry(6)
                        carry(7)
                        act.wait_ge(S["tp"], d_mid(t) + 1)
                        nc.scalar.copy(knat[:, 0:384], TP[:, 0:384]).then_inc(S["eva"], 1)
                        exp(0)
                        exp(1)
                    for u in range(U):
                        act.wait_ge(S["tp"], d_unit(t, u) + 1)
                        unit_evac_low(us[u], nc.scalar.copy, pt[u % 2], TP).then_inc(S["eva"], 1)
                        if u + 2 < U:
                            exp(u + 2)
                tiles(act, body)
                if not band:
                    out_square(NT)
                y_high(NT)
                if not band:
                    final_square(NT, 1)
                y_high(NT, d_y(NT) + 2)
                if not band:
                    final_square(NT + 1, 0)


_INS = ['x_prompt', 'x_sample', 'cache_a_k', 'cache_a_v', 'state_b', 'cache_mem_k', 'cache_mem_v', 'mem_prompt',
        'ln_g', 'w_in', 'w_out', 'rel_bias_table', 'lower_bounds', 'hgrn_norm_g', 'mem_norm_g', 'w_mem_kv', 'final_g']
_OUTS = [(1, 2048, 1024), (8, 16, 1024), (1, 1, 512, 12, 64), (1, 1, 512, 12, 64), (1, 1, 6, 128, 128),
         (2, 1, 256, 4, 64), (2, 1, 256, 4, 64), (1, 8, 16, 12, 64), (1, 8, 16, 12, 64), (1, 8, 6, 128, 128)]


def kernel(**inputs):
    import numpy as _np
    import concourse.bacc as _bacc
    from concourse import mybir as _mybir
    from concourse.bass_utils import run_bass_kernel_spmd as _run

    nc = _bacc.Bacc("TRN2", target_bir_lowering=False, num_devices=1)
    arrays, args = {}, []
    for name in _INS:
        a = _np.ascontiguousarray(inputs[name])
        arrays[f"in_{name}_dram"] = a
        args.append(nc.dram_tensor(f"in_{name}_dram", a.shape, _mybir.dt.from_np(a.dtype), kind="ExternalInput").ap())
    for i, shape in enumerate(_OUTS):
        args.append(nc.dram_tensor(f"out_{i}_dram", shape, F32, kind="ExternalOutput").ap())
    hybrid_encoder(nc, *args)
    r = _run(nc, [arrays], core_ids=[0])
    return tuple(r.results[0][f"out_{i}_dram"] for i in range(len(_OUTS)))
```

```python
from contextlib import ExitStack

import concourse.bass as bass
from concourse import mybir

F32 = mybir.dt.float32
F32R = mybir.dt.float32r
U32 = mybir.dt.uint32
ALU = mybir.AluOpType
ACT = mybir.ActivationFunctionType
AX_X = mybir.AxisListType.X

P = 128
D = 1024
KD = D // P
SEQ = 2048
NT = SEQ // P
TS = NT
NTOK = SEQ + P
SB, SL = 8, 16
MIX = 768
MG = MIX // P
HA, HD = 12, 64
HX = 4
NMEM = 256
XW = HX * HD
NG = (3 * MIX + XW + D) // P
CHUNK = 64
BAND = 640
CLIP = 128
EPS = 1e-6
DEPTH = 2
BIG = 1e30
GQ, GK, GV, GX, GG = 0, MG, 2 * MG, 3 * MG, 3 * MG + 2
BLOCKS = [(0, 512), (512, 512), (1024, 384), (1408, 384), (1792, 384)]
NBLK = len(BLOCKS)


def wait(eng, sem, value):
    if not (isinstance(value, int) and value <= 0):
        eng.wait_ge(sem, value)


def counted(eng, value):
    return value if isinstance(value, int) else eng.to_reg(value)


def sweep(eng, first, last, per, body):
    n = (last - first) // per
    for r in range(min(per, last - first)):
        body(first + r, r)
    if n > 1:
        with eng.Fori(1, n) as i:
            for r in range(per):
                body(i * per + (first + r), r)
    for r in range(n * per if n else last - first, last - first):
        body(first + r, r % per)


class Semaphores:

    def __init__(self, nc, software):
        self.nc, self.held, self.ctx, self._software = nc, [], ExitStack(), software

    def __enter__(self):
        return self

    def __call__(self, name):
        self.held.append(self.ctx.enter_context(self.nc.semaphore(name)))
        return self.held[-1]

    def software(self, name):
        return self._software.enter_context(self.nc.semaphore(name))

    def __exit__(self, *error):
        if error[0] is None:
            with self.nc.Block() as block:
                @block.gpsimd
                def _(pool):
                    for s in self.held:
                        pool.sem_clear(s)
        self.ctx.close()


class Chain:

    def __init__(self, eng, sem):
        self.eng, self.sem, self.n = eng, sem, 0

    def __call__(self, ins):
        self.n += 1
        ins.then_inc(self.sem, 1)
        self.eng.wait_ge(self.sem, self.n)


def hybrid_encoder(nc, x_prompt, x_sample, cache_a_k, cache_a_v, state_b, cache_mem_k, cache_mem_v, mem_prompt,
                   ln_g, w_in, w_out, rel_bias_table, lower_bounds, hgrn_norm_g, mem_norm_g, w_mem_kv, final_g,
                   y_prompt, y_sample, a_k_prompt, a_v_prompt, b_state_prompt, mem_k_prompt, mem_v_prompt,
                   a_k_sample, a_v_sample, b_state_sample):
    top = ExitStack()
    with top, nc.allow_non_contiguous_dma(reason="channel vectors onto partitions, and the small bias table"):
        def dram(name, shape):
            return nc.dram_tensor(name, shape, F32, kind="Internal").ap()

        def sb_in(ctx):
            return lambda name, shape, dt=F32: ctx.enter_context(nc.sbuf_tensor(name, shape, dt))

        def ps_in(ctx):
            return lambda name, shape, dt=F32: ctx.enter_context(nc.psum_tensor(name, shape, dt))

        software = top.enter_context(ExitStack())
        sb = sb_in(top)
        proj = dram("proj", (NG, P, NTOK))
        kgate = dram("kgate", (MG, P, NTOK))
        x_mid = dram("x_mid", (NT + 1, P, D))
        ext = dram("ext", (HA, P, 768))

        ident = sb("ident", [P, P])
        g_ln = sb("g_ln", [P, 2, KD])
        g_mem = sb("g_mem", [P, 2, KD])
        g_hgrn = sb("g_hgrn", [P, MG])
        lb = sb("lb", [P, MG])
        lb1 = sb("lb1", [P, MG])
        neg_half = sb("neg_half", [P, 16])
        seqmask = sb("seqmask", [P, SB])
        mem_kT = sb("mem_kT", [P, 2, 2, NMEM])
        mem_v = sb("mem_v", [P, 2, 2, XW])

        xp_t = x_prompt.rearrange("b (t p) d -> (b t) p d", p=P)
        xs_t = x_sample.rearrange("b s d -> (b s) d")

        with Semaphores(nc, software) as sem:
            setup(nc, sem, sb_in, ps_in, locals())
        for l in range(DEPTH):
            def x_of(t):
                if l:
                    return x_mid[t]
                return xs_t if isinstance(t, int) and t == TS else xp_t[t]
            with ExitStack() as ctx:
                xh = sb_in(ctx)(f"xh{l}", [P, KD, NTOK], F32R)
                xl = sb_in(ctx)(f"xl{l}", [P, KD, NTOK], F32R)
                with Semaphores(nc, software) as sem:
                    norm_transpose(nc, l, sem, sb_in, ps_in, x_of, ident, neg_half, xh, xl)
                    project(nc, l, sem, sb_in, ps_in, xh, xl, w_in, g_ln, lb, lb1, proj, kgate)
            if l == 0:
                with Semaphores(nc, software) as sem:
                    keys_out(nc, sem, sb_in, ps_in, ident, proj, a_k_prompt, a_v_prompt, a_k_sample, a_v_sample)
            mix(nc, l, software, sb_in, ps_in, locals())


def setup(nc, sem, sb_in, ps_in, v):
    ident, g_ln, g_mem, g_hgrn, lb, lb1 = (v[n] for n in ("ident", "g_ln", "g_mem", "g_hgrn", "lb", "lb1"))
    neg_half, seqmask, mem_kT, mem_v, ext = (v[n] for n in ("neg_half", "seqmask", "mem_kT", "mem_v", "ext"))
    mem_k_prompt, mem_v_prompt = v["mem_k_prompt"], v["mem_v_prompt"]
    s_cols, s_tab, s_mem, s_ext, s_out = (sem(f"su_{n}") for n in ("cols", "tab", "mem", "ext", "out"))
    s_wkv = [sem(f"su_wkv{i}") for i in range(2)]
    c_pool, c_dve, s_const, s_extv = (sem(f"su_{n}") for n in ("cpool", "cdve", "const", "extv"))
    s_sq, s_ms, s_rs, s_xn, s_tp, s_ev, s_wg, s_kv, s_kvev, s_kt, s_ktev, s_lbx, s_lbe = (
        sem(f"su_{n}") for n in ("sq", "ms", "rs", "xn", "tp", "ev", "wg", "kv", "kvev", "kt", "ktev", "lbx", "lbe"))
    with ExitStack() as ctx:
        sb, ps = sb_in(ctx), ps_in(ctx)
        tab = sb("tab", [HA, 2 * CLIP + 1])
        extv = sb("extv", [HA, 768])
        xm = sb("xm", [P, 2, D])
        sq = sb("sq", [P, D])
        ss = sb("ss", [P, 2])
        ms = sb("ms", [P, 2])
        rs = sb("rs", [P, 2])
        xn = sb("xn", [P, 2, D])
        xT = sb("xT", [P, KD, NMEM])
        wkv = sb("wkv", [P, 2, KD, 2 * XW])
        kv = sb("kv", [P, 4, 2 * XW])
        lbraw = sb("lbraw", [P, MG])
        lbd = sb("lbd", [P, MG])
        lbe = sb("lbe", [P, MG])
        lbr = sb("lbr", [P, MG])
        TP = [ps(f"suTP{i}", [P, 512]) for i in range(4)]
        KV = [ps(f"suKV{i}", [P, 512]) for i in range(4)]
        with nc.Block() as block:
            @block.sync
            def _(sp):
                sp.dma_start(xm[:], v["mem_prompt"].rearrange("b (t p) d -> p (b t) d", p=P)).then_inc(s_mem, 16)
                for l in range(2):
                    sp.dma_start(wkv[:, l], v["w_mem_kv"][l].rearrange("(k p) n -> p k n", p=P)).then_inc(s_wkv[l], 16)
                sp.wait_ge(s_extv, 1)
                sp.dma_start(ext, extv[:].unsqueeze(1).to_broadcast([HA, P, 768])).then_inc(s_ext, 16)
                for i in range(4):
                    l, t = divmod(i, 2)
                    sp.wait_ge(s_kvev, i + 1)
                    rows = slice(t * P, (t + 1) * P)
                    for out, cols in ((mem_k_prompt, slice(0, XW)), (mem_v_prompt, slice(XW, 2 * XW))):
                        sp.dma_start(out[l, 0, rows].rearrange("p h d -> p (h d)"), kv[:, i, cols]).then_inc(s_out, 16)
                sp.wait_ge(s_out, 128)
                sp.wait_ge(s_ext, 16)

            @block.scalar
            def _(act):
                act.dma_start(tab[:], v["rel_bias_table"][0]).then_inc(s_tab, 16)
                for l in range(2):
                    act.dma_start(g_ln[:, l], v["ln_g"][l].rearrange("(k p) -> p k", p=P)).then_inc(s_cols, 16)
                    act.dma_start(g_mem[:, l], v["mem_norm_g"][l].rearrange("(k p) -> p k", p=P)).then_inc(s_cols, 16)
                act.dma_start(g_hgrn[:], v["hgrn_norm_g"][0].rearrange("(k p) -> p k", p=P)).then_inc(s_cols, 16)
                act.dma_start(lbraw[:], v["lower_bounds"][0].rearrange("(k p) -> p k", p=P)).then_inc(s_cols, 16)
                act.wait_ge(s_mem, 16)
                for t in range(2):
                    nc.scalar.activation(sq[:], xm[:, t], ACT.Square, accum_out=ss[:, t:t + 1]).then_inc(s_sq, 1)
                    if t == 0:
                        act.wait_ge(s_sq, 1)
                act.wait_ge(s_lbx, 1)
                nc.scalar.activation(lbe[:], lbd[:], ACT.Exp).then_inc(s_lbe, 1)
                for i in range(4):
                    act.wait_ge(s_tp, i + 1)
                    t, half = divmod(i, 2)
                    nc.scalar.copy(xT[:, half * 4:half * 4 + 4, t * P:(t + 1) * P],
                                   TP[i][:].rearrange("p (k n) -> p k n", n=P)).then_inc(s_ev, 1)
                for i in range(4):
                    l, t = divmod(i, 2)
                    act.wait_ge(s_kv, i + 1)
                    nc.scalar.copy(kv[:, i], KV[i][:]).then_inc(s_kvev, 1)
                for i in range(4):
                    l, t = divmod(i, 2)
                    act.wait_ge(s_kt, i + 1)
                    nc.scalar.copy(mem_kT[:, l, :, t * P:(t + 1) * P],
                                   TP[i][:, 0:2 * P].rearrange("p (g n) -> p g n", n=P)).then_inc(s_ktev, 1)

            @block.gpsimd
            def _(pool):
                link = Chain(pool, c_pool)
                link(nc.gpsimd.memset(ident[:], 0.0))
                link(nc.gpsimd.affine_select(out=ident[:], in_=ident[:], compare_op=ALU.not_equal, fill=1.0,
                                             base=0, pattern=[[-1, P]], channel_multiplier=1))
                link(nc.gpsimd.memset(seqmask[:], 1.0))
                link(nc.gpsimd.affine_select(out=seqmask[:], in_=seqmask[:], compare_op=ALU.is_ge, fill=0.0,
                                             base=0, pattern=[[-SL, SB]], channel_multiplier=1))
                link(nc.gpsimd.affine_select(out=seqmask[:], in_=seqmask[:], compare_op=ALU.is_ge, fill=0.0,
                                             base=SL - 1, pattern=[[SL, SB]], channel_multiplier=-1))
                nc.gpsimd.memset(neg_half[:], -0.5).then_inc(s_const, 1)
                pool.wait_ge(s_const, 1)
                pool.wait_ge(s_ms, 1)
                nc.gpsimd.tensor_tensor(rs[:], ms[:], neg_half[:, 0:2], ALU.pow).then_inc(s_rs, 1)

            @block.vector
            def _(dve):
                link = Chain(dve, c_dve)
                dve.wait_ge(s_cols, 96)
                nc.vector.tensor_tensor(lbd[:], lbraw[:], lbraw[:], ALU.subtract).then_inc(s_lbx, 1)
                dve.wait_ge(s_tab, 16)
                link(nc.vector.memset(extv[:], 0.0))
                link(nc.vector.tensor_scalar(extv[:, 0:511], extv[:, 0:511], tab[:, 2 * CLIP:2 * CLIP + 1], None, ALU.subtract))
                back = bass.AP(tab[:].tensor, 2 * CLIP, [[2 * CLIP + 1, HA], [-1, 2 * CLIP]])
                nc.vector.tensor_scalar(extv[:, 511:511 + 2 * CLIP], back, -1.0, None, ALU.mult).then_inc(s_extv, 1)
                dve.wait_ge(s_lbe, 1)
                link(nc.vector.reciprocal(lbr[:], lbe[:]))
                link(nc.vector.tensor_tensor(lb[:], lbe[:], lbr[:], ALU.mult))
                link(nc.vector.tensor_tensor(lb[:], lb[:], lb[:], ALU.subtract))
                link(nc.vector.tensor_scalar(lb1[:], lb[:], -1.0, 1.0, ALU.mult, ALU.add))
                dve.wait_ge(s_sq, 2)
                nc.vector.tensor_scalar(ms[:], ss[:], 1.0 / D, EPS, ALU.mult, ALU.add).then_inc(s_ms, 1)
                dve.wait_ge(s_rs, 1)
                for t in range(2):
                    nc.vector.tensor_scalar(xn[:, t], xm[:, t], rs[:, t:t + 1], None, ALU.mult).then_inc(s_xn, 1)
                for l in range(2):
                    dve.wait_ge(s_wkv[l], 16)
                    nc.vector.tensor_tensor(wkv[:, l], wkv[:, l],
                                            g_mem[:, l].unsqueeze(2).to_broadcast([P, KD, 2 * XW]),
                                            ALU.mult).then_inc(s_wg, 1)
                for i in range(4):
                    l, t = divmod(i, 2)
                    dve.wait_ge(s_kvev, i + 1)
                    nc.vector.tensor_copy(mem_v[:, l, t], kv[:, i, XW:2 * XW]).then_inc(c_dve, 1)

            @block.tensor
            def _(pe):
                pe.wait_ge(c_pool, 2)
                for t in range(2):
                    pe.wait_ge(s_xn, t + 1)
                    for k in range(KD):
                        ins = nc.tensor.transpose(TP[2 * t + k // 4][:, (k % 4) * P:(k % 4 + 1) * P],
                                                  xn[:, t, k * P:(k + 1) * P], ident[:])
                        if k % 4 == 3:
                            ins.then_inc(s_tp, 1)
                pe.wait_ge(s_ev, 4)
                for i in range(4):
                    l, t = divmod(i, 2)
                    pe.wait_ge(s_wg, l + 1)
                    for k in range(KD):
                        ins = nc.tensor.matmul(KV[i][:], xT[:, k, t * P:(t + 1) * P], wkv[:, l, k],
                                               start=(k == 0), stop=(k == KD - 1))
                    ins.then_inc(s_kv, 1)
                for i in range(4):
                    pe.wait_ge(s_kvev, i + 1)
                    for g in range(2):
                        ins = nc.tensor.transpose(TP[i][:, g * P:(g + 1) * P], kv[:, i, g * P:(g + 1) * P], ident[:])
                    ins.then_inc(s_kt, 1)


def norm_transpose(nc, l, sem, sb_in, ps_in, x_of, ident, neg_half, xh, xl):
    s_in = [sem(f"nt{l}_in{i}") for i in range(2)]
    s_sq, s_ms, s_rs, s_xn, s_tp, s_hi, s_lo = (sem(f"nt{l}_{n}") for n in ("sq", "ms", "rs", "xn", "tp", "hi", "lo"))
    with ExitStack() as ctx:
        sb, ps = sb_in(ctx), ps_in(ctx)
        xt = [sb(f"nt{l}_x{i}", [P, D]) for i in range(2)]
        xn = [sb(f"nt{l}_xn{i}", [P, D]) for i in range(2)]
        sq = sb(f"nt{l}_sq", [P, D])
        ss = sb(f"nt{l}_ss", [P, 2])
        ms = sb(f"nt{l}_ms", [P, 2])
        rs = sb(f"nt{l}_rs", [P, 2])
        TP = [[ps(f"nt{l}_tp{i}{h}", [P, 512]) for h in range(2)] for i in range(2)]
        with nc.Block() as block:
            @block.sync
            def _(sp):
                def body(t, p):
                    wait(sp, s_xn, t - 1)
                    sp.dma_start(xt[p][:], x_of(t)).then_inc(s_in[p], 16)
                sweep(sp, 0, NT, 2, body)
                body(TS, TS % 2)

            def square(act, t, p):
                act.wait_ge(s_in[p], in_count(t, p))
                wait(act, s_ms, t - 1)
                wait(act, s_sq, t)
                nc.scalar.activation(sq[:], xt[p][:], ACT.Square, accum_out=ss[:, p:p + 1]).then_inc(s_sq, 1)

            def in_count(t, p):
                return (t - p) * 8 + 16

            @block.scalar
            def _(act):
                square(act, 0, 0)

                def body(t, p, last=False):
                    if not last:
                        square(act, t + 1, 1 - p)
                    for h in range(2):
                        act.wait_ge(s_tp, t * 2 + (h + 1))
                        nc.scalar.copy(xh[:, 4 * h:4 * h + 4, bass.ds(t * P, P)],
                                       TP[p][h][:].rearrange("p (k n) -> p k n", n=P)).then_inc(s_hi, 1)
                sweep(act, 0, NT, 2, body)
                body(TS, TS % 2, last=True)

            @block.gpsimd
            def _(pool):
                def body(t, p):
                    pool.wait_ge(s_ms, t + 1)
                    wait(pool, s_xn, t - 1)
                    nc.gpsimd.tensor_tensor(rs[:, p:p + 1], ms[:, p:p + 1], neg_half[:, 0:1], ALU.pow).then_inc(s_rs, 1)
                sweep(pool, 0, NT, 2, body)
                body(TS, TS % 2)

            @block.vector
            def _(dve):
                def norm(t, p):
                    dve.wait_ge(s_sq, t + 1)
                    wait(dve, s_rs, t - 1)
                    nc.vector.tensor_scalar(ms[:, p:p + 1], ss[:, p:p + 1], 1.0 / D, EPS, ALU.mult, ALU.add).then_inc(s_ms, 1)
                    dve.wait_ge(s_rs, t + 1)
                    wait(dve, s_tp, t * 2 - 2)
                    nc.vector.tensor_scalar(xn[p][:], xt[p][:], rs[:, p:p + 1], None, ALU.mult).then_inc(s_xn, 1)
                norm(0, 0)

                def body(t, p, last=False):
                    if not last:
                        norm(t + 1, 1 - p)
                    for h in range(2):
                        dve.wait_ge(s_hi, t * 2 + (h + 1))
                        nc.vector.tensor_tensor(xl[:, 4 * h:4 * h + 4, bass.ds(t * P, P)],
                                                TP[p][h][:].rearrange("p (k n) -> p k n", n=P),
                                                xh[:, 4 * h:4 * h + 4, bass.ds(t * P, P)].bitcast(F32),
                                                ALU.subtract).then_inc(s_lo, 1)
                sweep(dve, 0, NT, 2, body)
                body(TS, TS % 2, last=True)

            @block.tensor
            def _(pe):
                def body(t, p):
                    pe.wait_ge(s_xn, t + 1)
                    wait(pe, s_lo, t * 2 - 2)
                    for k in range(KD):
                        ins = nc.tensor.transpose(TP[p][k // 4][:, (k % 4) * P:(k % 4 + 1) * P],
                                                  xn[p][:, k * P:(k + 1) * P], ident[:])
                        if k % 4 == 3:
                            ins.then_inc(s_tp, 1)
                sweep(pe, 0, NT, 2, body)
                body(TS, TS % 2)


def project(nc, l, sem, sb_in, ps_in, xh, xl, w_in, g_ln, lb, lb1, proj, kgate):
    s_w = sem.software(f"pj{l}_w")
    s_wg, s_wh, s_wl, s_mm, s_free, s_stage, s_sig, s_act = (
        sem(f"pj{l}_{n}") for n in ("wg", "wh", "wl", "mm", "free", "stage", "sig", "act"))
    s_st = [sem(f"pj{l}_st{b}") for b in range(NBLK)]
    s_st2 = [sem(f"pj{l}_st2{b}") for b in range(NBLK)]
    plain, gate, forget = "plain", "gate", "forget"
    if l == 0:
        parts = [(GQ, GK, plain, -HD ** -0.5), (GK, GX, plain, 1.0), (GX, GG, plain, -HD ** -0.5), (GG, NG, gate, 1.0)]
    else:
        parts = [(GQ, GK, plain, 1.0), (GK, GV, forget, 1.0), (GV, GX, plain, 1.0), (GX, GG, plain, -HD ** -0.5),
                 (GG, NG, gate, 1.0)]
    with ExitStack() as ctx:
        sb, ps = sb_in(ctx), ps_in(ctx)
        wraw = sb(f"pj{l}_wraw", [P, KD, 2 * P])
        wg = sb(f"pj{l}_wg", [P, KD, P])
        wh = [sb(f"pj{l}_wh{i}", [P, KD, P], F32R) for i in range(2)]
        wl = [sb(f"pj{l}_wl{i}", [P, KD, P], F32R) for i in range(2)]
        stage = [sb(f"pj{l}_stg{b}", [P, BLOCKS[b][1]]) for b in range(NBLK)]
        stage2 = [sb(f"pj{l}_stg2{b}", [P, BLOCKS[b][1]]) for b in range(NBLK)]
        acc = [ps(f"pj{l}_acc{b}", [P, 512]) for b in range(NBLK)]
        w_pairs = w_in[l].rearrange("(k p) (c n) -> c p k n", p=P, n=2 * P)
        with nc.Block() as block:
            @block.gpsimd
            def _(pool):
                def body(i, _):
                    wait(pool, s_wg, i * 2)
                    pool.dma_start(wraw[:], w_pairs[i]).then_inc(s_w, 16)
                sweep(pool, 0, NG // 2, 1, body)

            @block.sync
            def _(sp):
                for lo, hi, kind, _ in parts:
                    def body(c, _):
                        for b, (at, n) in enumerate(BLOCKS):
                            sp.wait_ge(s_stage, c * NBLK + (b + 1))
                            sp.dma_start(proj[c][:, at:at + n], stage[b][:]).then_inc(s_st[b], 16)
                            if kind == forget:
                                sp.dma_start(kgate[c - GK][:, at:at + n], stage2[b][:]).then_inc(s_st2[b], 16)
                    sweep(sp, lo, hi, 1, body)
                for b in range(NBLK):
                    sp.wait_ge(s_st[b], 16 * NG)
                    if l == 1:
                        sp.wait_ge(s_st2[b], 16 * MG)

            @block.scalar
            def _(act):
                def high(c, p):
                    act.wait_ge(s_wg, c + 1)
                    wait(act, s_mm, (c - 1) * NBLK)
                    nc.scalar.copy(wh[p][:], wg[:]).then_inc(s_wh, 1)
                high(0, 0)
                for lo, hi, kind, scale in parts:
                    def body(c, p):
                        if not (isinstance(c, int) and c == NG - 1):
                            high(c + 1, 1 - p)
                        for b, (at, n) in enumerate(BLOCKS):
                            act.wait_ge(s_mm, c * NBLK + (b + 1))
                            wait(act, s_st[b], c * 16)
                            if kind == plain:
                                nc.scalar.mul(stage[b][:], acc[b][:, 0:n], scale).then_inc(s_stage, 1)
                            elif kind == gate:
                                nc.scalar.activation(stage[b][:], acc[b][:, 0:n], ACT.Sigmoid).then_inc(s_sig, 1)
                            else:
                                if not (isinstance(c, int) and c == GK):
                                    act.wait_ge(s_st2[b], (c - GK) * 16)
                                nc.scalar.activation(stage[b][:], acc[b][:, 0:n], ACT.Sigmoid)
                                nc.scalar.activation(stage2[b][:], acc[b][:, 0:n], ACT.Sigmoid, scale=-1.0).then_inc(s_sig, 1)
                    if hi == NG:
                        sweep(act, lo, hi - 2, 2, body)
                        body(hi - 2, 0)
                        body(hi - 1, 1)
                    else:
                        sweep(act, lo, hi, 2, body)

            @block.vector
            def _(dve):
                def low(c, p):
                    wait(dve, s_w, (c - p) * 8 + 16)
                    wait(dve, s_wl, c)
                    nc.vector.tensor_tensor(wg[:], wraw[:, :, p * P:(p + 1) * P],
                                            g_ln[:, l].unsqueeze(2).to_broadcast([P, KD, P]), ALU.mult).then_inc(s_wg, 1)
                    dve.wait_ge(s_wh, c + 1)
                    nc.vector.tensor_tensor(wl[p][:], wg[:], wh[p][:].bitcast(F32), ALU.subtract).then_inc(s_wl, 1)
                low(0, 0)
                seen = 0
                for lo, hi, kind, _ in parts:
                    def body(c, p):
                        if not (isinstance(c, int) and c == NG - 1):
                            low(c + 1, 1 - p)
                        if kind == plain:
                            return
                        for b, (at, n) in enumerate(BLOCKS):
                            dve.wait_ge(s_sig, (c - lo + seen) * NBLK + (b + 1))
                            if kind == gate:
                                nc.vector.tensor_tensor(stage[b][:], acc[b][:, 0:n], stage[b][:], ALU.mult).then_inc(s_stage, 1)
                            else:
                                g = bass.ds(c - GK, 1)
                                nc.vector.tensor_scalar(stage2[b][:], stage2[b][:], lb1[:, g], None, ALU.mult)
                                nc.vector.tensor_scalar(stage[b][:], stage[b][:], lb1[:, g], lb[:, g],
                                                        ALU.mult, ALU.add).then_inc(s_stage, 1)
                    if hi == NG:
                        sweep(dve, lo, hi - 2, 2, body)
                        body(hi - 2, 0)
                        body(hi - 1, 1)
                    else:
                        sweep(dve, lo, hi, 2, body)
                    if kind != plain:
                        seen += hi - lo

            @block.tensor
            def _(pe):
                def body(c, p):
                    pe.wait_ge(s_wl, c + 1)
                    for b, (at, n) in enumerate(BLOCKS):
                        wait(pe, s_stage, c * NBLK - NBLK + (b + 1))
                        for k in range(KD):
                            for w, x in ((wh, xh), (wl, xh), (wh, xl)):
                                ins = nc.tensor.matmul(acc[b][:, 0:n], w[p][:, k], x[:, k, at:at + n],
                                                       start=(k == 0 and x is xh and w is wh),
                                                       stop=(k == KD - 1 and x is xl))
                        ins.then_inc(s_mm, 1)
                sweep(pe, 0, NG, 2, body)


def keys_out(nc, sem, sb_in, ps_in, ident, proj, a_k_prompt, a_v_prompt, a_k_sample, a_v_sample):
    s_in = [sem(f"ko_in{i}") for i in range(2)]
    s_out = [sem.software(f"ko_out{i}") for i in range(2)]
    s_tp, s_ev = sem("ko_tp"), sem("ko_ev")
    jobs = [(g, t) for t in range(NT - 4, NT + 1) for g in (GK, GV)]
    with ExitStack() as ctx:
        sb, ps = sb_in(ctx), ps_in(ctx)
        src = [sb(f"ko_src{i}", [P, MG, P]) for i in range(2)]
        dst = [sb(f"ko_dst{i}", [P, MIX]) for i in range(2)]
        TP = [[ps(f"ko_tp{i}{h}", [P, 512]) for h in range(2)] for i in range(2)]
        with nc.Block() as block:
            @block.sync
            def _(sp):
                for n, (g, t) in enumerate(jobs):
                    wait(sp, s_tp, n - 1)
                    sp.dma_start(src[n % 2][:], proj[g:g + MG, :, t * P:(t + 1) * P].rearrange("g p n -> p g n")
                                 ).then_inc(s_in[n % 2], 16)

            @block.gpsimd
            def _(pool):
                for n, (g, t) in enumerate(jobs):
                    pool.wait_ge(s_ev, 2 * n + 2)
                    if t == TS:
                        out = (a_k_sample if g == GK else a_v_sample)[0].rearrange("b s h d -> (b s) (h d)")
                    else:
                        r = (t - (NT - 4)) * P
                        out = (a_k_prompt if g == GK else a_v_prompt)[0, 0, r:r + P].rearrange("p h d -> p (h d)")
                    pool.dma_start(out, dst[n % 2][:]).then_inc(s_out[n % 2], 16)
                for i in range(2):
                    pool.wait_ge(s_out[i], 16 * (len(jobs) // 2))

            @block.tensor
            def _(pe):
                for n in range(len(jobs)):
                    pe.wait_ge(s_in[n % 2], 16 * (n // 2 + 1))
                    wait(pe, s_ev, 2 * n - 2)
                    for g in range(MG):
                        ins = nc.tensor.transpose(TP[n % 2][g // 3][:, (g % 3) * P:(g % 3 + 1) * P], src[n % 2][:, g], ident[:])
                    ins.then_inc(s_tp, 1)

            @block.vector
            def _(dve):
                for n in range(len(jobs)):
                    dve.wait_ge(s_tp, n + 1)
                    wait(dve, s_out[n % 2], 16 * (n // 2))
                    for h in range(2):
                        nc.vector.tensor_copy(dst[n % 2][:, h * 384:(h + 1) * 384], TP[n % 2][h][:, 0:384]).then_inc(s_ev, 1)


class Unit:

    def __init__(self, col, tiles, split, score, bias, pv, heads=(0,), at=None):
        self.col, self.tiles, self.split, self.score, self.bias, self.pv = col, tiles, split, score, bias, pv
        self.width = tiles * P
        self.heads = heads
        self.at = at


def tp_cols(unit, i):
    return i * P if i < unit.split else 512 + (i - unit.split) * P


def unit_scores(nc, unit, sc):
    for cols, rows, q, k in unit.score:
        ins = nc.tensor.matmul(sc[rows, cols], q, k, start=True, stop=True)
    return ins


def unit_min(nc, unit, sc, se, minimum):
    n = unit.width
    if unit.bias is None:
        return nc.vector.tensor_reduce(minimum, sc[:, 0:n].rearrange("p (h k) -> p h k", h=len(unit.heads)), AX_X, ALU.min)
    return nc.vector.tensor_tensor_reduce(se[:, 0:n], sc[:, 0:n], unit.bias, 1.0, 3e38, ALU.add, ALU.min, minimum)


def unit_exp(nc, unit, sc, se, minimum, total):
    src = sc if unit.bias is None else se
    w = unit.width // len(unit.heads)
    for i, h in enumerate(unit.heads):
        ins = nc.scalar.activation(se[:, i * w:(i + 1) * w], src[:, i * w:(i + 1) * w], ACT.Exp, bias=minimum[:, i:i + 1],
                                   scale=-1.0, accum_out=total[:, h:h + 1])
    return ins


def unit_transposes(nc, unit, se, tp, ident):
    for i in range(unit.tiles):
        at = tp_cols(unit, i)
        ins = nc.tensor.transpose(tp[:, at:at + P], se[:, i * P:(i + 1) * P], ident[:])
    return ins


def unit_evac_low(unit, copy, pt, tp):
    if unit.tiles == 1:
        return copy(pt[0:64, 0:P], tp[0:64, 0:P])
    return copy(pt[:, 0:unit.split * P], tp[:, 0:unit.split * P])


def unit_evac_high(unit, copy, pt, tp):
    if unit.tiles == 1:
        return copy(pt[64:P, 0:P], tp[64:P, 0:P])
    n = (unit.tiles - unit.split) * P
    return copy(pt[:, unit.split * P:unit.width], tp[:, 512:512 + n])


def unit_pv(nc, unit, pt, ob):
    first = {}
    last = {}
    def head(i):
        return unit.heads[i * len(unit.heads) // unit.tiles]

    def sum_of(rows, i):
        return rows.start, head(i)
    for n, (rows, i, *_) in enumerate(unit.pv):
        first.setdefault(sum_of(rows, i), n)
        last[sum_of(rows, i)] = n
    for n, (rows, i, cols, val) in enumerate(unit.pv):
        col = unit.col + head(i) * HD
        ins = nc.tensor.matmul(ob[rows, col:col + HD], pt[:, i * P + cols.start:i * P + cols.stop], val,
                               start=first[sum_of(rows, i)] == n, stop=last[sum_of(rows, i)] == n)
    return ins


ALL = slice(0, P)


def cross_unit(q, keys, vals, at):
    score = []
    heads = tuple(range(0, HX, 2)) + tuple(range(1, HX, 2))
    for c, h in enumerate(heads):
        g, po = h // 2, HD * (h % 2)
        score.append((slice(c * NMEM, (c + 1) * NMEM), ALL, q[po:po + HD, g], keys[po:po + HD, g]))
    n = NMEM // P
    return Unit(MIX, HX * n, HX * n // 2, score, None,
                [(ALL, n * c + i, ALL, vals[:, i, h * HD:(h + 1) * HD]) for c, h in enumerate(heads) for i in range(n)],
                heads=heads, at=slice(at, at + HX))


def sample_attention(nc, name, sem, sb_in, ps_in, ident, units_of, loads, o_s, bias_width, extra=None):
    s_ld, s_tp, s_eva, s_evd, s_sc, s_min, s_exp, s_pv, s_rs, s_bias = (
        sem(f"{name}_{n}") for n in ("ld", "tp", "eva", "evd", "sc", "min", "exp", "pv", "rs", "bias"))
    with ExitStack() as ctx:
        sb, ps = sb_in(ctx), ps_in(ctx)
        bufs, dmas, turns = loads(sb)
        se = [sb(f"{name}_se{i}", [P, bias_width]) for i in range(2)]
        pt = [sb(f"{name}_pt{i}", [P, bias_width]) for i in range(2)]
        mn = sb(f"{name}_mn", [P, 16])
        tot = sb(f"{name}_tot", [P, 16])
        rs = sb(f"{name}_rs", [P, 16])
        SC = [ps(f"{name}_SC{i}", [P, 1024]) for i in range(2)]
        TP = ps(f"{name}_TP", [P, 1024])
        OB = ps(f"{name}_OB", [P, 1024])
        units = units_of(bufs)
        U, NR = len(units), len(turns)
        o_cols = slice(units[0].col, units[-1].col + HD)
        with nc.Block() as block:
            @block.sync
            def _(sp):
                for out, src in dmas:
                    sp.dma_start(out, src).then_inc(s_ld, 16)

            @block.gpsimd
            def _(pool):
                pool.wait_ge(s_ld, 16 * len(dmas))
                if extra:
                    extra(bufs, pool, s_bias)

            @block.tensor
            def _(pe):
                pe.wait_ge(s_ld, 16 * len(dmas))
                for n, (srcs, _) in enumerate(turns):
                    wait(pe, s_eva, n)
                    wait(pe, s_evd, n)
                    for i, src in enumerate(srcs):
                        at = i % (len(srcs) // 2) * P + 512 * (i // (len(srcs) // 2))
                        ins = nc.tensor.transpose(TP[:, at:at + P], src, ident[:])
                    ins.then_inc(s_tp, 1)

                def scores(u):
                    wait(pe, s_exp, u - 1)
                    unit_scores(nc, units[u], SC[u % 2]).then_inc(s_sc, 1)

                def values(u):
                    pe.wait_ge(s_eva, NR + u + 1)
                    pe.wait_ge(s_evd, NR + u + 1)
                    unit_pv(nc, units[u], pt[u % 2], OB).then_inc(s_pv, 1)
                pe.wait_ge(s_eva, NR)
                pe.wait_ge(s_evd, NR)
                scores(0)
                scores(1)
                for u in range(U):
                    pe.wait_ge(s_exp, u + 1)
                    wait(pe, s_eva, NR + u)
                    wait(pe, s_evd, NR + u)
                    unit_transposes(nc, units[u], se[u % 2], TP, ident).then_inc(s_tp, 1)
                    if u:
                        values(u - 1)
                    if u + 2 < U:
                        scores(u + 2)
                values(U - 1)

            @block.vector
            def _(dve):
                def low_min(u):
                    dve.wait_ge(s_sc, u + 1)
                    unit_min(nc, units[u], SC[u % 2], se[u % 2], mn[:, u:u + 1]).then_inc(s_min, 1)
                for n, (srcs, dst) in enumerate(turns):
                    dve.wait_ge(s_tp, n + 1)
                    half = len(srcs) // 2
                    nc.vector.tensor_copy(dst[1], TP[:, 512:512 + half * P].rearrange("p (g n) -> p g n", n=P)
                                          ).then_inc(s_evd, 1)
                if extra:
                    dve.wait_ge(s_bias, 1)
                low_min(0)
                low_min(1)
                for u in range(U):
                    dve.wait_ge(s_tp, NR + u + 1)
                    unit_evac_high(units[u], nc.vector.tensor_copy, pt[u % 2], TP).then_inc(s_evd, 1)
                    if u + 2 < U:
                        low_min(u + 2)
                dve.wait_ge(s_pv, U)
                nc.vector.reciprocal(rs[:, 0:U], tot[:, 0:U]).then_inc(s_rs, 1)
                dve.wait_ge(s_rs, 1)
                for c in range(o_cols.start, o_cols.stop, 256):
                    u0 = (c - o_cols.start) // HD
                    nc.vector.tensor_tensor(o_s[:, c:c + 256].rearrange("p (h d) -> p h d", d=HD),
                                            OB[:, c:c + 256].rearrange("p (h d) -> p h d", d=HD),
                                            rs[:, u0:u0 + 4].unsqueeze(2).to_broadcast([P, 4, HD]), ALU.mult)

            @block.scalar
            def _(act):
                def exp(u):
                    act.wait_ge(s_min, u + 1)
                    unit_exp(nc, units[u], SC[u % 2], se[u % 2], mn[:, u:u + 1], tot[:, u:u + 1]).then_inc(s_exp, 1)
                for n, (srcs, dst) in enumerate(turns):
                    act.wait_ge(s_tp, n + 1)
                    half = len(srcs) // 2
                    nc.scalar.copy(dst[0], TP[:, 0:half * P].rearrange("p (g n) -> p g n", n=P)).then_inc(s_eva, 1)
                exp(0)
                exp(1)
                for u in range(U):
                    act.wait_ge(s_tp, NR + u + 1)
                    unit_evac_low(units[u], nc.scalar.copy, pt[u % 2], TP).then_inc(s_eva, 1)
                    if u + 2 < U:
                        exp(u + 2)


def halves(h, po, g, q, keys, new, vals, vnew, tiles, split, bias, col):
    score, pv = [], []
    n = tiles - (1 if new is not None else 0)
    for half in range(2):
        rows = slice(64 * half, 64 * half + 64)
        for at in range(0, n * P, 512):
            score.append((slice(at, at + 512), rows, q[po:po + HD, g, rows], keys[po:po + HD, g, n * P * half + at:n * P * half + at + 512]))
    if new is not None:
        score.append((slice(n * P, n * P + P), ALL, q[po:po + HD, g], new[po:po + HD, g]))
    for half in range(2):
        rows = slice(64 * half, 64 * half + 64)
        for i in range(tiles):
            v = vals[:, n * half + i, h * HD:(h + 1) * HD] if i < n else vnew[:, h * HD:(h + 1) * HD]
            pv.append((rows, i, rows, v))
    return Unit(col, tiles, split, score, bias, pv)


def sample_band(nc, sem, sb_in, ps_in, v, o_s):
    ident, proj, ext, seqmask = v["ident"], v["proj"], v["ext"], v["seqmask"]
    ck = v["cache_a_k"][0].rearrange("b s h d -> s b (h d)")
    cv = v["cache_a_v"][0].rearrange("b s h d -> s b (h d)")
    vn = v["a_v_sample"][0].rearrange("b s h d -> (b s) (h d)")
    tok = slice(SEQ, NTOK)

    def loads(sb):
        raw = sb("sa_raw", [P, SB, MIX])
        kT = sb("sa_kT", [P, MG, SB * P])
        vals = sb("sa_v", [P, SB, MIX])
        knew = sb("sa_knew", [P, MG, P])
        vnew = sb("sa_vnew", [P, MIX])
        q = sb("sa_q", [P, MG, P])
        tb = sb("sa_tb", [P, HA, P])
        tn = sb("sa_tn", [P, HA, SL])
        bias = sb("sa_bias", [P, HA, 5 * P])
        off = sb("sa_off", [P, 4])
        offn = sb("sa_offn", [P, SB])
        dmas = [(raw[:], ck), (vals[:], cv),
                (q[:], proj[GQ:GQ + MG, :, tok].rearrange("g p n -> p g n")),
                (knew[:], proj[GK:GK + MG, :, tok].rearrange("g p n -> p g n")), (vnew[:], vn)]
        for b in range(SB):
            rows = slice(b * SL, (b + 1) * SL)
            dmas.append((tb[rows], bass.AP(ext.tensor, 511, [[767, SL], [P * 768, HA], [1, P]])))
            dmas.append((tn[rows], bass.AP(ext.tensor, 639, [[767, SL], [P * 768, HA], [1, SL]])))
        turns = [([raw[:, b, g * P:(g + 1) * P] for g in range(MG)],
                  (kT[:, 0:3, b * P:(b + 1) * P], kT[:, 3:6, b * P:(b + 1) * P])) for b in range(SB)]
        return (kT, vals, knew, vnew, q, tb, tn, bias, off, offn), dmas, turns

    def units_of(bufs):
        kT, vals, knew, vnew, q, tb, tn, bias, off, offn = bufs
        return [halves(h, HD * (h % 2), h // 2, q, kT, knew, vals, vnew, 5, 3, bias[:, h], h * HD) for h in range(HA)]

    def extra(bufs, pool, s_bias):
        kT, vals, knew, vnew, q, tb, tn, bias, off, offn = bufs
        link = Chain(pool, sem("sa_cpool"))
        link(nc.gpsimd.tensor_tensor(off[:], seqmask[:, 0:4], seqmask[:, 4:8], ALU.add))
        link(nc.gpsimd.tensor_scalar(off[:], off[:], -BIG, BIG, ALU.mult, ALU.add))
        link(nc.gpsimd.tensor_scalar(offn[:], seqmask[:], -BIG, BIG, ALU.mult, ALU.add))
        for i in range(4):
            nc.gpsimd.tensor_scalar(bias[:, :, i * P:(i + 1) * P], tb[:], off[:, i:i + 1], None, ALU.add)
        for b in range(SB):
            ins = nc.gpsimd.tensor_scalar(bias[:, :, 4 * P + b * SL:4 * P + (b + 1) * SL], tn[:], offn[:, b:b + 1], None,
                                          ALU.add)
        ins.then_inc(s_bias, 1)

    sample_attention(nc, "sa", sem, sb_in, ps_in, ident, units_of, loads, o_s, 5 * P, extra)


def sample_cross(nc, l, sem, sb_in, ps_in, v, o_s):
    ident, proj, seqmask = v["ident"], v["proj"], v["seqmask"]
    ck = v["cache_mem_k"][l].rearrange("b (t p) h d -> p (b t) (h d)", p=P)
    cv = v["cache_mem_v"][l].rearrange("b (t p) h d -> p (b t) (h d)", p=P)
    name = f"sx{l}"

    def loads(sb):
        raw = sb(f"{name}_raw", [P, 2 * SB, XW])
        kT = sb(f"{name}_kT", [P, 2, 2 * SB * P])
        vals = sb(f"{name}_v", [P, 2 * SB, XW])
        q = sb(f"{name}_q", [P, 2, P])
        off = sb(f"{name}_off", [P, 4])
        bias = sb(f"{name}_bias", [P, 4, 2 * P])
        dmas = [(raw[:], ck), (vals[:], cv), (q[:], proj[GX:GX + 2, :, SEQ:NTOK].rearrange("g p n -> p g n"))]
        turns = [([raw[:, 2 * b + t, g * P:(g + 1) * P] for g in range(2) for t in range(2)],
                  (kT[:, 0, b * 2 * P:(b + 1) * 2 * P].rearrange("p (t n) -> p t n", n=P),
                   kT[:, 1, b * 2 * P:(b + 1) * 2 * P].rearrange("p (t n) -> p t n", n=P))) for b in range(SB)]
        return (kT, vals, q, off, bias), dmas, turns

    def units_of(bufs):
        kT, vals, q, off, bias = bufs
        flat = bias[:].rearrange("p b n -> p (b n)")
        return [halves(h, HD * (h % 2), h // 2, q, kT, None, vals, None, 8, 4, flat, MIX + h * HD) for h in range(HX)]

    def extra(bufs, pool, s_bias):
        kT, vals, q, off, bias = bufs
        link = Chain(pool, sem(f"{name}_cpool"))
        link(nc.gpsimd.tensor_tensor(off[:], seqmask[:, 0:4], seqmask[:, 4:8], ALU.add))
        link(nc.gpsimd.tensor_scalar(off[:], off[:], -BIG, BIG, ALU.mult, ALU.add))
        nc.gpsimd.tensor_copy(bias[:], off[:].unsqueeze(2).to_broadcast([P, 4, 2 * P])).then_inc(s_bias, 1)

    sample_attention(nc, name, sem, sb_in, ps_in, ident, units_of, loads, o_s, 8 * P, extra)


def sample_hgrn(nc, sem, sb_in, ps_in, v, o_s):
    ident, proj, seqmask, neg_half = v["ident"], v["proj"], v["seqmask"], v["neg_half"]
    tok = slice(SEQ, NTOK)
    LEVELS = 5
    s_ld, s_st, s_tp, s_ev, s_lv, s_cp, s_qz, s_o, s_kz, s_kv, s_s, s_oc, s_sq, s_ms, s_rs, s_out, c_pool, c_dve = (
        sem(f"sh_{n}") for n in ("ld", "st", "tp", "ev", "lv", "cp", "qz", "o", "kz", "kv", "s", "oc", "sq", "ms", "rs",
                                 "out", "cpool", "cdve"))
    with ExitStack() as ctx:
        sb, ps = sb_in(ctx), ps_in(ctx)
        q, f, k, iT = (sb(f"sh_{n}", [P, MIX]) for n in ("q", "f", "k", "iT"))
        qm = {m: sb(f"sh_q{m}", [P, MIX]) for m in (1, 2, 4, 8, 16)}
        km = {m: sb(f"sh_k{m}", [P, MIX]) for m in (2, 4, 8, 16)}
        tm = {m: sb(f"sh_t{m}", [P, MIX // m]) for m in (2, 4, 8, 16)}
        qm[0], km[0], km[1], tm[1] = q, k, k, f
        am, inat, knat = (sb(f"sh_{n}", [P, MIX]) for n in ("a", "inat", "knat"))
        masks = sb("sh_masks", [P, LEVELS, P])
        st = sb("sh_state", [P, SB, MG, P])
        qz = [sb(f"sh_qz{i}", [P, SB * P]) for i in range(2)]
        kz = [sb(f"sh_kz{i}", [P, SB, P]) for i in range(2)]
        sq = sb("sh_sq", [P, MIX])
        ssq, ms, rs = (sb(f"sh_{n}", [P, MG]) for n in ("ssq", "ms", "rs"))
        SC = [ps(f"sh_SC{i}", [P, 1024]) for i in range(2)]
        TP = ps("sh_TP", [P, 1024])
        OB = ps("sh_OB", [P, 1024])
        with nc.Block() as block:
            @block.sync
            def _(sp):
                for buf, src in ((q, proj[GQ:GQ + MG, :, tok]), (f, proj[GK:GK + MG, :, tok]), (k, v["kgate"][:, :, tok]),
                                 (iT, proj[GV:GV + MG, :, tok])):
                    sp.dma_start(buf[:].rearrange("p (g n) -> p g n", n=P), src.rearrange("g p n -> p g n")).then_inc(s_ld, 16)
                for h in range(MG):
                    sp.dma_start(st[:, :, h], v["state_b"][0, :, h].rearrange("b k v -> k b v")).then_inc(s_st, 16)
                for h in range(MG):
                    sp.wait_ge(s_s, h + 1)
                    sp.dma_start(v["b_state_sample"][0, :, h].rearrange("b k v -> k b v"), st[:, :, h]).then_inc(s_out, 16)
                sp.wait_ge(s_out, 16 * MG)

            @block.gpsimd
            def _(pool):
                link = Chain(pool, c_pool)
                link(nc.gpsimd.memset(masks[:], 1.0))
                link(nc.gpsimd.affine_select(out=masks[:, 0], in_=masks[:, 0], compare_op=ALU.is_equal, fill=0.0,
                                             base=0, pattern=[[-1, P]], channel_multiplier=1))
                for i in range(1, LEVELS):
                    m = 1 << (i - 1)
                    nb = P // (2 * m)
                    view = masks[:, i].rearrange("p (b two m) -> p b two m", two=2, m=m)
                    link(nc.gpsimd.memset(view[:, :, 0, :], 0.0))
                    sel = view[:, :, 1, :]
                    link(nc.gpsimd.affine_select(out=sel, in_=sel, compare_op=ALU.is_ge, fill=0.0, base=0,
                                                 pattern=[[-2 * m, nb], [0, m]], channel_multiplier=1))
                    link(nc.gpsimd.affine_select(out=sel, in_=sel, compare_op=ALU.is_ge, fill=0.0, base=m - 1,
                                                 pattern=[[2 * m, nb], [0, m]], channel_multiplier=-1))
                for z in (am, qz[0], qz[1]):
                    link(nc.gpsimd.memset(z[:], 0.0))
                pool.wait_ge(s_ms, 1)
                nc.gpsimd.tensor_tensor(rs[:], ms[:], neg_half[:, 0:MG], ALU.pow).then_inc(s_rs, 1)
            N_POOL = 2 + 3 * (LEVELS - 1) + 3

            def update(h, dve, link):
                dve.wait_ge(s_o, h + 1)
                link(nc.vector.tensor_tensor(st[:, :, h], st[:, :, h],
                                             tm[16][:, h * SB:(h + 1) * SB].unsqueeze(2).to_broadcast([P, SB, P]), ALU.mult))
                dve.wait_ge(s_kv, h + 1)
                for c in range(2):
                    bs = slice(4 * c, 4 * c + 4)
                    ins = nc.vector.tensor_tensor(st[:, bs, h], st[:, bs, h],
                                                  SC[h % 2][:, 512 * c:512 * c + 512].rearrange("p (b v) -> p b v", v=P), ALU.add)
                ins.then_inc(s_s, 1)

            @block.scalar
            def _(act):
                act.wait_ge(s_oc, 1)
                nc.scalar.activation(sq[:], o_s[:, 0:MIX], ACT.Square).then_inc(s_sq, 1)

            @block.vector
            def _(dve):
                link = Chain(dve, c_dve)
                dve.wait_ge(s_ld, 64)
                dve.wait_ge(c_pool, N_POOL)
                link(nc.vector.tensor_tensor(qm[1][:], q[:], f[:], ALU.mult))
                for m in (1, 2, 4, 8):
                    n = MIX // (2 * m)

                    def two(a, width=m):
                        return a[:].rearrange("p (n two m) -> p n two m", two=2, m=width)
                    tot = two(tm[m], 1)
                    nc.vector.tensor_copy(two(qm[2 * m])[:, :, 0], two(qm[m])[:, :, 0])
                    nc.vector.tensor_copy(two(km[2 * m])[:, :, 1], two(km[m])[:, :, 1])
                    nc.vector.tensor_tensor(two(qm[2 * m])[:, :, 1], two(qm[m])[:, :, 1],
                                            tot[:, :, 0].to_broadcast([P, n, m]), ALU.mult)
                    nc.vector.tensor_tensor(two(km[2 * m])[:, :, 0], two(km[m])[:, :, 0],
                                            tot[:, :, 1].to_broadcast([P, n, m]), ALU.mult)
                    link(nc.vector.tensor_tensor(tm[2 * m][:].unsqueeze(2), tot[:, :, 0], tot[:, :, 1], ALU.mult))
                dve.wait_ge(s_tp, 1)
                nc.vector.tensor_copy(inat[:].rearrange("p (c n) -> p c n", n=384),
                                      TP[:].rearrange("p (c n) -> p c n", n=512)[:, :, 0:384]).then_inc(s_ev, 1)
                for i in range(LEVELS):
                    dve.wait_ge(s_lv, i + 1)
                    nc.vector.copy_predicated(am[:].rearrange("p (c n) -> p c n", n=P),
                                              masks[:, i:i + 1].bitcast(U32).to_broadcast([P, MG, P]),
                                              SC[i % 2][:, 0:MIX].rearrange("p (h n) -> p h n", n=P)).then_inc(s_cp, 1)
                    dve.wait_ge(s_cp, i + 1)
                dve.wait_ge(s_tp, 2)
                nc.vector.tensor_copy(knat[:].rearrange("p (c n) -> p c n", n=384),
                                      TP[:].rearrange("p (c n) -> p c n", n=512)[:, :, 0:384]).then_inc(s_ev, 1)
                dve.wait_ge(s_ev, 2)
                dve.wait_ge(s_st, 16 * MG)
                for h in range(MG):
                    hs = slice(h * P, (h + 1) * P)
                    wait(dve, s_o, h - 1)
                    nc.vector.tensor_copy(bass.AP(qz[h % 2][:].tensor, 0, [[SB * P, P], [P + SL, SB], [1, SL]]),
                                          qm[16][:, hs].rearrange("p (b n) -> p b n", n=SL)).then_inc(s_qz, 1)
                    wait(dve, s_kv, h - 1)
                    nc.vector.tensor_tensor(kz[h % 2][:], knat[:, hs].unsqueeze(1).to_broadcast([P, SB, P]),
                                            seqmask[:].unsqueeze(2).to_broadcast([P, SB, P]), ALU.mult).then_inc(s_kz, 1)
                    if h:
                        update(h - 1, dve, link)
                update(MG - 1, dve, link)
                nc.vector.tensor_copy(o_s[:, 0:512], OB[:, 0:512])
                nc.vector.tensor_copy(o_s[:, 512:MIX], OB[:, 512:MIX]).then_inc(s_oc, 1)
                dve.wait_ge(s_sq, 1)
                link(nc.vector.tensor_reduce(ssq[:], sq[:].rearrange("p (h d) -> p h d", d=P), AX_X, ALU.add))
                nc.vector.tensor_scalar(ms[:], ssq[:], 1.0 / P, EPS, ALU.mult, ALU.add).then_inc(s_ms, 1)
                dve.wait_ge(s_rs, 1)
                nc.vector.tensor_tensor(o_s[:, 0:MIX].rearrange("p (h d) -> p h d", d=P),
                                        o_s[:, 0:MIX].rearrange("p (h d) -> p h d", d=P),
                                        rs[:].unsqueeze(2).to_broadcast([P, MG, P]), ALU.mult)

            @block.tensor
            def _(pe):
                def turn(src):
                    for g in range(MG):
                        at = (g % 3) * P + 512 * (g // 3)
                        ins = nc.tensor.transpose(TP[:, at:at + P], src[:, g * P:(g + 1) * P], ident[:])
                    ins.then_inc(s_tp, 1)
                pe.wait_ge(s_ld, 64)
                pe.wait_ge(c_dve, 5)
                turn(iT)
                for i in range(LEVELS):
                    wait(pe, s_cp, i - 1)
                    m = 0 if i == 0 else 1 << (i - 1)
                    for h in range(MG):
                        hs = slice(h * P, (h + 1) * P)
                        ins = nc.tensor.matmul(SC[i % 2][:, hs], km[m][:, hs], qm[m][:, hs], start=True, stop=True)
                    ins.then_inc(s_lv, 1)
                pe.wait_ge(s_ev, 1)
                turn(km[16])
                pe.wait_ge(s_cp, LEVELS)
                pe.wait_ge(s_st, 16 * MG)
                for h in range(MG):
                    hs = slice(h * P, (h + 1) * P)
                    pe.wait_ge(s_qz, h + 1)
                    nc.tensor.matmul(OB[:, hs], am[:, hs], inat[:, hs], start=True, stop=False)
                    for b in range(SB):
                        ins = nc.tensor.matmul(OB[:, hs], qz[h % 2][:, b * P:(b + 1) * P], st[:, b, h], start=False,
                                               stop=(b == SB - 1))
                    ins.then_inc(s_o, 1)
                    pe.wait_ge(s_kz, h + 1)
                    wait(pe, s_s, h - 1)
                    for b in range(SB):
                        ins = nc.tensor.matmul(SC[h % 2][:, b * P:(b + 1) * P], kz[h % 2][:, b], inat[:, hs], start=True, stop=True)
                    ins.then_inc(s_kv, 1)


def load_w_out(nc, l, sem, sb_in, w_out, g_hgrn, woh, wol):
    s_in = [sem(f"wo{l}_in{i}") for i in range(2)]
    s_g, s_h, s_l = sem(f"wo{l}_g"), sem(f"wo{l}_h"), sem(f"wo{l}_l")
    with ExitStack() as ctx:
        raw = [sb_in(ctx)(f"wo{l}_raw{i}", [P, D]) for i in range(2)]
        with nc.Block() as block:
            @block.sync
            def _(sp):
                for k in range(KD):
                    wait(sp, s_l, k - 1)
                    sp.dma_start(raw[k % 2][:], w_out[l, k * P:(k + 1) * P]).then_inc(s_in[k % 2], 16)

            @block.vector
            def _(dve):
                for k in range(KD):
                    dve.wait_ge(s_in[k % 2], 16 * (k // 2 + 1))
                    g = g_hgrn[:, k:k + 1] if l == 1 and k < MG else 1.0
                    nc.vector.tensor_scalar(raw[k % 2][:], raw[k % 2][:], g, None, ALU.mult).then_inc(s_g, 1)
                    dve.wait_ge(s_h, k + 1)
                    nc.vector.tensor_tensor(wol[:, k], raw[k % 2][:], woh[:, k].bitcast(F32), ALU.subtract).then_inc(s_l, 1)

            @block.scalar
            def _(act):
                for k in range(KD):
                    act.wait_ge(s_g, k + 1)
                    nc.scalar.copy(woh[:, k], raw[k % 2][:]).then_inc(s_h, 1)


def mix(nc, l, software, sb_in, ps_in, v):
    with ExitStack() as ctx:
        sb = sb_in(ctx)
        o_s = sb(f"o_s{l}", [P, D])
        with Semaphores(nc, software) as sem:
            if l == 0:
                sample_band(nc, sem, sb_in, ps_in, v, o_s)
            else:
                sample_hgrn(nc, sem, sb_in, ps_in, v, o_s)
            sample_cross(nc, l, sem, sb_in, ps_in, v, o_s)
        woh = sb(f"woh{l}", [P, KD, D], F32R)
        wol = sb(f"wol{l}", [P, KD, D], F32R)
        with Semaphores(nc, software) as sem:
            load_w_out(nc, l, sem, sb_in, v["w_out"], v["g_hgrn"], woh, wol)
            prompt(nc, l, sem, sb_in, ps_in, v, o_s, woh, wol)


def prompt(nc, l, sem, sb_in, ps_in, v, o_s, woh, wol):
    ident, proj, mem_kT, mem_v, neg_half = (v[n] for n in ("ident", "proj", "mem_kT", "mem_v", "neg_half"))
    band = l == 0
    nm = f"pr{l}_"
    U = (HA if band else 0) + 1
    PRE, MID = 1, (0 if band else 1)
    PER_D, PER_A = PRE + 1 + MID + U, PRE + MID + U
    LEVELS = 8
    both = ["tp", "eva", "evd", "sc", "min", "exp", "pv", "rs", "o", "yg", "yh", "yl", "op", "xadd", "ldg"]
    of_layer = (["vc", "kc", "ld_b", "bias"] if band else
                ["out", "ldf", "fsq", "fms", "frs", "hq", "hst", "hcp", "hv", "ocp", "lv", "cp", "kv", "s", "osq", "oms", "ors", "init"])
    S = {n: sem(nm + n) for n in both + of_layer}
    s_ld = [sem(nm + f"ld{i}") for i in range(2)]
    s_ldk = [sem(nm + f"ldk{i}") for i in range(2 if band else 0)]
    s_ldx = [sem(nm + f"ldx{i}") for i in range(2)]
    s_stx = [sem.software(nm + f"stx{i}") for i in range(2)]
    LOADS = 3 if band else 5
    with ExitStack() as ctx:
        sb, ps = sb_in(ctx), ps_in(ctx)
        xq = [sb(nm + f"xq{i}", [P, 2, P]) for i in range(2)]
        gt = sb(nm + "gate", [P, KD, P])
        xt = [sb(nm + f"x{i}", [P, D]) for i in range(2)]
        se = [sb(nm + f"se{i}", [P, HX * NMEM]) for i in range(min(U, 2))]
        pt = [sb(nm + f"pt{i}", [P, BAND if band else HX * NMEM]) for i in range(min(U, 2))]
        mn = sb(nm + "mn", [P, 16])
        tot = sb(nm + "tot", [P, 16])
        rs = sb(nm + "rs", [P, 16])
        o = sb(nm + "o", [P, D])
        y = sb(nm + "y", [P, D])
        yh = sb(nm + "yh", [P, KD, P], F32R)
        yl = sb(nm + "yl", [P, KD, P], F32R)
        SC = [ps(nm + f"SC{i}", [P, 1024]) for i in range(2)]
        TP = ps(nm + "TP", [P, 1024])
        OB = ps(nm + "OB", [P, 1024])
        tT = sb(nm + "vT", [P, MG, P])
        if band:
            q = [sb(nm + f"q{i}", [P, MG, P]) for i in range(2)]
            kcur, kprev = sb(nm + "kcur", [P, MG, 512]), sb(nm + "kprev", [P, MG, 512])
            vcur, vprev = sb(nm + "vcur", [P, 4, MIX]), sb(nm + "vprev", [P, 4, MIX])
            bias = sb(nm + "bias", [P, HA, BAND])
        else:
            qm = {m: sb(nm + f"q{m}", [P, MIX]) for m in (1, 2, 4, 8, 16, 32, 64, 128)}
            km = {m: sb(nm + f"k{m}", [P, MIX]) for m in (2, 4, 8, 16, 32, 64, 128)}
            tm = {m: sb(nm + f"t{m}", [P, MIX // m]) for m in (2, 4, 8, 16, 32, 64, 128)}
            q = [sb(nm + f"q0{i}", [P, MIX]) for i in range(2)]
            k1 = [sb(nm + f"k1{i}", [P, MIX]) for i in range(2)]
            t1 = [sb(nm + f"t1{i}", [P, MIX]) for i in range(2)]
            am = [sb(nm + f"a{i}", [P, MIX]) for i in range(2)]
            masks = sb(nm + "masks", [P, LEVELS, P])
            inat = sb(nm + "inat", [P, MIX])
            knat = sb(nm + "knat", [P, MIX])
            st = sb(nm + "state", [P, MIX])
            fg = sb(nm + "fg", [P, D])
            ssq = sb(nm + "ssq", [P, 16])
            ms6 = sb(nm + "ms6", [P, 16])
            rs6 = sb(nm + "rs6", [P, 16])
            fs = sb(nm + "fs", [P, 2])
            fm = sb(nm + "fm", [P, 2])
            fr = sb(nm + "fr", [P, 2])

        def units(j, first_block, p):
            out = [cross_unit(xq[p], mem_kT[:, l], mem_v[:, l], HA if band else 0)]
            if band:
                n = j + 1 if first_block else 5
                keys = [(kcur, vcur, i) for i in range(j + 1)]
                if not first_block:
                    keys = [(kprev, vprev, i) for i in range(j, 4)] + keys
                for h in range(HA):
                    g, po = h // 2, HD * (h % 2)
                    score, at = [], 0
                    while at < n:
                        end = at + 1
                        while end < n and keys[end][0] is keys[at][0] and end != 4:
                            end += 1
                        slot = keys[at][2]
                        score.append((slice(at * P, end * P), ALL, q[p][po:po + HD, g],
                                      keys[at][0][po:po + HD, g, slot * P:(slot + end - at) * P]))
                        at = end
                    out.append(Unit(h * HD, n, (n + 1) // 2, score, bias[:, h, (5 - n) * P:],
                                    [(ALL, i, ALL, keys[i][1][:, keys[i][2], h * HD:(h + 1) * HD]) for i in range(n)],
                                    at=slice(h, h + 1)))
            return out

        def d_pre(t):
            return t * PER_D - 1 if not (isinstance(t, int) and t == 0) else 0

        def d_y(t):
            if isinstance(t, int) and t == NT:
                return NT * PER_D - 1
            return t * PER_D + (PRE - 1)

        def d_mid(t):
            return t * PER_D + PRE

        def d_unit(t, u):
            return t * PER_D + (PRE + MID + u)

        def a_pre(t):
            return t * PER_A

        def a_y(t):
            if isinstance(t, int) and t == NT:
                return NT * PER_A
            return t * PER_A + PRE

        def a_unit(t, u):
            return t * PER_A + (PRE + MID + u)

        def bank(p, u):
            return (p * U + u) % 2 if band else 0

        def pt_of(p, u):
            return y if band and u == 0 else pt[bank(p, u)]

        def tiles(eng, body):
            for j in range(4):
                body(j, j, 0)
            with eng.Fori(1, NT // 4) as b:
                for j in range(4):
                    body(b * 4 + j, j, b)

        with nc.Block() as block:
            @block.sync
            def _(sp):
                if band:
                    sp.dma_start(bias[:], bass.AP(v["ext"].tensor, P - 1, [[767, P], [P * 768, HA], [1, BAND]])
                                 ).then_inc(S["ld_b"], 16)
                else:
                    sp.dma_start(fg[:], bass.AP(v["final_g"].tensor, 0, [[0, P], [1, D]])).then_inc(S["ldf"], 16)

                def cols(g, n, t):
                    return proj[g:g + n, :, bass.ds(t * P, P)].rearrange("g p n -> p g n")

                def body(t, j, b):
                    first = isinstance(b, int)
                    p = j % 2
                    if band:
                        wait(sp, S["sc"], (t - 1) * U)
                        sp.dma_start(xq[p][:], cols(GX, 2, t)).then_inc(s_ld[p], 16)
                        sp.dma_start(q[p][:], cols(GQ, MG, t)).then_inc(s_ld[p], 16)
                    else:
                        wait(sp, S["pv"], t - 1)
                        for buf, src in ((q, cols(GQ, MG, t)), (t1, cols(GK, MG, t)),
                                         (k1, v["kgate"][:, :, bass.ds(t * P, P)].rearrange("g p n -> p g n"))):
                            sp.dma_start(buf[p][:].rearrange("p (g n) -> p g n", n=P), src).then_inc(s_ld[p], 16)
                        sp.dma_start(xq[p][:], cols(GX, 2, t)).then_inc(s_ld[p], 16)
                    if not (isinstance(t, int) and t == 0):
                        sp.wait_ge(S["tp"], d_pre(t - 1) + 1)
                    sp.dma_start(tT[:], cols(GV, MG, t)).then_inc(s_ld[p], 16)
                    if band:
                        if not first:
                            moved, scored = counted(sp, t - 3), counted(sp, t * U)
                            sp.wait_ge(S["kc"], moved)
                            if j == 0:
                                sp.wait_ge(S["sc"], scored)
                        sp.dma_start(kcur[:, :, j * P:(j + 1) * P], cols(GK, MG, t)).then_inc(s_ldk[p], 16)
                    load_x(t, p)
                    if not (isinstance(t, int) and t == 0):
                        sp.wait_ge(S["evd"], d_y(t) + 1)
                    sp.dma_start(gt[:], cols(GG, KD, t)).then_inc(S["ldg"], 16)

                def load_x(t, p):
                    if not (isinstance(t, int) and t < 2):
                        sp.wait_ge(s_stx[p], (t - p) * 8)
                    sp.dma_start(xt[p][:], v["x_of"](t)).then_inc(s_ldx[p], 16)
                tiles(sp, body)
                load_x(NT, 0)
                sp.wait_ge(S["evd"], d_y(NT) + 1)
                sp.dma_start(gt[:], cols(GG, KD, NT)).then_inc(S["ldg"], 16)

            def out_of(t):
                if band:
                    return v["x_mid"][t]
                if isinstance(t, int) and t == NT:
                    return v["y_sample"].rearrange("b s d -> (b s) d")
                return v["y_prompt"].rearrange("b (t p) d -> (b t) p d", p=P)[t]

            def level_masks(pool):
                link = Chain(pool, S["init"])
                link(nc.gpsimd.memset(masks[:], 1.0))
                link(nc.gpsimd.affine_select(out=masks[:, 0], in_=masks[:, 0], compare_op=ALU.is_equal, fill=0.0,
                                             base=0, pattern=[[-1, P]], channel_multiplier=1))
                for i in range(1, LEVELS):
                    m = 1 << (i - 1)
                    nb = P // (2 * m)
                    whole = masks[:, i]
                    view = whole.rearrange("p (b two m) -> p b two m", two=2, m=m)
                    link(nc.gpsimd.memset(view[:, :, 0, :], 0.0))
                    sel = view[:, :, 1, :]
                    link(nc.gpsimd.affine_select(out=sel, in_=sel, compare_op=ALU.is_ge, fill=0.0, base=0,
                                                 pattern=[[-2 * m, nb], [0, m]], channel_multiplier=1))
                    link(nc.gpsimd.affine_select(out=sel, in_=sel, compare_op=ALU.is_ge, fill=0.0, base=m - 1,
                                                 pattern=[[2 * m, nb], [0, m]], channel_multiplier=-1))
                link(nc.gpsimd.memset(am[0][:], 0.0))
                link(nc.gpsimd.memset(am[1][:], 0.0))
                link(nc.gpsimd.memset(st[:], 0.0))

            @block.gpsimd
            def _(pool):
                if band:
                    pool.wait_ge(S["ld_b"], 16)
                    nc.gpsimd.memset(bias[64:P, :, 0:CHUNK], BIG)
                    nc.gpsimd.memset(bias[0:64, :, BAND - CHUNK:], BIG).then_inc(S["bias"], 1)
                else:
                    level_masks(pool)

                def body(t, j, b):
                    first = isinstance(b, int)
                    p = j % 2
                    if not band:
                        powers(pool, t, p)
                    pool.wait_ge(S["xadd" if band else "out"], t + 1)
                    pool.dma_start(out_of(t), xt[p][:]).then_inc(s_stx[p], 16)

                def powers(pool, t, p, hgrn=True):
                    if hgrn:
                        pool.wait_ge(S["oms"], t + 1)
                        wait(pool, S["o"], t)
                        nc.gpsimd.tensor_tensor(rs6[:, 0:MG], ms6[:, 0:MG], neg_half[:, 0:MG], ALU.pow).then_inc(S["ors"], 1)
                    pool.wait_ge(S["fms"], t + 1)
                    nc.gpsimd.tensor_tensor(fr[:, 0:1], fm[:, 0:1], neg_half[:, 0:1], ALU.pow).then_inc(S["frs"], 1)
                tiles(pool, body)
                if not band:
                    powers(pool, NT, 0, hgrn=False)
                pool.wait_ge(S["xadd" if band else "out"], NT + 1)
                pool.dma_start(out_of(NT), xt[0][:]).then_inc(s_stx[0], 16)
                if not band:
                    pool.wait_ge(S["s"], NT)
                    pool.dma_start(v["b_state_prompt"][0, 0].rearrange("h k v -> k h v"),
                                   st[:].rearrange("k (h v) -> k h v", v=P)).then_inc(s_stx[1], 16)
                pool.wait_ge(s_stx[0], 16 * (NT // 2 + 1))
                pool.wait_ge(s_stx[1], 16 * (NT // 2 + (0 if band else 1)))

            N_INIT = 2 + 3 * (LEVELS - 1) + 3

            def q_of(m, p):
                return q[p] if m == 0 else qm[m]

            def k_of(m, p):
                return k1[p] if m <= 1 else km[m]

            def t_of(m, p):
                return t1[p] if m == 1 else tm[m]

            @block.tensor
            def _(pe):
                def turn_outputs(t, src, sample=False):
                    if not sample:
                        pe.wait_ge(S["o"], t)
                    pe.wait_ge(S["evd"], d_y(t) if not sample else d_y(t) + 1)
                    pe.wait_ge(S["eva"], a_y(t))
                    for k in range(KD):
                        ins = nc.tensor.transpose(TP[:, k * P:(k + 1) * P], src[:, k * P:(k + 1) * P], ident[:])
                    ins.then_inc(S["tp"], 1)

                def project_half(n, c):
                    pe.wait_ge(S["yh"], n * 2 + (c - 1))
                    for low in (False, True):
                        if low:
                            pe.wait_ge(S["yl"], n * 2 + (c - 1))
                        for half in range(2):
                            cols = slice(half * 512, half * 512 + 512)
                            for k in range(4 * c, 4 * c + 4):
                                for a, w in ([(yl, woh)] if low else [(yh, woh), (yh, wol)]):
                                    ins = nc.tensor.matmul(OB[:, cols], a[:, k], w[:, k, cols],
                                                           start=(k == 0 and a is yh and w is woh), stop=(k == KD - 1 and low))
                    if c:
                        ins.then_inc(S["op"], 1)

                def body(t, j, b):
                    first = isinstance(b, int)
                    p = j % 2
                    us = units(j, first, p)
                    has_prev = not (isinstance(t, int) and t == 0)

                    def scores(u):
                        if band:
                            wait(pe, S["exp"], t * U + (u - 1))
                        else:
                            pe.wait_ge(S["cp"], t * 16 + 14)
                        unit_scores(nc, us[u], SC[bank(p, u)]).then_inc(S["sc"], 1)

                    def values(u):
                        pe.wait_ge(S["eva"], a_unit(t, u) + 1)
                        pe.wait_ge(S["evd"], d_unit(t, u) + 1)
                        if u == 0 and has_prev:
                            pe.wait_ge(S["xadd"], t)
                        ins = unit_pv(nc, us[u], pt_of(p, u), OB)
                        if u == U - 1:
                            ins.then_inc(S["pv"], 1)

                    def turn(srcs, n_d, n_a):
                        wait(pe, S["evd"], n_d)
                        wait(pe, S["eva"], n_a)
                        for g in range(MG):
                            at = (g % 3) * P + 512 * (g // 3)
                            ins = nc.tensor.transpose(TP[:, at:at + P], srcs(g), ident[:])
                        ins.then_inc(S["tp"], 1)

                    pe.wait_ge(s_ld[p], (t - p) * 8 * LOADS + 16 * LOADS)
                    turn(lambda g: tT[:, g], d_pre(t), a_pre(t))
                    if band:
                        scores(0)
                        if has_prev:
                            turn_outputs(t, o)
                        pe.wait_ge(s_ldk[p], (t - p) * 8 + 16)
                        if has_prev:
                            pe.wait_ge(S["kc"], t)
                        scores(1)
                        if has_prev:
                            project_half(t, 0)
                            project_half(t, 1)
                        for u in range(U):
                            pe.wait_ge(S["exp"], t * U + (u + 1))
                            pe.wait_ge(S["eva"], a_unit(t, u))
                            pe.wait_ge(S["evd"], d_unit(t, u))
                            unit_transposes(nc, us[u], se[bank(p, u)], TP, ident).then_inc(S["tp"], 1)
                            if u:
                                values(u - 1)
                            elif has_prev:
                                pe.wait_ge(S["vc"], t)
                            if u + 2 < U:
                                scores(u + 2)
                        values(U - 1)
                        return

                    def level(i):
                        m = 0 if i == 0 else 1 << (i - 1)
                        if i == 0:
                            wait(pe, S["exp"], t)
                        elif i == 1:
                            wait(pe, S["s"], t)
                        else:
                            pe.wait_ge(S["cp"], t * 16 + 2 * (i - 1))
                        if i:
                            pe.wait_ge(S["hst"], t * 8 + i)
                        if i > 1:
                            pe.wait_ge(S["hcp"], t * 7 + (i - 1))
                        for h in range(MG):
                            at = (h % 3) * P + 512 * (h // 3)
                            hs = slice(h * P, (h + 1) * P)
                            ins = nc.tensor.matmul(SC[i % 2][:, at:at + P], k_of(m, p)[:, hs], q_of(m, p)[:, hs],
                                                   start=True, stop=True)
                            if h % 3 == 2:
                                ins.then_inc(S["lv"], 1)
                    level(0)
                    level(1)
                    level(2)
                    if has_prev:
                        turn_outputs(t, o)
                    level(3)
                    if has_prev:
                        project_half(t, 0)
                    level(4)
                    level(5)
                    if has_prev:
                        project_half(t, 1)
                    level(6)
                    level(7)
                    scores(0)
                    pe.wait_ge(S["hst"], t * 8 + 8)
                    pe.wait_ge(S["hcp"], t * 7 + 7)
                    turn(lambda g: km[128][:, g * P:(g + 1) * P], d_mid(t), t * PER_A + PRE)
                    pe.wait_ge(S["cp"], t * 16 + 16)
                    if has_prev:
                        pe.wait_ge(S["xadd"], t)
                        pe.wait_ge(S["s"], t)
                    for h in range(MG):
                        hs = slice(h * P, (h + 1) * P)
                        nc.tensor.matmul(OB[:, hs], am[p][:, hs], inat[:, hs], start=True, stop=False)
                        ins = nc.tensor.matmul(OB[:, hs], qm[128][:, hs], st[:, hs], start=False, stop=True)
                    ins.then_inc(S["hv"], 1)
                    pe.wait_ge(S["evd"], d_mid(t) + 1)
                    pe.wait_ge(S["eva"], t * PER_A + (PRE + 1))
                    for h in range(MG):
                        at = (h % 3) * P + 512 * (h // 3)
                        hs = slice(h * P, (h + 1) * P)
                        ins = nc.tensor.matmul(SC[1][:, at:at + P], knat[:, hs], inat[:, hs], start=True, stop=True)
                    ins.then_inc(S["kv"], 1)
                    pe.wait_ge(S["exp"], t + 1)
                    unit_transposes(nc, us[0], se[0], TP, ident).then_inc(S["tp"], 1)
                    values(0)

                if band:
                    pe.wait_ge(S["bias"], 1)
                else:
                    pe.wait_ge(S["init"], N_INIT)
                tiles(pe, body)
                turn_outputs(NT, o)
                project_half(NT, 0)
                project_half(NT, 1)
                turn_outputs(NT, o_s, sample=True)
                pe.wait_ge(S["xadd"], NT)
                project_half(NT + 1, 0)
                project_half(NT + 1, 1)

            @block.vector
            def _(dve):
                def outputs(t):
                    dve.wait_ge(S["pv"], t)
                    n = HA + HX if band else HX
                    nc.vector.reciprocal(rs[:, 0:n], tot[:, 0:n]).then_inc(S["rs"], 1)
                    dve.wait_ge(S["rs"], t)
                    for at, heads in ((0, 8), (8, 8)) if band else ((HA, HX),):
                        cs = slice(at * HD, (at + heads) * HD)
                        of = at if band else 0
                        ins = nc.vector.tensor_tensor(o[:, cs].rearrange("p (h d) -> p h d", d=HD),
                                                      OB[:, cs].rearrange("p (h d) -> p h d", d=HD),
                                                      rs[:, of:of + heads].unsqueeze(2).to_broadcast([P, heads, HD]), ALU.mult)
                    ins.then_inc(S["o"], 1)

                def outputs_copy(t):
                    dve.wait_ge(S["hv"], t + 1)
                    nc.vector.tensor_copy(o[:, 512:MIX], OB[:, 512:MIX]).then_inc(S["ocp"], 1)

                def outputs_mean(t):
                    dve.wait_ge(S["osq"], t + 1)
                    nc.vector.tensor_reduce(ssq[:, 0:MG], y[:, 0:MIX].rearrange("p (h d) -> p h d", d=P), AX_X, ALU.add
                                            ).then_inc(S["hq"], 1)
                    dve.wait_ge(S["hq"], t + 1)
                    nc.vector.tensor_scalar(ms6[:, 0:MG], ssq[:, 0:MG], 1.0 / P, EPS, ALU.mult, ALU.add).then_inc(S["oms"], 1)

                def outputs_norm(t):
                    dve.wait_ge(S["ors"], t + 1)
                    for c in range(2):
                        hs, cs = slice(c * 4, 4 + c * 2), slice(c * 512, 512 + c * 256)
                        nc.vector.tensor_tensor(o[:, cs].rearrange("p (h d) -> p h d", d=P),
                                                (o if c else OB)[:, cs].rearrange("p (h d) -> p h d", d=P),
                                                rs6[:, hs].unsqueeze(2).to_broadcast([P, 4 - 2 * c, P]), ALU.mult)

                def gate(t, sample=False):
                    n = t + 1 if sample else t
                    dve.wait_ge(S["tp"], d_y(t) + (2 if sample else 1))
                    dve.wait_ge(S["ldg"], n * 16)
                    for c in range(2):
                        cs = slice(c * 512, (c + 1) * 512)
                        nc.vector.tensor_tensor(y[:, cs], TP[:, cs], gt[:, 4 * c:4 * c + 4].rearrange("p k n -> p (k n)"),
                                                ALU.mult).then_inc(S["evd" if c else "yg"], 1)

                def low_parts(n):
                    for c in range(2):
                        cs = slice(c * 512, (c + 1) * 512)
                        dve.wait_ge(S["yh"], n * 2 + (c - 1))
                        nc.vector.tensor_tensor(yl[:, 4 * c:4 * c + 4].rearrange("p k n -> p (k n)"), y[:, cs],
                                                yh[:, 4 * c:4 * c + 4].bitcast(F32).rearrange("p k n -> p (k n)"),
                                                ALU.subtract).then_inc(S["yl"], 1)

                def add(n, p):
                    dve.wait_ge(S["op"], n)
                    dve.wait_ge(s_ldx[p], (n - 1 - p) * 8 + 16)
                    for c in range(2):
                        ins = nc.vector.tensor_tensor(xt[p][:, c * 512:(c + 1) * 512], xt[p][:, c * 512:(c + 1) * 512],
                                                      OB[:, c * 512:(c + 1) * 512], ALU.add)
                    ins.then_inc(S["xadd"], 1)

                def final_mean(n):
                    dve.wait_ge(S["fsq"], n)
                    wait(dve, S["frs"], n - 1)
                    nc.vector.tensor_scalar(fm[:, 0:1], fs[:, 0:1], 1.0 / D, EPS, ALU.mult, ALU.add).then_inc(S["fms"], 1)

                def final_scale(n, p):
                    dve.wait_ge(S["frs"], n)
                    nc.vector.scalar_tensor_tensor(out=xt[p][:], in0=xt[p][:], scalar=fr[:, 0:1], in1=fg[:],
                                                   op0=ALU.mult, op1=ALU.mult).then_inc(S["out"], 1)

                def body(t, j, b):
                    first = isinstance(b, int)
                    p = j % 2
                    us = units(j, first, p)
                    has_prev = not (isinstance(t, int) and t == 0)

                    def low_min(u):
                        scored = counted(dve, t * U + (u + 1))
                        if band:
                            dve.wait_ge(S["bias"], 1)
                        dve.wait_ge(S["sc"], scored)
                        unit_min(nc, us[u], SC[bank(p, u)], se[bank(p, u)], mn[:, us[u].at]).then_inc(S["min"], 1)
                    if has_prev:
                        outputs(t)
                    if band and has_prev:
                        i = (j - 1) % 4
                        nc.vector.tensor_copy(vprev[:, i], vcur[:, i]).then_inc(S["vc"], 1)
                        wait(dve, S["vc"], t - 1)
                    dve.wait_ge(S["tp"], d_pre(t) + 1)
                    dst = vcur[:, j] if band else inat[:]
                    nc.vector.tensor_copy(dst[:, 384:MIX], TP[:, 512:896]).then_inc(S["evd"], 1)
                    if band:
                        low_min(0)
                        if has_prev:
                            gate(t)
                            low_parts(t)
                        low_min(1)
                        if has_prev:
                            add(t, 1 - p)
                        for u in range(U):
                            dve.wait_ge(S["tp"], d_unit(t, u) + 1)
                            unit_evac_high(us[u], nc.vector.tensor_copy, pt_of(p, u), TP).then_inc(S["evd"], 1)
                            if u + 2 < U:
                                low_min(u + 2)
                    else:
                        dve.wait_ge(s_ld[p], (t - p) * 8 * LOADS + 16 * LOADS)

                        def step(i):
                            if i == 0:
                                nc.vector.tensor_tensor(qm[1][:], q[p][:], t1[p][:], ALU.mult).then_inc(S["hst"], 1)
                                return
                            m = 1 << (i - 1)
                            dve.wait_ge(S["hst"], t * 8 + i)
                            wait(dve, S["hcp"], t * 7 + (i - 1))
                            n = MIX // (2 * m)

                            def two(a, width=m):
                                return a[:].rearrange("p (n two m) -> p n two m", two=2, m=width)
                            tot_m = two(t_of(m, p), 1)
                            nc.vector.tensor_tensor(two(qm[2 * m])[:, :, 1], two(q_of(m, p))[:, :, 1],
                                                    tot_m[:, :, 0].to_broadcast([P, n, m]), ALU.mult)
                            nc.vector.tensor_tensor(two(km[2 * m])[:, :, 0], two(k_of(m, p))[:, :, 0],
                                                    tot_m[:, :, 1].to_broadcast([P, n, m]), ALU.mult)
                            nc.vector.tensor_tensor(tm[2 * m][:].unsqueeze(2), tot_m[:, :, 0], tot_m[:, :, 1], ALU.mult
                                                    ).then_inc(S["hst"], 1)

                        def place(i):
                            for c in range(2):
                                made = counted(dve, t * 16 + (2 * i + c + 1))
                                placed = counted(dve, t * 16 + (2 * i + c - 1))
                                dve.wait_ge(S["init"], N_INIT)
                                dve.wait_ge(S["lv"], made)
                                if i:
                                    dve.wait_ge(S["cp"], placed)
                                hs = slice(c * 384, c * 384 + 384)
                                nc.vector.copy_predicated(am[p][:, hs].rearrange("p (h n) -> p h n", n=P),
                                                          masks[:, i:i + 1].bitcast(U32).to_broadcast([P, 3, P]),
                                                          SC[i % 2][:, 512 * c:512 * c + 384].rearrange("p (h n) -> p h n", n=P)
                                                          ).then_inc(S["cp"], 1)
                        step(0)
                        step(1)
                        place(0)
                        step(2)
                        place(1)
                        if has_prev:
                            gate(t)
                        step(3)
                        place(2)
                        if has_prev:
                            low_parts(t)
                        for i in range(4, LEVELS):
                            step(i)
                            place(i - 1)
                        if has_prev:
                            add(t, 1 - p)
                        place(LEVELS - 1)
                        if has_prev:
                            final_mean(t)
                        dve.wait_ge(S["tp"], d_mid(t) + 1)
                        nc.vector.tensor_copy(knat[:, 384:MIX], TP[:, 512:896]).then_inc(S["evd"], 1)
                        low_min(0)
                        outputs_copy(t)
                        if has_prev:
                            final_scale(t, 1 - p)
                        outputs_mean(t)
                        dve.wait_ge(S["kv"], t + 1)
                        for h in range(MG):
                            at = (h % 3) * P + 512 * (h // 3)
                            hs = slice(h * P, (h + 1) * P)
                            ins = nc.vector.scalar_tensor_tensor(out=st[:, hs], in0=st[:, hs], scalar=tm[128][:, h:h + 1],
                                                                 in1=SC[1][:, at:at + P], op0=ALU.mult, op1=ALU.add)
                        ins.then_inc(S["s"], 1)
                        dve.wait_ge(S["tp"], d_unit(t, 0) + 1)
                        unit_evac_high(us[0], nc.vector.tensor_copy, pt[0], TP).then_inc(S["evd"], 1)
                        outputs_norm(t)
                if not band:
                    dve.wait_ge(S["ldf"], 16)
                tiles(dve, body)
                outputs(NT)
                gate(NT)
                low_parts(NT)
                add(NT, 1)
                if not band:
                    final_mean(NT)
                    final_scale(NT, 1)
                gate(NT, sample=True)
                low_parts(NT + 1)
                add(NT + 1, 0)
                if not band:
                    final_mean(NT + 1)
                    final_scale(NT + 1, 0)

            @block.scalar
            def _(act):
                def y_high(n, sample=False):
                    act.wait_ge(S["yg"], n)
                    for c in range(2):
                        if c:
                            act.wait_ge(S["evd"], d_y(NT) + 2 if sample else d_y(n) + 1)
                        nc.scalar.copy(yh[:, 4 * c:4 * c + 4].rearrange("p k n -> p (k n)"), y[:, c * 512:(c + 1) * 512]
                                       ).then_inc(S["yh"], 1)

                def final_square(n, p):
                    act.wait_ge(S["xadd"], n)
                    wait(act, S["fms"], n - 1)
                    nc.scalar.activation(y[:], xt[p][:], ACT.Square, accum_out=fs[:, 0:1]).then_inc(S["fsq"], 1)

                def out_square(t):
                    act.wait_ge(S["hv"], t + 1)
                    wait(act, S["fsq"], t)
                    for c in range(2):
                        cs = slice(c * 512, 512 + c * 256)
                        if c:
                            act.wait_ge(S["ocp"], t + 1)
                        ins = nc.scalar.activation(y[:, cs], (o if c else OB)[:, cs], ACT.Square)
                    ins.then_inc(S["osq"], 1)

                def body(t, j, b):
                    first = isinstance(b, int)
                    p = j % 2
                    us = units(j, first, p)
                    has_prev = not (isinstance(t, int) and t == 0)

                    def exp(u):
                        act.wait_ge(S["min"], t * U + (u + 1))
                        unit_exp(nc, us[u], SC[bank(p, u)], se[bank(p, u)], mn[:, us[u].at], tot[:, us[u].at]
                                 ).then_inc(S["exp"], 1)
                    act.wait_ge(S["tp"], d_pre(t) + 1)
                    if band:
                        wait(act, S["vc"], t - 1)
                    dst = vcur[:, j] if band else inat[:]
                    nc.scalar.copy(dst[:, 0:384], TP[:, 0:384]).then_inc(S["eva"], 1)
                    if band:
                        if has_prev:
                            i = (j - 1) % 4
                            nc.scalar.copy(kprev[:, :, i * P:(i + 1) * P], kcur[:, :, i * P:(i + 1) * P]).then_inc(S["kc"], 1)
                            y_high(t)
                        exp(0)
                        exp(1)
                        for u in range(U):
                            act.wait_ge(S["tp"], d_unit(t, u) + 1)
                            unit_evac_low(us[u], nc.scalar.copy, pt_of(p, u), TP).then_inc(S["eva"], 1)
                            if u + 2 < U:
                                exp(u + 2)
                    else:
                        act.wait_ge(s_ld[p], (t - p) * 8 * LOADS + 16 * LOADS)

                        def carry(i):
                            m = 1 << (i - 1)
                            act.wait_ge(S["hst"], t * 8 + i)
                            wait(act, S["hcp"], t * 7 + (i - 1))

                            def two(a):
                                return a[:].rearrange("p (n two m) -> p n two m", two=2, m=m)
                            nc.scalar.copy(two(qm[2 * m])[:, :, 0], two(q_of(m, p))[:, :, 0])
                            nc.scalar.copy(two(km[2 * m])[:, :, 1], two(k_of(m, p))[:, :, 1]).then_inc(S["hcp"], 1)
                        carry(1)
                        carry(2)
                        if has_prev:
                            y_high(t)
                        for i in range(3, LEVELS):
                            carry(i)
                        if has_prev:
                            final_square(t, 1 - p)
                        act.wait_ge(S["tp"], d_mid(t) + 1)
                        nc.scalar.copy(knat[:, 0:384], TP[:, 0:384]).then_inc(S["eva"], 1)
                        exp(0)
                        out_square(t)
                        act.wait_ge(S["tp"], d_unit(t, 0) + 1)
                        unit_evac_low(us[0], nc.scalar.copy, pt[0], TP).then_inc(S["eva"], 1)
                tiles(act, body)
                y_high(NT)
                if not band:
                    final_square(NT, 1)
                y_high(NT + 1, sample=True)
                if not band:
                    final_square(NT + 1, 0)


_INS = ['x_prompt', 'x_sample', 'cache_a_k', 'cache_a_v', 'state_b', 'cache_mem_k', 'cache_mem_v', 'mem_prompt',
        'ln_g', 'w_in', 'w_out', 'rel_bias_table', 'lower_bounds', 'hgrn_norm_g', 'mem_norm_g', 'w_mem_kv', 'final_g']
_OUTS = [(1, 2048, 1024), (8, 16, 1024), (1, 1, 512, 12, 64), (1, 1, 512, 12, 64), (1, 1, 6, 128, 128),
         (2, 1, 256, 4, 64), (2, 1, 256, 4, 64), (1, 8, 16, 12, 64), (1, 8, 16, 12, 64), (1, 8, 6, 128, 128)]


def kernel(**inputs):
    import numpy as _np
    import concourse.bacc as _bacc
    from concourse import mybir as _mybir
    from concourse.bass_utils import run_bass_kernel_spmd as _run

    nc = _bacc.Bacc("TRN2", target_bir_lowering=False, num_devices=1)
    arrays, args = {}, []
    for name in _INS:
        a = _np.ascontiguousarray(inputs[name])
        arrays[f"in_{name}_dram"] = a
        args.append(nc.dram_tensor(f"in_{name}_dram", a.shape, _mybir.dt.from_np(a.dtype), kind="ExternalInput").ap())
    for i, shape in enumerate(_OUTS):
        args.append(nc.dram_tensor(f"out_{i}_dram", shape, F32, kind="ExternalOutput").ap())
    hybrid_encoder(nc, *args)
    r = _run(nc, [arrays], core_ids=[0])
    return tuple(r.results[0][f"out_{i}_dram"] for i in range(len(_OUTS)))
```

```python
from contextlib import ExitStack

import concourse.bass as bass
from concourse import mybir

F32 = mybir.dt.float32
F32R = mybir.dt.float32r
U32 = mybir.dt.uint32
ALU = mybir.AluOpType
ACT = mybir.ActivationFunctionType
AX_X = mybir.AxisListType.X

P = 128
D = 1024
KD = D // P
SEQ = 2048
NT = SEQ // P
TS = NT
NTOK = SEQ + P
SB, SL = 8, 16
MIX = 768
MG = MIX // P
HA, HD = 12, 64
HX = 4
NMEM = 256
XW = HX * HD
NG = (3 * MIX + XW + D) // P
CHUNK = 64
BAND = 640
CLIP = 128
EPS = 1e-6
DEPTH = 2
BIG = 1e30
GQ, GK, GV, GX, GG = 0, MG, 2 * MG, 3 * MG, 3 * MG + 2
BLOCKS = [(0, 512), (512, 512), (1024, 384), (1408, 384), (1792, 384)]
NBLK = len(BLOCKS)


def wait(eng, sem, value):
    if not (isinstance(value, int) and value <= 0):
        eng.wait_ge(sem, value)


def counted(eng, value):
    return value if isinstance(value, int) else eng.to_reg(value)


def sweep(eng, first, last, per, body):
    n = (last - first) // per
    for r in range(min(per, last - first)):
        body(first + r, r)
    if n > 1:
        with eng.Fori(1, n) as i:
            for r in range(per):
                body(i * per + (first + r), r)
    for r in range(n * per if n else last - first, last - first):
        body(first + r, r % per)


class Semaphores:

    def __init__(self, nc, software):
        self.nc, self.held, self.ctx, self._software = nc, [], ExitStack(), software

    def __enter__(self):
        return self

    def __call__(self, name):
        self.held.append(self.ctx.enter_context(self.nc.semaphore(name)))
        return self.held[-1]

    def software(self, name):
        return self._software.enter_context(self.nc.semaphore(name))

    def __exit__(self, *error):
        if error[0] is None:
            with self.nc.Block() as block:
                @block.gpsimd
                def _(pool):
                    for s in self.held:
                        pool.sem_clear(s)
        self.ctx.close()


class Ahead:

    def __init__(self, sem, name):
        self.sem, self.loads = sem(name), []

    def issue(self, sp):
        for out, src in self.loads:
            sp.dma_start(out, src).then_inc(self.sem, 16)

    def wait(self, eng):
        eng.wait_ge(self.sem, 16 * len(self.loads))


class Chain:

    def __init__(self, eng, sem):
        self.eng, self.sem, self.n = eng, sem, 0

    def __call__(self, ins):
        self.n += 1
        ins.then_inc(self.sem, 1)
        self.eng.wait_ge(self.sem, self.n)


def hybrid_encoder(nc, x_prompt, x_sample, cache_a_k, cache_a_v, state_b, cache_mem_k, cache_mem_v, mem_prompt,
                   ln_g, w_in, w_out, rel_bias_table, lower_bounds, hgrn_norm_g, mem_norm_g, w_mem_kv, final_g,
                   y_prompt, y_sample, a_k_prompt, a_v_prompt, b_state_prompt, mem_k_prompt, mem_v_prompt,
                   a_k_sample, a_v_sample, b_state_sample):
    top = ExitStack()
    with top, nc.allow_non_contiguous_dma(reason="channel vectors onto partitions, and the small bias table"):
        def dram(name, shape):
            return nc.dram_tensor(name, shape, F32, kind="Internal").ap()

        def sb_in(ctx):
            return lambda name, shape, dt=F32: ctx.enter_context(nc.sbuf_tensor(name, shape, dt))

        def sb_far_in(ctx):
            return lambda name, shape, dt=F32: ctx.enter_context(nc.sbuf_tensor(name, shape, dt, side="right"))

        def ps_in(ctx):
            return lambda name, shape, dt=F32: ctx.enter_context(nc.psum_tensor(name, shape, dt))

        software = top.enter_context(ExitStack())
        sb = sb_in(top)
        proj = dram("proj", (NG, P, NTOK))
        kgate = dram("kgate", (MG, P, NTOK))
        x_mid = dram("x_mid", (NT + 1, P, D))
        ext = dram("ext", (HA, P, 768))

        ident = sb("ident", [P, P])
        g_ln = sb("g_ln", [P, 2, KD])
        g_mem = sb("g_mem", [P, 2, KD])
        g_hgrn = sb("g_hgrn", [P, MG])
        lb = sb("lb", [P, MG])
        lb1 = sb("lb1", [P, MG])
        neg_half = sb("neg_half", [P, 16])
        seqmask = sb("seqmask", [P, SB])
        mem_kT = sb("mem_kT", [P, 2, 2, NMEM])
        mem_v = sb("mem_v", [P, 2, 2, XW])

        xp_t = x_prompt.rearrange("b (t p) d -> (b t) p d", p=P)
        xs_t = x_sample.rearrange("b s d -> (b s) d")

        with Semaphores(nc, software) as sem:
            setup(nc, sem, sb_in, ps_in, locals())
        for l in range(DEPTH):
            def x_of(t):
                if l:
                    return x_mid[t]
                return xs_t if isinstance(t, int) and t == TS else xp_t[t]
            with ExitStack() as ctx:
                xh = sb_in(ctx)(f"xh{l}", [P, KD, NTOK], F32R)
                xl = sb_in(ctx)(f"xl{l}", [P, KD, NTOK], F32R)
                with Semaphores(nc, software) as sem:
                    first = Ahead(sem, f"pj{l}_first")
                    first.buf = sb_in(ctx)(f"pj{l}_wraw", [P, KD, 2 * P])
                    w_pairs = w_in[l].rearrange("(k p) (c n) -> c p k n", p=P, n=2 * P)
                    first.loads = [(first.buf[:], w_pairs[0])]
                    norm_transpose(nc, l, sem, sb_in, ps_in, x_of, ident, neg_half, xh, xl, first)
                    project(nc, l, sem, sb_in, ps_in, xh, xl, w_pairs, first, g_ln, lb, lb1, proj, kgate)
            mix(nc, l, software, sb_in, ps_in, locals())


def setup(nc, sem, sb_in, ps_in, v):
    ident, g_ln, g_mem, g_hgrn, lb, lb1 = (v[n] for n in ("ident", "g_ln", "g_mem", "g_hgrn", "lb", "lb1"))
    neg_half, seqmask, mem_kT, mem_v, ext = (v[n] for n in ("neg_half", "seqmask", "mem_kT", "mem_v", "ext"))
    mem_k_prompt, mem_v_prompt = v["mem_k_prompt"], v["mem_v_prompt"]
    s_cols, s_tab, s_mem, s_ext, s_out = (sem(f"su_{n}") for n in ("cols", "tab", "mem", "ext", "out"))
    s_wkv = [sem(f"su_wkv{i}") for i in range(2)]
    s_gm = sem("su_gm")
    c_pool, c_dve, s_const, s_extv = (sem(f"su_{n}") for n in ("cpool", "cdve", "const", "extv"))
    s_sq, s_ms, s_rs, s_xn, s_tp, s_ev, s_wg, s_kv, s_kvev, s_kt, s_ktev, s_lbx, s_lbe = (
        sem(f"su_{n}") for n in ("sq", "ms", "rs", "xn", "tp", "ev", "wg", "kv", "kvev", "kt", "ktev", "lbx", "lbe"))
    with ExitStack() as ctx:
        sb, ps = sb_in(ctx), ps_in(ctx)
        tab = sb("tab", [HA, 2 * CLIP + 1])
        extv = sb("extv", [HA, 768])
        xm = sb("xm", [P, 2, D])
        sq = sb("sq", [P, D])
        ss = sb("ss", [P, 2])
        ms = sb("ms", [P, 2])
        rs = sb("rs", [P, 2])
        xn = sb("xn", [P, 2, D])
        xT = sb("xT", [P, KD, NMEM])
        wkv = sb("wkv", [P, 2, KD, 2 * XW])
        kv = sb("kv", [P, 4, 2 * XW])
        lbraw = sb("lbraw", [P, MG])
        lbd = sb("lbd", [P, MG])
        lbe = sb("lbe", [P, MG])
        lbr = sb("lbr", [P, MG])
        TP = [ps(f"suTP{i}", [P, 512]) for i in range(4)]
        KV = [ps(f"suKV{i}", [P, 512]) for i in range(4)]
        with nc.Block() as block:
            @block.sync
            def _(sp):
                sp.dma_start(xm[:], v["mem_prompt"].rearrange("b (t p) d -> p (b t) d", p=P)).then_inc(s_mem, 16)
                for l in range(2):
                    sp.dma_start(wkv[:, l], v["w_mem_kv"][l].rearrange("(k p) n -> p k n", p=P)).then_inc(s_wkv[l], 16)
                sp.wait_ge(s_extv, 1)
                sp.dma_start(ext, extv[:].unsqueeze(1).to_broadcast([HA, P, 768])).then_inc(s_ext, 16)
                for i in range(4):
                    l, t = divmod(i, 2)
                    sp.wait_ge(s_kvev, i + 1)
                    rows = slice(t * P, (t + 1) * P)
                    for out, cols in ((mem_k_prompt, slice(0, XW)), (mem_v_prompt, slice(XW, 2 * XW))):
                        sp.dma_start(out[l, 0, rows].rearrange("p h d -> p (h d)"), kv[:, i, cols]).then_inc(s_out, 16)
                sp.wait_ge(s_out, 128)
                sp.wait_ge(s_ext, 16)

            @block.scalar
            def _(act):
                for l in range(2):
                    act.dma_start(g_mem[:, l], v["mem_norm_g"][l].rearrange("(k p) -> p k", p=P)).then_inc(s_gm, 16)
                act.dma_start(tab[:], v["rel_bias_table"][0]).then_inc(s_tab, 16)
                for l in range(2):
                    act.dma_start(g_ln[:, l], v["ln_g"][l].rearrange("(k p) -> p k", p=P)).then_inc(s_cols, 16)
                act.dma_start(g_hgrn[:], v["hgrn_norm_g"][0].rearrange("(k p) -> p k", p=P)).then_inc(s_cols, 16)
                act.dma_start(lbraw[:], v["lower_bounds"][0].rearrange("(k p) -> p k", p=P)).then_inc(s_cols, 16)
                act.wait_ge(s_mem, 16)
                for t in range(2):
                    nc.scalar.activation(sq[:], xm[:, t], ACT.Square, accum_out=ss[:, t:t + 1]).then_inc(s_sq, 1)
                    if t == 0:
                        act.wait_ge(s_sq, 1)
                for i in range(4):
                    act.wait_ge(s_tp, i + 1)
                    t, half = divmod(i, 2)
                    nc.scalar.copy(xT[:, half * 4:half * 4 + 4, t * P:(t + 1) * P],
                                   TP[i][:].rearrange("p (k n) -> p k n", n=P)).then_inc(s_ev, 1)
                act.wait_ge(s_lbx, 1)
                nc.scalar.activation(lbe[:], lbd[:], ACT.Exp).then_inc(s_lbe, 1)
                for i in range(4):
                    l, t = divmod(i, 2)
                    act.wait_ge(s_kv, i + 1)
                    nc.scalar.copy(kv[:, i], KV[i][:]).then_inc(s_kvev, 1)
                for i in range(4):
                    l, t = divmod(i, 2)
                    act.wait_ge(s_kt, i + 1)
                    nc.scalar.copy(mem_kT[:, l, :, t * P:(t + 1) * P],
                                   TP[i][:, 0:2 * P].rearrange("p (g n) -> p g n", n=P)).then_inc(s_ktev, 1)

            @block.gpsimd
            def _(pool):
                link = Chain(pool, c_pool)
                link(nc.gpsimd.memset(ident[:], 0.0))
                link(nc.gpsimd.affine_select(out=ident[:], in_=ident[:], compare_op=ALU.not_equal, fill=1.0,
                                             base=0, pattern=[[-1, P]], channel_multiplier=1))
                link(nc.gpsimd.memset(seqmask[:], 1.0))
                link(nc.gpsimd.affine_select(out=seqmask[:], in_=seqmask[:], compare_op=ALU.is_ge, fill=0.0,
                                             base=0, pattern=[[-SL, SB]], channel_multiplier=1))
                link(nc.gpsimd.affine_select(out=seqmask[:], in_=seqmask[:], compare_op=ALU.is_ge, fill=0.0,
                                             base=SL - 1, pattern=[[SL, SB]], channel_multiplier=-1))
                nc.gpsimd.memset(neg_half[:], -0.5).then_inc(s_const, 1)
                pool.wait_ge(s_const, 1)
                pool.wait_ge(s_ms, 1)
                nc.gpsimd.tensor_tensor(rs[:], ms[:], neg_half[:, 0:2], ALU.pow).then_inc(s_rs, 1)

            @block.vector
            def _(dve):
                link = Chain(dve, c_dve)
                dve.wait_ge(s_sq, 2)
                nc.vector.tensor_scalar(ms[:], ss[:], 1.0 / D, EPS, ALU.mult, ALU.add).then_inc(s_ms, 1)
                dve.wait_ge(s_rs, 1)
                for t in range(2):
                    nc.vector.tensor_scalar(xn[:, t], xm[:, t], rs[:, t:t + 1], None, ALU.mult).then_inc(s_xn, 1)
                dve.wait_ge(s_gm, 32)
                for l in range(2):
                    dve.wait_ge(s_wkv[l], 16)
                    for half in range(2):
                        ks = slice(4 * half, 4 * half + 4)
                        nc.vector.tensor_tensor(wkv[:, l, ks], wkv[:, l, ks],
                                                g_mem[:, l, ks].unsqueeze(2).to_broadcast([P, 4, 2 * XW]),
                                                ALU.mult).then_inc(s_wg, 1)
                dve.wait_ge(s_tab, 16)
                link(nc.vector.memset(extv[:], 0.0))
                link(nc.vector.tensor_scalar(extv[:, 0:511], extv[:, 0:511], tab[:, 2 * CLIP:2 * CLIP + 1], None, ALU.subtract))
                back = bass.AP(tab[:].tensor, 2 * CLIP, [[2 * CLIP + 1, HA], [-1, 2 * CLIP]])
                nc.vector.tensor_scalar(extv[:, 511:511 + 2 * CLIP], back, -1.0, None, ALU.mult).then_inc(s_extv, 1)
                dve.wait_ge(s_cols, 64)
                nc.vector.tensor_tensor(lbd[:], lbraw[:], lbraw[:], ALU.subtract).then_inc(s_lbx, 1)
                dve.wait_ge(s_lbe, 1)
                link(nc.vector.reciprocal(lbr[:], lbe[:]))
                link(nc.vector.tensor_tensor(lb[:], lbe[:], lbr[:], ALU.mult))
                link(nc.vector.tensor_tensor(lb[:], lb[:], lb[:], ALU.subtract))
                link(nc.vector.tensor_scalar(lb1[:], lb[:], -1.0, 1.0, ALU.mult, ALU.add))
                for i in range(4):
                    l, t = divmod(i, 2)
                    dve.wait_ge(s_kvev, i + 1)
                    nc.vector.tensor_copy(mem_v[:, l, t], kv[:, i, XW:2 * XW]).then_inc(c_dve, 1)

            @block.tensor
            def _(pe):
                pe.wait_ge(c_pool, 2)
                for t in range(2):
                    pe.wait_ge(s_xn, t + 1)
                    for k in range(KD):
                        ins = nc.tensor.transpose(TP[2 * t + k // 4][:, (k % 4) * P:(k % 4 + 1) * P],
                                                  xn[:, t, k * P:(k + 1) * P], ident[:])
                        if k % 4 == 3:
                            ins.then_inc(s_tp, 1)
                pe.wait_ge(s_ev, 4)
                for i in range(4):
                    l, t = divmod(i, 2)
                    for k in range(KD):
                        if t == 0 and k % 4 == 0:
                            pe.wait_ge(s_wg, 2 * l + k // 4 + 1)
                        ins = nc.tensor.matmul(KV[i][:], xT[:, k, t * P:(t + 1) * P], wkv[:, l, k],
                                               start=(k == 0), stop=(k == KD - 1))
                    ins.then_inc(s_kv, 1)
                for i in range(4):
                    pe.wait_ge(s_kvev, i + 1)
                    for g in range(2):
                        ins = nc.tensor.transpose(TP[i][:, g * P:(g + 1) * P], kv[:, i, g * P:(g + 1) * P], ident[:])
                    ins.then_inc(s_kt, 1)


def norm_transpose(nc, l, sem, sb_in, ps_in, x_of, ident, neg_half, xh, xl, ahead):
    s_in = [sem(f"nt{l}_in{i}") for i in range(4)]
    s_sq, s_ms, s_rs, s_xn, s_tp, s_hi, s_lo = (sem(f"nt{l}_{n}") for n in ("sq", "ms", "rs", "xn", "tp", "hi", "lo"))
    with ExitStack() as ctx:
        sb, ps = sb_in(ctx), ps_in(ctx)
        xt = [sb(f"nt{l}_x{i}", [P, D]) for i in range(4)]
        xn = [sb(f"nt{l}_xn{i}", [P, D]) for i in range(2)]
        sq = sb(f"nt{l}_sq", [P, D])
        ss = sb(f"nt{l}_ss", [P, 4])
        ms = sb(f"nt{l}_ms", [P, 4])
        rs = sb(f"nt{l}_rs", [P, 4])
        TP = [[ps(f"nt{l}_tp{i}{h}", [P, 512]) for h in range(2)] for i in range(2)]

        def tiles(eng, body):
            sweep(eng, 0, NT - 4, 4, body)
            for t in range(NT - 4, NT + 1):
                body(t, t % 4)

        def exists(t):
            return not isinstance(t, int) or t <= TS

        with nc.Block() as block:
            @block.sync
            def _(sp):
                def body(t, p):
                    wait(sp, s_xn, t - 3)
                    sp.dma_start(xt[p][:], x_of(t)).then_inc(s_in[p], 16)
                tiles(sp, body)
                ahead.issue(sp)

            @block.scalar
            def _(act):
                def square(t, p):
                    act.wait_ge(s_in[p], (t - p) * 4 + 16)
                    wait(act, s_ms, t - 3)
                    wait(act, s_sq, t)
                    nc.scalar.activation(sq[:], xt[p][:], ACT.Square, accum_out=ss[:, p:p + 1]).then_inc(s_sq, 1)
                square(0, 0)
                square(1, 1)

                def body(t, p):
                    if exists(t + 2):
                        square(t + 2, (p + 2) % 4)
                    for h in range(2):
                        act.wait_ge(s_tp, t * 2 + (h + 1))
                        nc.scalar.copy(xh[:, 4 * h:4 * h + 4, bass.ds(t * P, P)],
                                       TP[p % 2][h][:].rearrange("p (k n) -> p k n", n=P)).then_inc(s_hi, 1)
                tiles(act, body)

            @block.gpsimd
            def _(pool):
                def body(t, p):
                    pool.wait_ge(s_ms, t + 1)
                    wait(pool, s_xn, t - 3)
                    nc.gpsimd.tensor_tensor(rs[:, p:p + 1], ms[:, p:p + 1], neg_half[:, 0:1], ALU.pow).then_inc(s_rs, 1)
                tiles(pool, body)

            @block.vector
            def _(dve):
                def mean(t, p):
                    dve.wait_ge(s_sq, t + 1)
                    wait(dve, s_rs, t - 3)
                    nc.vector.tensor_scalar(ms[:, p:p + 1], ss[:, p:p + 1], 1.0 / D, EPS, ALU.mult, ALU.add).then_inc(s_ms, 1)

                def scale(t, p):
                    dve.wait_ge(s_rs, t + 1)
                    wait(dve, s_tp, t * 2 - 2)
                    nc.vector.tensor_scalar(xn[p % 2][:], xt[p][:], rs[:, p:p + 1], None, ALU.mult).then_inc(s_xn, 1)
                mean(0, 0)
                mean(1, 1)
                scale(0, 0)

                def body(t, p):
                    if exists(t + 2):
                        mean(t + 2, (p + 2) % 4)
                    if exists(t + 1):
                        scale(t + 1, (p + 1) % 4)
                    for h in range(2):
                        dve.wait_ge(s_hi, t * 2 + (h + 1))
                        nc.vector.tensor_tensor(xl[:, 4 * h:4 * h + 4, bass.ds(t * P, P)],
                                                TP[p % 2][h][:].rearrange("p (k n) -> p k n", n=P),
                                                xh[:, 4 * h:4 * h + 4, bass.ds(t * P, P)].bitcast(F32),
                                                ALU.subtract).then_inc(s_lo, 1)
                tiles(dve, body)

            @block.tensor
            def _(pe):
                def body(t, p):
                    pe.wait_ge(s_xn, t + 1)
                    wait(pe, s_lo, t * 2 - 2)
                    for k in range(KD):
                        ins = nc.tensor.transpose(TP[p % 2][k // 4][:, (k % 4) * P:(k % 4 + 1) * P],
                                                  xn[p % 2][:, k * P:(k + 1) * P], ident[:])
                        if k % 4 == 3:
                            ins.then_inc(s_tp, 1)
                tiles(pe, body)


def project(nc, l, sem, sb_in, ps_in, xh, xl, w_pairs, first, g_ln, lb, lb1, proj, kgate):
    s_w = sem.software(f"pj{l}_w")
    s_wg, s_wh, s_wl, s_mm, s_free, s_stage, s_sig, s_act = (
        sem(f"pj{l}_{n}") for n in ("wg", "wh", "wl", "mm", "free", "stage", "sig", "act"))
    s_st = [sem(f"pj{l}_st{b}") for b in range(NBLK)]
    s_st2 = [sem(f"pj{l}_st2{b}") for b in range(NBLK)]
    plain, gate, forget = "plain", "gate", "forget"
    if l == 0:
        parts = [(GQ, GK, plain, -HD ** -0.5), (GK, GX, plain, 1.0), (GX, GG, plain, -HD ** -0.5), (GG, NG, gate, 1.0)]
    else:
        parts = [(GQ, GK, plain, 1.0), (GK, GV, forget, 1.0), (GV, GX, plain, 1.0), (GX, GG, plain, -HD ** -0.5),
                 (GG, NG, gate, 1.0)]
    with ExitStack() as ctx:
        sb, ps = sb_in(ctx), ps_in(ctx)
        wraw = first.buf
        wg = sb(f"pj{l}_wg", [P, KD, P])
        wh = [sb(f"pj{l}_wh{i}", [P, KD, P], F32R) for i in range(2)]
        wl = [sb(f"pj{l}_wl{i}", [P, KD, P], F32R) for i in range(2)]
        stage = [sb(f"pj{l}_stg{b}", [P, BLOCKS[b][1]]) for b in range(NBLK)]
        stage2 = [sb(f"pj{l}_stg2{b}", [P, BLOCKS[b][1]]) for b in range(NBLK)]
        acc = [ps(f"pj{l}_acc{b}", [P, 512]) for b in range(NBLK)]
        with nc.Block() as block:
            @block.gpsimd
            def _(pool):
                def body(i, _):
                    wait(pool, s_wg, i * 2)
                    pool.dma_start(wraw[:], w_pairs[i]).then_inc(s_w, 16)
                sweep(pool, 1, NG // 2, 1, body)

            @block.sync
            def _(sp):
                for lo, hi, kind, _ in parts:
                    def body(c, _):
                        for b, (at, n) in enumerate(BLOCKS):
                            sp.wait_ge(s_stage, c * NBLK + (b + 1))
                            sp.dma_start(proj[c][:, at:at + n], stage[b][:]).then_inc(s_st[b], 16)
                            if kind == forget:
                                sp.dma_start(kgate[c - GK][:, at:at + n], stage2[b][:]).then_inc(s_st2[b], 16)
                    sweep(sp, lo, hi, 1, body)
                for b in range(NBLK):
                    sp.wait_ge(s_st[b], 16 * NG)
                    if l == 1:
                        sp.wait_ge(s_st2[b], 16 * MG)

            @block.scalar
            def _(act):
                def high(c, p):
                    act.wait_ge(s_wg, c + 1)
                    wait(act, s_mm, (c - 1) * NBLK)
                    nc.scalar.copy(wh[p][:], wg[:]).then_inc(s_wh, 1)
                high(0, 0)
                for lo, hi, kind, scale in parts:
                    def body(c, p):
                        if not (isinstance(c, int) and c == NG - 1):
                            high(c + 1, 1 - p)
                        for b, (at, n) in enumerate(BLOCKS):
                            act.wait_ge(s_mm, c * NBLK + (b + 1))
                            wait(act, s_st[b], c * 16)
                            if kind == plain:
                                nc.scalar.mul(stage[b][:], acc[b][:, 0:n], scale).then_inc(s_stage, 1)
                            elif kind == gate:
                                nc.scalar.activation(stage[b][:], acc[b][:, 0:n], ACT.Sigmoid).then_inc(s_sig, 1)
                            else:
                                if not (isinstance(c, int) and c == GK):
                                    act.wait_ge(s_st2[b], (c - GK) * 16)
                                nc.scalar.activation(stage[b][:], acc[b][:, 0:n], ACT.Sigmoid)
                                nc.scalar.activation(stage2[b][:], acc[b][:, 0:n], ACT.Sigmoid, scale=-1.0).then_inc(s_sig, 1)
                    if hi == NG:
                        sweep(act, lo, hi - 2, 2, body)
                        body(hi - 2, 0)
                        body(hi - 1, 1)
                    else:
                        sweep(act, lo, hi, 2, body)

            @block.vector
            def _(dve):
                def low(c, p):
                    wait(dve, s_w, (c - p) * 8)
                    wait(dve, s_wl, c)
                    nc.vector.tensor_tensor(wg[:], wraw[:, :, p * P:(p + 1) * P],
                                            g_ln[:, l].unsqueeze(2).to_broadcast([P, KD, P]), ALU.mult).then_inc(s_wg, 1)
                    dve.wait_ge(s_wh, c + 1)
                    nc.vector.tensor_tensor(wl[p][:], wg[:], wh[p][:].bitcast(F32), ALU.subtract).then_inc(s_wl, 1)
                first.wait(dve)
                low(0, 0)
                seen = 0
                for lo, hi, kind, _ in parts:
                    def body(c, p):
                        if not (isinstance(c, int) and c == NG - 1):
                            low(c + 1, 1 - p)
                        if kind == plain:
                            return
                        for b, (at, n) in enumerate(BLOCKS):
                            dve.wait_ge(s_sig, (c - lo + seen) * NBLK + (b + 1))
                            if kind == gate:
                                nc.vector.tensor_tensor(stage[b][:], acc[b][:, 0:n], stage[b][:], ALU.mult).then_inc(s_stage, 1)
                            else:
                                g = bass.ds(c - GK, 1)
                                nc.vector.tensor_scalar(stage2[b][:], stage2[b][:], lb1[:, g], None, ALU.mult)
                                nc.vector.tensor_scalar(stage[b][:], stage[b][:], lb1[:, g], lb[:, g],
                                                        ALU.mult, ALU.add).then_inc(s_stage, 1)
                    if hi == NG:
                        sweep(dve, lo, hi - 2, 2, body)
                        body(hi - 2, 0)
                        body(hi - 1, 1)
                    else:
                        sweep(dve, lo, hi, 2, body)
                    if kind != plain:
                        seen += hi - lo

            @block.tensor
            def _(pe):
                def body(c, p):
                    pe.wait_ge(s_wl, c + 1)
                    for b, (at, n) in enumerate(BLOCKS):
                        wait(pe, s_stage, c * NBLK - NBLK + (b + 1))
                        for k in range(KD):
                            for w, x in ((wh, xh), (wl, xh), (wh, xl)):
                                ins = nc.tensor.matmul(acc[b][:, 0:n], w[p][:, k], x[:, k, at:at + n],
                                                       start=(k == 0 and x is xh and w is wh),
                                                       stop=(k == KD - 1 and x is xl))
                        ins.then_inc(s_mm, 1)
                sweep(pe, 0, NG, 2, body)


def keys_out(nc, sem, sb_in, ps_in, ident, proj, a_k_prompt, a_v_prompt, a_k_sample, a_v_sample, ahead):
    s_in = [sem(f"ko_in{i}") for i in range(2)]
    s_out = [sem.software(f"ko_out{i}") for i in range(2)]
    s_tp, s_ev = sem("ko_tp"), sem("ko_ev")
    jobs = [(g, t) for t in range(NT - 4, NT + 1) for g in (GK, GV)]
    with ExitStack() as ctx:
        sb, ps = sb_in(ctx), ps_in(ctx)
        src = [sb(f"ko_src{i}", [P, MG, P]) for i in range(2)]
        dst = [sb(f"ko_dst{i}", [P, MIX]) for i in range(2)]
        TP = [[ps(f"ko_tp{i}{h}", [P, 512]) for h in range(2)] for i in range(2)]
        with nc.Block() as block:
            @block.sync
            def _(sp):
                for n, (g, t) in enumerate(jobs):
                    wait(sp, s_tp, n - 1)
                    sp.dma_start(src[n % 2][:], proj[g:g + MG, :, t * P:(t + 1) * P].rearrange("g p n -> p g n")
                                 ).then_inc(s_in[n % 2], 16)
                    if n == len(jobs) - 4:
                        ahead.issue(sp)

            @block.gpsimd
            def _(pool):
                for n, (g, t) in enumerate(jobs):
                    pool.wait_ge(s_ev, 2 * n + 2)
                    if t == TS:
                        out = (a_k_sample if g == GK else a_v_sample)[0].rearrange("b s h d -> (b s) (h d)")
                    else:
                        r = (t - (NT - 4)) * P
                        out = (a_k_prompt if g == GK else a_v_prompt)[0, 0, r:r + P].rearrange("p h d -> p (h d)")
                    pool.dma_start(out, dst[n % 2][:]).then_inc(s_out[n % 2], 16)
                for i in range(2):
                    pool.wait_ge(s_out[i], 16 * (len(jobs) // 2))

            @block.tensor
            def _(pe):
                for n in range(len(jobs)):
                    pe.wait_ge(s_in[n % 2], 16 * (n // 2 + 1))
                    wait(pe, s_ev, 2 * n - 2)
                    for g in range(MG):
                        ins = nc.tensor.transpose(TP[n % 2][g // 3][:, (g % 3) * P:(g % 3 + 1) * P], src[n % 2][:, g], ident[:])
                    ins.then_inc(s_tp, 1)

            @block.vector
            def _(dve):
                for n in range(len(jobs)):
                    dve.wait_ge(s_tp, n + 1)
                    wait(dve, s_out[n % 2], 16 * (n // 2))
                    for h in range(2):
                        nc.vector.tensor_copy(dst[n % 2][:, h * 384:(h + 1) * 384], TP[n % 2][h][:, 0:384]).then_inc(s_ev, 1)


class Unit:

    def __init__(self, col, tiles, split, score, bias, pv, heads=(0,), at=None):
        self.col, self.tiles, self.split, self.score, self.bias, self.pv = col, tiles, split, score, bias, pv
        self.width = tiles * P
        self.heads = heads
        self.at = at


def tp_cols(unit, i):
    return i * P if i < unit.split else 512 + (i - unit.split) * P


def unit_scores(nc, unit, sc):
    for cols, rows, q, k in unit.score:
        ins = nc.tensor.matmul(sc[rows, cols], q, k, start=True, stop=True)
    return ins


def unit_min(nc, unit, sc, se, minimum):
    n = unit.width
    if unit.bias is None:
        return nc.vector.tensor_reduce(minimum, sc[:, 0:n].rearrange("p (h k) -> p h k", h=len(unit.heads)), AX_X, ALU.min)
    return nc.vector.tensor_tensor_reduce(se[:, 0:n], sc[:, 0:n], unit.bias, 1.0, 3e38, ALU.add, ALU.min, minimum)


def unit_exp(nc, unit, sc, se, minimum, total):
    src = sc if unit.bias is None else se
    w = unit.width // len(unit.heads)
    for i, h in enumerate(unit.heads):
        ins = nc.scalar.activation(se[:, i * w:(i + 1) * w], src[:, i * w:(i + 1) * w], ACT.Exp, bias=minimum[:, i:i + 1],
                                   scale=-1.0, accum_out=total[:, h:h + 1])
    return ins


def unit_transposes(nc, unit, se, tp, ident):
    for i in range(unit.tiles):
        at = tp_cols(unit, i)
        ins = nc.tensor.transpose(tp[:, at:at + P], se[:, i * P:(i + 1) * P], ident[:])
    return ins


def unit_evac_low(unit, copy, pt, tp):
    if unit.tiles == 1:
        return copy(pt[0:64, 0:P], tp[0:64, 0:P])
    return copy(pt[:, 0:unit.split * P], tp[:, 0:unit.split * P])


def unit_evac_high(unit, copy, pt, tp):
    if unit.tiles == 1:
        return copy(pt[64:P, 0:P], tp[64:P, 0:P])
    n = (unit.tiles - unit.split) * P
    return copy(pt[:, unit.split * P:unit.width], tp[:, 512:512 + n])


def unit_pv(nc, unit, pt, ob):
    first = {}
    last = {}
    def head(i):
        return unit.heads[i * len(unit.heads) // unit.tiles]

    def sum_of(rows, i):
        return rows.start, head(i)
    for n, (rows, i, *_) in enumerate(unit.pv):
        first.setdefault(sum_of(rows, i), n)
        last[sum_of(rows, i)] = n
    for n, (rows, i, cols, val) in enumerate(unit.pv):
        col = unit.col + head(i) * HD
        ins = nc.tensor.matmul(ob[rows, col:col + HD], pt[:, i * P + cols.start:i * P + cols.stop], val,
                               start=first[sum_of(rows, i)] == n, stop=last[sum_of(rows, i)] == n)
    return ins


ALL = slice(0, P)


def cross_unit(q, keys, vals, at):
    score = []
    heads = tuple(range(0, HX, 2)) + tuple(range(1, HX, 2))
    for c, h in enumerate(heads):
        g, po = h // 2, HD * (h % 2)
        score.append((slice(c * NMEM, (c + 1) * NMEM), ALL, q[po:po + HD, g], keys[po:po + HD, g]))
    n = NMEM // P
    return Unit(MIX, HX * n, HX * n // 2, score, None,
                [(ALL, n * c + i, ALL, vals[:, i, h * HD:(h + 1) * HD]) for c, h in enumerate(heads) for i in range(n)],
                heads=heads, at=slice(at, at + HX))


def sample_attention(nc, name, sem, sb_in, ps_in, ident, units_of, loads, o_s, bias_width, ahead, extra=None, later=None,
                     side=None):
    s_ld, s_tp, s_eva, s_evd, s_sc, s_min, s_exp, s_pv, s_rs, s_bias = (
        sem(f"{name}_{n}") for n in ("ld", "tp", "eva", "evd", "sc", "min", "exp", "pv", "rs", "bias"))
    with ExitStack() as ctx:
        sb, ps = sb_in(ctx), ps_in(ctx)
        bufs, dmas, turns = loads(sb)
        se = [sb(f"{name}_se{i}", [P, bias_width]) for i in range(2)]
        pt = [sb(f"{name}_pt{i}", [P, bias_width]) for i in range(2)]
        mn = sb(f"{name}_mn", [P, 16])
        tot = sb(f"{name}_tot", [P, 16])
        rs = sb(f"{name}_rs", [P, 16])
        SC = [ps(f"{name}_SC{i}", [P, 1024]) for i in range(2)]
        TP = ps(f"{name}_TP", [P, 1024])
        OB = ps(f"{name}_OB", [P, 1024])
        units = units_of(bufs)
        U, NR = len(units), len(turns)
        o_cols = slice(units[0].col, units[-1].col + HD)
        with nc.Block() as block:
            @block.sync
            def _(sp):
                for out, src in dmas:
                    sp.dma_start(out, src).then_inc(s_ld, 16)
                if later:
                    later.issue(sp)
                if side:
                    side.sync(sp)

            @block.gpsimd
            def _(pool):
                if side:
                    side.gpsimd(pool)

            @block.tensor
            def _(pe):
                ahead.wait(pe)
                for n, (srcs, _) in enumerate(turns):
                    wait(pe, s_eva, n - 1)
                    wait(pe, s_evd, n - 1)
                    for i, src in enumerate(srcs):
                        at = i % (len(srcs) // 2) * P + 512 * (i // (len(srcs) // 2))
                        ins = nc.tensor.transpose((TP, OB)[n % 2][:, at:at + P], src, ident[:])
                    ins.then_inc(s_tp, 1)

                def scores(u):
                    wait(pe, s_exp, u - 1)
                    unit_scores(nc, units[u], SC[u % 2]).then_inc(s_sc, 1)

                def values(u):
                    pe.wait_ge(s_eva, NR + u + 1)
                    pe.wait_ge(s_evd, NR + u + 1)
                    unit_pv(nc, units[u], pt[u % 2], OB).then_inc(s_pv, 1)
                pe.wait_ge(s_ld, 16 * len(dmas))
                pe.wait_ge(s_eva, NR)
                pe.wait_ge(s_evd, NR)
                scores(0)
                scores(1)
                for u in range(U):
                    pe.wait_ge(s_exp, u + 1)
                    wait(pe, s_eva, NR + u)
                    wait(pe, s_evd, NR + u)
                    unit_transposes(nc, units[u], se[u % 2], TP, ident).then_inc(s_tp, 1)
                    if u:
                        values(u - 1)
                    if u + 2 < U:
                        scores(u + 2)
                values(U - 1)

            @block.vector
            def _(dve):
                def low_min(u):
                    dve.wait_ge(s_sc, u + 1)
                    unit_min(nc, units[u], SC[u % 2], se[u % 2], mn[:, u:u + 1]).then_inc(s_min, 1)
                if extra:
                    ahead.wait(dve)
                    extra(bufs, dve, s_bias)
                for n, (srcs, dst) in enumerate(turns):
                    dve.wait_ge(s_tp, n + 1)
                    half = len(srcs) // 2
                    nc.vector.tensor_copy(dst[1], (TP, OB)[n % 2][:, 512:512 + half * P].rearrange("p (g n) -> p g n", n=P)
                                          ).then_inc(s_evd, 1)
                if extra:
                    dve.wait_ge(s_bias, 1)
                low_min(0)
                low_min(1)
                for u in range(U):
                    dve.wait_ge(s_tp, NR + u + 1)
                    unit_evac_high(units[u], nc.vector.tensor_copy, pt[u % 2], TP).then_inc(s_evd, 1)
                    if u + 2 < U:
                        low_min(u + 2)
                    if side:
                        side.vector(dve, u)
                dve.wait_ge(s_pv, U)
                nc.vector.reciprocal(rs[:, 0:U], tot[:, 0:U]).then_inc(s_rs, 1)
                dve.wait_ge(s_rs, 1)
                for c in range(o_cols.start, o_cols.stop, 256):
                    u0 = (c - o_cols.start) // HD
                    nc.vector.tensor_tensor(o_s[:, c:c + 256].rearrange("p (h d) -> p h d", d=HD),
                                            OB[:, c:c + 256].rearrange("p (h d) -> p h d", d=HD),
                                            rs[:, u0:u0 + 4].unsqueeze(2).to_broadcast([P, 4, HD]), ALU.mult)

            @block.scalar
            def _(act):
                def exp(u):
                    act.wait_ge(s_min, u + 1)
                    unit_exp(nc, units[u], SC[u % 2], se[u % 2], mn[:, u:u + 1], tot[:, u:u + 1]).then_inc(s_exp, 1)
                for n, (srcs, dst) in enumerate(turns):
                    act.wait_ge(s_tp, n + 1)
                    half = len(srcs) // 2
                    nc.scalar.copy(dst[0], (TP, OB)[n % 2][:, 0:half * P].rearrange("p (g n) -> p g n", n=P)).then_inc(s_eva, 1)
                exp(0)
                exp(1)
                for u in range(U):
                    act.wait_ge(s_tp, NR + u + 1)
                    unit_evac_low(units[u], nc.scalar.copy, pt[u % 2], TP).then_inc(s_eva, 1)
                    if u + 2 < U:
                        exp(u + 2)
                    if side:
                        side.scalar(act, u)


def halves(h, po, g, q, keys, new, vals, vnew, tiles, split, bias, col):
    score, pv = [], []
    n = tiles - (1 if new is not None else 0)
    for half in range(2):
        rows = slice(64 * half, 64 * half + 64)
        for at in range(0, n * P, 512):
            score.append((slice(at, at + 512), rows, q[po:po + HD, g, rows], keys[po:po + HD, g, n * P * half + at:n * P * half + at + 512]))
    if new is not None:
        score.append((slice(n * P, n * P + P), ALL, q[po:po + HD, g], new[po:po + HD, g]))
    for half in range(2):
        rows = slice(64 * half, 64 * half + 64)
        for i in range(tiles):
            v = vals[:, n * half + i, h * HD:(h + 1) * HD] if i < n else vnew[:, h * HD:(h + 1) * HD]
            pv.append((rows, i, rows, v))
    return Unit(col, tiles, split, score, bias, pv)


def band_loads(sem, sb, v):
    ck = v["cache_a_k"][0].rearrange("b s h d -> s b (h d)")
    cv = v["cache_a_v"][0].rearrange("b s h d -> s b (h d)")
    ahead = Ahead(sem, "sa_ahead")
    ahead.raw = sb("sa_raw", [P, SB, MIX])
    ahead.vals = sb("sa_v", [P, SB, MIX])
    ahead.tb = sb("sa_tb", [P, HA, P])
    ahead.tn = sb("sa_tn", [P, HA, SL])
    for b in range(SB):
        rows = slice(b * SL, (b + 1) * SL)
        ahead.loads.append((ahead.tb[rows], bass.AP(v["ext"].tensor, 511, [[767, SL], [P * 768, HA], [1, P]])))
        ahead.loads.append((ahead.tn[rows], bass.AP(v["ext"].tensor, 639, [[767, SL], [P * 768, HA], [1, SL]])))
    ahead.loads += [(ahead.raw[:], ck), (ahead.vals[:], cv)]
    return ahead


def sample_band(nc, sem, sb_in, ps_in, v, o_s, ahead, later):
    ident, proj, seqmask = v["ident"], v["proj"], v["seqmask"]
    raw, vals, tb, tn = ahead.raw, ahead.vals, ahead.tb, ahead.tn
    vn = v["a_v_sample"][0].rearrange("b s h d -> (b s) (h d)")
    tok = slice(SEQ, NTOK)

    def loads(sb):
        kT = sb("sa_kT", [P, MG, SB * P])
        knew = sb("sa_knew", [P, MG, P])
        vnew = sb("sa_vnew", [P, MIX])
        q = sb("sa_q", [P, MG, P])
        bias = sb("sa_bias", [P, HA, 5 * P])
        off = sb("sa_off", [P, 4])
        offn = sb("sa_offn", [P, SB])
        dmas = [(q[:], proj[GQ:GQ + MG, :, tok].rearrange("g p n -> p g n")),
                (knew[:], proj[GK:GK + MG, :, tok].rearrange("g p n -> p g n")), (vnew[:], vn)]
        turns = [([raw[:, b, g * P:(g + 1) * P] for g in range(MG)],
                  (kT[:, 0:3, b * P:(b + 1) * P], kT[:, 3:6, b * P:(b + 1) * P])) for b in range(SB)]
        return (kT, vals, knew, vnew, q, tb, tn, bias, off, offn), dmas, turns

    def units_of(bufs):
        kT, vals, knew, vnew, q, tb, tn, bias, off, offn = bufs
        return [halves(h, HD * (h % 2), h // 2, q, kT, knew, vals, vnew, 5, 3, bias[:, h], h * HD) for h in range(HA)]

    def extra(bufs, dve, s_bias):
        kT, vals, knew, vnew, q, tb, tn, bias, off, offn = bufs
        link = Chain(dve, sem("sa_cdve"))
        link(nc.vector.tensor_tensor(off[:], seqmask[:, 0:4], seqmask[:, 4:8], ALU.add))
        link(nc.vector.tensor_scalar(off[:], off[:], -BIG, BIG, ALU.mult, ALU.add))
        link(nc.vector.tensor_scalar(offn[:], seqmask[:], -BIG, BIG, ALU.mult, ALU.add))
        for i in range(4):
            nc.vector.tensor_scalar(bias[:, :, i * P:(i + 1) * P], tb[:], off[:, i:i + 1], None, ALU.add)
        for b in range(SB):
            ins = nc.vector.tensor_scalar(bias[:, :, 4 * P + b * SL:4 * P + (b + 1) * SL], tn[:], offn[:, b:b + 1], None,
                                          ALU.add)
        ins.then_inc(s_bias, 1)

    sample_attention(nc, "sa", sem, sb_in, ps_in, ident, units_of, loads, o_s, 5 * P, ahead, extra, later)


def cross_loads(l, sem, sb, v):
    ahead = Ahead(sem, f"sx{l}_ahead")
    ahead.raw = sb(f"sx{l}_raw", [P, 2 * SB, XW])
    ahead.vals = sb(f"sx{l}_v", [P, 2 * SB, XW])
    ahead.loads = [(ahead.raw[:], v["cache_mem_k"][l].rearrange("b (t p) h d -> p (b t) (h d)", p=P)),
                   (ahead.vals[:], v["cache_mem_v"][l].rearrange("b (t p) h d -> p (b t) (h d)", p=P))]
    return ahead


def sample_cross(nc, l, sem, sb_in, ps_in, v, o_s, ahead, side):
    ident, proj, seqmask = v["ident"], v["proj"], v["seqmask"]
    raw, vals = ahead.raw, ahead.vals
    name = f"sx{l}"

    def loads(sb):
        kT = sb(f"{name}_kT", [P, 2, 2 * SB * P])
        q = sb(f"{name}_q", [P, 2, P])
        off = sb(f"{name}_off", [P, 4])
        bias = sb(f"{name}_bias", [P, 4, 2 * P])
        dmas = [(q[:], proj[GX:GX + 2, :, SEQ:NTOK].rearrange("g p n -> p g n"))]
        turns = [([raw[:, 2 * b + t, g * P:(g + 1) * P] for g in range(2) for t in range(2)],
                  (kT[:, 0, b * 2 * P:(b + 1) * 2 * P].rearrange("p (t n) -> p t n", n=P),
                   kT[:, 1, b * 2 * P:(b + 1) * 2 * P].rearrange("p (t n) -> p t n", n=P))) for b in range(SB)]
        return (kT, vals, q, off, bias), dmas, turns

    def units_of(bufs):
        kT, vals, q, off, bias = bufs
        flat = bias[:].rearrange("p b n -> p (b n)")
        return [halves(h, HD * (h % 2), h // 2, q, kT, None, vals, None, 8, 4, flat, MIX + h * HD) for h in range(HX)]

    def extra(bufs, dve, s_bias):
        kT, vals, q, off, bias = bufs
        link = Chain(dve, sem(f"{name}_cdve"))
        link(nc.vector.tensor_tensor(off[:], seqmask[:, 0:4], seqmask[:, 4:8], ALU.add))
        link(nc.vector.tensor_scalar(off[:], off[:], -BIG, BIG, ALU.mult, ALU.add))
        nc.vector.tensor_copy(bias[:], off[:].unsqueeze(2).to_broadcast([P, 4, 2 * P])).then_inc(s_bias, 1)

    sample_attention(nc, name, sem, sb_in, ps_in, ident, units_of, loads, o_s, 8 * P, ahead, extra, side=side)


def sample_hgrn(nc, sem, sb_in, ps_in, v, o_s, later):
    ident, proj, seqmask, neg_half = v["ident"], v["proj"], v["seqmask"], v["neg_half"]
    tok = slice(SEQ, NTOK)
    LEVELS = 5
    s_ld, s_st, s_tp, s_ev, s_lv, s_cp, s_qz, s_o, s_kz, s_kv, s_s, s_oc, s_sq, s_ms, s_rs, s_out, c_pool, c_dve = (
        sem(f"sh_{n}") for n in ("ld", "st", "tp", "ev", "lv", "cp", "qz", "o", "kz", "kv", "s", "oc", "sq", "ms", "rs",
                                 "out", "cpool", "cdve"))
    with ExitStack() as ctx:
        sb, ps = sb_in(ctx), ps_in(ctx)
        q, f, k, iT = (sb(f"sh_{n}", [P, MIX]) for n in ("q", "f", "k", "iT"))
        qm = {m: sb(f"sh_q{m}", [P, MIX]) for m in (1, 2, 4, 8, 16)}
        km = {m: sb(f"sh_k{m}", [P, MIX]) for m in (2, 4, 8, 16)}
        tm = {m: sb(f"sh_t{m}", [P, MIX // m]) for m in (2, 4, 8, 16)}
        qm[0], km[0], km[1], tm[1] = q, k, k, f
        am, inat, knat = (sb(f"sh_{n}", [P, MIX]) for n in ("a", "inat", "knat"))
        masks = sb("sh_masks", [P, LEVELS, P])
        st = sb("sh_state", [P, SB, MG, P])
        qz = [sb(f"sh_qz{i}", [P, SB * P]) for i in range(2)]
        kz = [sb(f"sh_kz{i}", [P, SB, P]) for i in range(2)]
        sq = sb("sh_sq", [P, MIX])
        ssq, ms, rs = (sb(f"sh_{n}", [P, MG]) for n in ("ssq", "ms", "rs"))
        SC = [ps(f"sh_SC{i}", [P, 1024]) for i in range(2)]
        TP = ps("sh_TP", [P, 1024])
        OB = ps("sh_OB", [P, 1024])
        with nc.Block() as block:
            @block.sync
            def _(sp):
                for buf, src in ((q, proj[GQ:GQ + MG, :, tok]), (f, proj[GK:GK + MG, :, tok]), (k, v["kgate"][:, :, tok]),
                                 (iT, proj[GV:GV + MG, :, tok])):
                    sp.dma_start(buf[:].rearrange("p (g n) -> p g n", n=P), src.rearrange("g p n -> p g n")).then_inc(s_ld, 16)
                for h in range(MG):
                    sp.dma_start(st[:, :, h], v["state_b"][0, :, h].rearrange("b k v -> k b v")).then_inc(s_st, 16)
                later.issue(sp)
                for h in range(MG):
                    sp.wait_ge(s_s, h + 1)
                    sp.dma_start(v["b_state_sample"][0, :, h].rearrange("b k v -> k b v"), st[:, :, h]).then_inc(s_out, 16)
                sp.wait_ge(s_out, 16 * MG)

            @block.gpsimd
            def _(pool):
                link = Chain(pool, c_pool)
                link(nc.gpsimd.memset(masks[:], 1.0))
                link(nc.gpsimd.affine_select(out=masks[:, 0], in_=masks[:, 0], compare_op=ALU.is_equal, fill=0.0,
                                             base=0, pattern=[[-1, P]], channel_multiplier=1))
                for i in range(1, LEVELS):
                    m = 1 << (i - 1)
                    nb = P // (2 * m)
                    view = masks[:, i].rearrange("p (b two m) -> p b two m", two=2, m=m)
                    link(nc.gpsimd.memset(view[:, :, 0, :], 0.0))
                    sel = view[:, :, 1, :]
                    link(nc.gpsimd.affine_select(out=sel, in_=sel, compare_op=ALU.is_ge, fill=0.0, base=0,
                                                 pattern=[[-2 * m, nb], [0, m]], channel_multiplier=1))
                    link(nc.gpsimd.affine_select(out=sel, in_=sel, compare_op=ALU.is_ge, fill=0.0, base=m - 1,
                                                 pattern=[[2 * m, nb], [0, m]], channel_multiplier=-1))
                for z in (am, qz[0], qz[1]):
                    link(nc.gpsimd.memset(z[:], 0.0))
                pool.wait_ge(s_ms, 1)
                nc.gpsimd.tensor_tensor(rs[:], ms[:], neg_half[:, 0:MG], ALU.pow).then_inc(s_rs, 1)
            N_POOL = 2 + 3 * (LEVELS - 1) + 3

            def update(h, dve, link):
                dve.wait_ge(s_o, h + 1)
                link(nc.vector.tensor_tensor(st[:, :, h], st[:, :, h],
                                             tm[16][:, h * SB:(h + 1) * SB].unsqueeze(2).to_broadcast([P, SB, P]), ALU.mult))
                dve.wait_ge(s_kv, h + 1)
                for c in range(2):
                    bs = slice(4 * c, 4 * c + 4)
                    ins = nc.vector.tensor_tensor(st[:, bs, h], st[:, bs, h],
                                                  SC[h % 2][:, 512 * c:512 * c + 512].rearrange("p (b v) -> p b v", v=P), ALU.add)
                ins.then_inc(s_s, 1)

            @block.scalar
            def _(act):
                act.wait_ge(s_oc, 1)
                nc.scalar.activation(sq[:], o_s[:, 0:MIX], ACT.Square).then_inc(s_sq, 1)

            @block.vector
            def _(dve):
                link = Chain(dve, c_dve)
                dve.wait_ge(s_ld, 64)
                dve.wait_ge(c_pool, N_POOL)
                link(nc.vector.tensor_tensor(qm[1][:], q[:], f[:], ALU.mult))
                for m in (1, 2, 4, 8):
                    n = MIX // (2 * m)

                    def two(a, width=m):
                        return a[:].rearrange("p (n two m) -> p n two m", two=2, m=width)
                    tot = two(tm[m], 1)
                    nc.vector.tensor_copy(two(qm[2 * m])[:, :, 0], two(qm[m])[:, :, 0])
                    nc.vector.tensor_copy(two(km[2 * m])[:, :, 1], two(km[m])[:, :, 1])
                    nc.vector.tensor_tensor(two(qm[2 * m])[:, :, 1], two(qm[m])[:, :, 1],
                                            tot[:, :, 0].to_broadcast([P, n, m]), ALU.mult)
                    nc.vector.tensor_tensor(two(km[2 * m])[:, :, 0], two(km[m])[:, :, 0],
                                            tot[:, :, 1].to_broadcast([P, n, m]), ALU.mult)
                    link(nc.vector.tensor_tensor(tm[2 * m][:].unsqueeze(2), tot[:, :, 0], tot[:, :, 1], ALU.mult))
                dve.wait_ge(s_tp, 1)
                nc.vector.tensor_copy(inat[:].rearrange("p (c n) -> p c n", n=384),
                                      TP[:].rearrange("p (c n) -> p c n", n=512)[:, :, 0:384]).then_inc(s_ev, 1)
                for i in range(LEVELS):
                    dve.wait_ge(s_lv, i + 1)
                    nc.vector.copy_predicated(am[:].rearrange("p (c n) -> p c n", n=P),
                                              masks[:, i:i + 1].bitcast(U32).to_broadcast([P, MG, P]),
                                              SC[i % 2][:, 0:MIX].rearrange("p (h n) -> p h n", n=P)).then_inc(s_cp, 1)
                    dve.wait_ge(s_cp, i + 1)
                dve.wait_ge(s_tp, 2)
                nc.vector.tensor_copy(knat[:].rearrange("p (c n) -> p c n", n=384),
                                      TP[:].rearrange("p (c n) -> p c n", n=512)[:, :, 0:384]).then_inc(s_ev, 1)
                dve.wait_ge(s_ev, 2)
                dve.wait_ge(s_st, 16 * MG)
                for h in range(MG):
                    hs = slice(h * P, (h + 1) * P)
                    wait(dve, s_o, h - 1)
                    nc.vector.tensor_copy(bass.AP(qz[h % 2][:].tensor, 0, [[SB * P, P], [P + SL, SB], [1, SL]]),
                                          qm[16][:, hs].rearrange("p (b n) -> p b n", n=SL)).then_inc(s_qz, 1)
                    wait(dve, s_kv, h - 1)
                    nc.vector.tensor_tensor(kz[h % 2][:], knat[:, hs].unsqueeze(1).to_broadcast([P, SB, P]),
                                            seqmask[:].unsqueeze(2).to_broadcast([P, SB, P]), ALU.mult).then_inc(s_kz, 1)
                    if h:
                        update(h - 1, dve, link)
                update(MG - 1, dve, link)
                nc.vector.tensor_copy(o_s[:, 0:512], OB[:, 0:512])
                nc.vector.tensor_copy(o_s[:, 512:MIX], OB[:, 512:MIX]).then_inc(s_oc, 1)
                dve.wait_ge(s_sq, 1)
                link(nc.vector.tensor_reduce(ssq[:], sq[:].rearrange("p (h d) -> p h d", d=P), AX_X, ALU.add))
                nc.vector.tensor_scalar(ms[:], ssq[:], 1.0 / P, EPS, ALU.mult, ALU.add).then_inc(s_ms, 1)
                dve.wait_ge(s_rs, 1)
                nc.vector.tensor_tensor(o_s[:, 0:MIX].rearrange("p (h d) -> p h d", d=P),
                                        o_s[:, 0:MIX].rearrange("p (h d) -> p h d", d=P),
                                        rs[:].unsqueeze(2).to_broadcast([P, MG, P]), ALU.mult)

            @block.tensor
            def _(pe):
                def turn(src):
                    for g in range(MG):
                        at = (g % 3) * P + 512 * (g // 3)
                        ins = nc.tensor.transpose(TP[:, at:at + P], src[:, g * P:(g + 1) * P], ident[:])
                    ins.then_inc(s_tp, 1)
                pe.wait_ge(s_ld, 64)
                pe.wait_ge(c_dve, 5)
                turn(iT)
                for i in range(LEVELS):
                    wait(pe, s_cp, i - 1)
                    m = 0 if i == 0 else 1 << (i - 1)
                    for h in range(MG):
                        hs = slice(h * P, (h + 1) * P)
                        ins = nc.tensor.matmul(SC[i % 2][:, hs], km[m][:, hs], qm[m][:, hs], start=True, stop=True)
                    ins.then_inc(s_lv, 1)
                pe.wait_ge(s_ev, 1)
                turn(km[16])
                pe.wait_ge(s_cp, LEVELS)
                pe.wait_ge(s_st, 16 * MG)
                for h in range(MG):
                    hs = slice(h * P, (h + 1) * P)
                    pe.wait_ge(s_qz, h + 1)
                    nc.tensor.matmul(OB[:, hs], am[:, hs], inat[:, hs], start=True, stop=False)
                    for b in range(SB):
                        ins = nc.tensor.matmul(OB[:, hs], qz[h % 2][:, b * P:(b + 1) * P], st[:, b, h], start=False,
                                               stop=(b == SB - 1))
                    ins.then_inc(s_o, 1)
                    pe.wait_ge(s_kz, h + 1)
                    wait(pe, s_s, h - 1)
                    for b in range(SB):
                        ins = nc.tensor.matmul(SC[h % 2][:, b * P:(b + 1) * P], kz[h % 2][:, b], inat[:, hs], start=True, stop=True)
                    ins.then_inc(s_kv, 1)


class SplitOutWeights:
    BUFS = 4

    def __init__(self, nc, l, sem, sb, v, woh, wol, bias):
        self.nc, self.l, self.v, self.woh, self.wol, self.bias = nc, l, v, woh, wol, bias
        self.s_in = [sem(f"wo{l}_in{i}") for i in range(self.BUFS)]
        self.s_h, self.s_l, self.s_b = sem(f"wo{l}_h"), sem(f"wo{l}_l"), sem(f"wo{l}_b")
        self.raw = [sb(f"wo{l}_raw{i}", [P, D]) for i in range(self.BUFS)]

    def sync(self, sp):
        for k in range(KD):
            wait(sp, self.s_l, k - self.BUFS + 1)
            sp.dma_start(self.raw[k % self.BUFS][:], self.v["w_out"][self.l, k * P:(k + 1) * P]
                         ).then_inc(self.s_in[k % self.BUFS], 16)
            if k == self.BUFS - 1 and self.bias is not None:
                sp.dma_start(self.bias[:], bass.AP(self.v["ext"].tensor, P - 1, [[767, P], [P * 768, HA], [1, BAND]])
                             ).then_inc(self.s_b, 16)

    def gpsimd(self, pool):
        if self.bias is not None:
            pool.wait_ge(self.s_b, 16)

    def rows(self, u):
        for k in range(KD // HX * u, KD // HX * (u + 1)):
            yield k, self.v["g_hgrn"][:, k:k + 1] if self.l == 1 and k < MG else 1.0

    def scalar(self, act, u):
        for k, g in self.rows(u):
            act.wait_ge(self.s_in[k % self.BUFS], 16 * (k // self.BUFS + 1))
            self.nc.scalar.activation(self.woh[:, k], self.raw[k % self.BUFS][:], ACT.Copy, scale=g).then_inc(self.s_h, 1)

    def vector(self, dve, u):
        for k, g in self.rows(u):
            dve.wait_ge(self.s_h, k + 1)
            self.nc.vector.scalar_tensor_tensor(out=self.wol[:, k], in0=self.raw[k % self.BUFS][:], scalar=g,
                                                in1=self.woh[:, k].bitcast(F32), op0=ALU.mult, op1=ALU.subtract
                                                ).then_inc(self.s_l, 1)


def mix(nc, l, software, sb_in, ps_in, v):
    with ExitStack() as ctx:
        sb = sb_in(ctx)
        o_s = sb(f"o_s{l}", [P, D])
        woh = wol = bias = None
        with ExitStack() as outer:
            sem_l = outer.enter_context(Semaphores(nc, software))
            cross = cross_loads(l, sem_l, v["sb_far_in"](outer), v)
            with ExitStack() as inner:
                if l == 0:
                    band = band_loads(sem_l, sb_in(inner), v)
                    keys_out(nc, sem_l, sb_in, ps_in, v["ident"], v["proj"], v["a_k_prompt"], v["a_v_prompt"],
                             v["a_k_sample"], v["a_v_sample"], band)
                    sample_band(nc, sem_l, sb_in, ps_in, v, o_s, band, cross)
                else:
                    sample_hgrn(nc, sem_l, sb_in, ps_in, v, o_s, cross)
            woh = sb(f"woh{l}", [P, KD, D], F32R)
            wol = sb(f"wol{l}", [P, KD, D], F32R)
            bias = sb("pr_bias", [P, HA, BAND]) if l == 0 else None
            side = SplitOutWeights(nc, l, sem_l, sb_in(outer), v, woh, wol, bias)
            sample_cross(nc, l, sem_l, sb_in, ps_in, v, o_s, cross, side)
        with Semaphores(nc, software) as sem:
            prompt(nc, l, sem, sb_in, ps_in, v, o_s, woh, wol, bias)


def prompt(nc, l, sem, sb_in, ps_in, v, o_s, woh, wol, bias):
    ident, proj, mem_kT, mem_v, neg_half = (v[n] for n in ("ident", "proj", "mem_kT", "mem_v", "neg_half"))
    band = l == 0
    nm = f"pr{l}_"
    U = (HA if band else 0) + 1
    PRE, MID = 1, (0 if band else 1)
    PER_D, PER_A = PRE + 1 + MID + U, PRE + MID + U
    LEVELS = 8
    both = ["tp", "eva", "evd", "sc", "min", "exp", "pv", "rs", "o", "yg", "yh", "yl", "op", "xadd", "ldg"]
    of_layer = (["vc", "kc", "bias"] if band else
                ["out", "ldf", "fsq", "fms", "frs", "fsc", "hst", "hcp", "hv", "ocp", "lv", "cp", "kv", "s", "osq", "oms", "ors", "init"])
    S = {n: sem(nm + n) for n in both + of_layer}
    s_ld = [sem(nm + f"ld{i}") for i in range(2)]
    s_ldk = [sem(nm + f"ldk{i}") for i in range(2 if band else 0)]
    s_ldx = [sem(nm + f"ldx{i}") for i in range(2)]
    s_stx = [sem.software(nm + f"stx{i}") for i in range(2)]
    LOADS = 3 if band else 5
    with ExitStack() as ctx:
        sb, ps = sb_in(ctx), ps_in(ctx)
        xq = [sb(nm + f"xq{i}", [P, 2, P]) for i in range(2)]
        gt = sb(nm + "gate", [P, KD, P])
        xt = [sb(nm + f"x{i}", [P, D]) for i in range(2)]
        se = [sb(nm + f"se{i}", [P, HX * NMEM]) for i in range(min(U, 2))]
        pt = [sb(nm + f"pt{i}", [P, BAND if band else HX * NMEM]) for i in range(min(U, 2))]
        mn = sb(nm + "mn", [P, 16])
        tot = sb(nm + "tot", [P, 16])
        rs = sb(nm + "rs", [P, 16])
        o = sb(nm + "o", [P, D])
        y = sb(nm + "y", [P, D])
        yh = sb(nm + "yh", [P, KD, P], F32R)
        yl = sb(nm + "yl", [P, KD, P], F32R)
        SC = [ps(nm + f"SC{i}", [P, 1024]) for i in range(2)]
        TP = ps(nm + "TP", [P, 1024])
        OB = ps(nm + "OB", [P, 1024])
        tT = sb(nm + "vT", [P, MG, P])
        if band:
            q = [sb(nm + f"q{i}", [P, MG, P]) for i in range(2)]
            kcur, kprev = sb(nm + "kcur", [P, MG, 512]), sb(nm + "kprev", [P, MG, 512])
            vcur, vprev = sb(nm + "vcur", [P, 4, MIX]), sb(nm + "vprev", [P, 4, MIX])
        else:
            qm = {m: sb(nm + f"q{m}", [P, MIX]) for m in (1, 2, 4, 8, 16, 32, 64, 128)}
            km = {m: sb(nm + f"k{m}", [P, MIX]) for m in (2, 4, 8, 16, 32, 64, 128)}
            tm = {m: sb(nm + f"t{m}", [P, MIX // m]) for m in (2, 4, 8, 16, 32, 64, 128)}
            q = [sb(nm + f"q0{i}", [P, MIX]) for i in range(2)]
            k1 = [sb(nm + f"k1{i}", [P, MIX]) for i in range(2)]
            t1 = [sb(nm + f"t1{i}", [P, MIX]) for i in range(2)]
            am = [sb(nm + f"a{i}", [P, MIX]) for i in range(2)]
            masks = sb(nm + "masks", [P, LEVELS, P])
            inat = sb(nm + "inat", [P, MIX])
            knat = sb(nm + "knat", [P, MIX])
            st = sb(nm + "state", [P, MIX])
            fg = sb(nm + "fg", [P, D])
            ssq = sb(nm + "ssq", [P, 16])
            ms6 = sb(nm + "ms6", [P, 16])
            rs6 = sb(nm + "rs6", [P, 16])
            fs = sb(nm + "fs", [P, 2])
            fm = sb(nm + "fm", [P, 2])
            fr = sb(nm + "fr", [P, 2])

        def units(j, first_block, p):
            out = [cross_unit(xq[p], mem_kT[:, l], mem_v[:, l], HA if band else 0)]
            if band:
                n = j + 1 if first_block else 5
                keys = [(kcur, vcur, i) for i in range(j + 1)]
                if not first_block:
                    keys = [(kprev, vprev, i) for i in range(j, 4)] + keys
                for h in range(HA):
                    g, po = h // 2, HD * (h % 2)
                    score, at = [], 0
                    while at < n:
                        end = at + 1
                        while end < n and keys[end][0] is keys[at][0] and end != 4:
                            end += 1
                        slot = keys[at][2]
                        score.append((slice(at * P, end * P), ALL, q[p][po:po + HD, g],
                                      keys[at][0][po:po + HD, g, slot * P:(slot + end - at) * P]))
                        at = end
                    out.append(Unit(h * HD, n, (n + 1) // 2, score, bias[:, h, (5 - n) * P:],
                                    [(ALL, i, ALL, keys[i][1][:, keys[i][2], h * HD:(h + 1) * HD]) for i in range(n)],
                                    at=slice(h, h + 1)))
            return out

        def d_pre(t):
            return t * PER_D - 1 if not (isinstance(t, int) and t == 0) else 0

        def d_y(t):
            if isinstance(t, int) and t == NT:
                return NT * PER_D - 1
            return t * PER_D + (PRE - 1)

        def d_mid(t):
            return t * PER_D + PRE

        def d_unit(t, u):
            return t * PER_D + (PRE + MID + u)

        def a_pre(t):
            return t * PER_A

        def a_y(t):
            if isinstance(t, int) and t == NT:
                return NT * PER_A
            return t * PER_A + PRE

        def a_unit(t, u):
            return t * PER_A + (PRE + MID + u)

        def bank(p, u):
            return (p * U + u) % 2 if band else 0

        def pt_of(p, u):
            return y if band and u == 0 else pt[bank(p, u)]

        def tiles(eng, body):
            for j in range(4):
                body(j, j, 0)
            with eng.Fori(1, NT // 4) as b:
                for j in range(4):
                    body(b * 4 + j, j, b)

        with nc.Block() as block:
            @block.sync
            def _(sp):
                if not band:
                    sp.dma_start(fg[:], bass.AP(v["final_g"].tensor, 0, [[0, P], [1, D]])).then_inc(S["ldf"], 16)

                def cols(g, n, t):
                    return proj[g:g + n, :, bass.ds(t * P, P)].rearrange("g p n -> p g n")

                def body(t, j, b):
                    first = isinstance(b, int)
                    p = j % 2
                    if band:
                        wait(sp, S["sc"], (t - 1) * U)
                        sp.dma_start(xq[p][:], cols(GX, 2, t)).then_inc(s_ld[p], 16)
                        sp.dma_start(q[p][:], cols(GQ, MG, t)).then_inc(s_ld[p], 16)
                    else:
                        wait(sp, S["pv"], t - 1)
                        for buf, src in ((q, cols(GQ, MG, t)), (t1, cols(GK, MG, t)),
                                         (k1, v["kgate"][:, :, bass.ds(t * P, P)].rearrange("g p n -> p g n"))):
                            sp.dma_start(buf[p][:].rearrange("p (g n) -> p g n", n=P), src).then_inc(s_ld[p], 16)
                        sp.dma_start(xq[p][:], cols(GX, 2, t)).then_inc(s_ld[p], 16)
                    if not (isinstance(t, int) and t == 0):
                        sp.wait_ge(S["tp"], d_pre(t - 1) + 1)
                    sp.dma_start(tT[:], cols(GV, MG, t)).then_inc(s_ld[p], 16)
                    if band:
                        if not first:
                            moved, scored = counted(sp, t - 3), counted(sp, t * U)
                            sp.wait_ge(S["kc"], moved)
                            if j == 0:
                                sp.wait_ge(S["sc"], scored)
                        sp.dma_start(kcur[:, :, j * P:(j + 1) * P], cols(GK, MG, t)).then_inc(s_ldk[p], 16)
                    load_x(t, p)
                    if not (isinstance(t, int) and t == 0):
                        sp.wait_ge(S["evd"], d_y(t) + 1)
                    sp.dma_start(gt[:], cols(GG, KD, t)).then_inc(S["ldg"], 16)

                def load_x(t, p):
                    if not (isinstance(t, int) and t < 2):
                        sp.wait_ge(s_stx[p], (t - p) * 8)
                    sp.dma_start(xt[p][:], v["x_of"](t)).then_inc(s_ldx[p], 16)
                tiles(sp, body)
                load_x(NT, 0)
                sp.wait_ge(S["evd"], d_y(NT) + 1)
                sp.dma_start(gt[:], cols(GG, KD, NT)).then_inc(S["ldg"], 16)

            def out_of(t):
                if band:
                    return v["x_mid"][t]
                if isinstance(t, int) and t == NT:
                    return v["y_sample"].rearrange("b s d -> (b s) d")
                return v["y_prompt"].rearrange("b (t p) d -> (b t) p d", p=P)[t]

            def level_masks(pool):
                link = Chain(pool, S["init"])
                link(nc.gpsimd.memset(masks[:], 1.0))
                link(nc.gpsimd.affine_select(out=masks[:, 0], in_=masks[:, 0], compare_op=ALU.is_equal, fill=0.0,
                                             base=0, pattern=[[-1, P]], channel_multiplier=1))
                for i in range(1, LEVELS):
                    m = 1 << (i - 1)
                    nb = P // (2 * m)
                    whole = masks[:, i]
                    view = whole.rearrange("p (b two m) -> p b two m", two=2, m=m)
                    link(nc.gpsimd.memset(view[:, :, 0, :], 0.0))
                    sel = view[:, :, 1, :]
                    link(nc.gpsimd.affine_select(out=sel, in_=sel, compare_op=ALU.is_ge, fill=0.0, base=0,
                                                 pattern=[[-2 * m, nb], [0, m]], channel_multiplier=1))
                    link(nc.gpsimd.affine_select(out=sel, in_=sel, compare_op=ALU.is_ge, fill=0.0, base=m - 1,
                                                 pattern=[[2 * m, nb], [0, m]], channel_multiplier=-1))
                link(nc.gpsimd.memset(am[0][:], 0.0))
                link(nc.gpsimd.memset(am[1][:], 0.0))
                link(nc.gpsimd.memset(st[:], 0.0))

            @block.gpsimd
            def _(pool):
                if band:
                    nc.gpsimd.memset(bias[64:P, :, 0:CHUNK], BIG)
                    nc.gpsimd.memset(bias[0:64, :, BAND - CHUNK:], BIG).then_inc(S["bias"], 1)
                else:
                    level_masks(pool)

                def store(t, p):
                    pool.wait_ge(S["xadd" if band else "out"], t + 1)
                    pool.dma_start(out_of(t), xt[p][:]).then_inc(s_stx[p], 16)

                def final_power(n):
                    pool.wait_ge(S["fms"], n)
                    nc.gpsimd.tensor_tensor(fr[:, 0:1], fm[:, 0:1], neg_half[:, 0:1], ALU.pow).then_inc(S["frs"], 1)

                def final_gain(n, p):
                    scaled = counted(pool, n)
                    pool.wait_ge(S["ldf"], 16)
                    pool.wait_ge(S["fsc"], scaled)
                    nc.gpsimd.tensor_tensor(xt[p][:], xt[p][:], fg[:], ALU.mult).then_inc(S["out"], 1)

                def body(t, j, b):
                    p = j % 2
                    if band:
                        store(t, p)
                        return
                    has_prev = not (isinstance(t, int) and t == 0)
                    if has_prev:
                        final_power(t)
                    pool.wait_ge(S["oms"], t + 1)
                    wait(pool, S["o"], t)
                    nc.gpsimd.tensor_tensor(rs6[:, 0:MG], ms6[:, 0:MG], neg_half[:, 0:MG], ALU.pow).then_inc(S["ors"], 1)
                    if has_prev:
                        final_gain(t, 1 - p)
                        store(t - 1, 1 - p)
                tiles(pool, body)
                if not band:
                    final_power(NT)
                    final_gain(NT, 1)
                    store(NT - 1, 1)
                    final_power(NT + 1)
                    final_gain(NT + 1, 0)
                store(NT, 0)
                if not band:
                    pool.wait_ge(S["s"], NT)
                    pool.dma_start(v["b_state_prompt"][0, 0].rearrange("h k v -> k h v"),
                                   st[:].rearrange("k (h v) -> k h v", v=P)).then_inc(s_stx[1], 16)
                pool.wait_ge(s_stx[0], 16 * (NT // 2 + 1))
                pool.wait_ge(s_stx[1], 16 * (NT // 2 + (0 if band else 1)))

            N_INIT = 2 + 3 * (LEVELS - 1) + 3

            def q_of(m, p):
                return q[p] if m == 0 else qm[m]

            def k_of(m, p):
                return k1[p] if m <= 1 else km[m]

            def t_of(m, p):
                return t1[p] if m == 1 else tm[m]

            @block.tensor
            def _(pe):
                def turn_outputs(t, src, sample=False):
                    if not sample:
                        pe.wait_ge(S["o"], t)
                    pe.wait_ge(S["evd"], d_y(t) if not sample else d_y(t) + 1)
                    pe.wait_ge(S["eva"], a_y(t))
                    for k in range(KD):
                        ins = nc.tensor.transpose(TP[:, k * P:(k + 1) * P], src[:, k * P:(k + 1) * P], ident[:])
                    ins.then_inc(S["tp"], 1)

                def project_half(n, c):
                    pe.wait_ge(S["yh"], n * 2 + (c - 1))
                    for low in (False, True):
                        if low:
                            pe.wait_ge(S["yl"], n * 2 + (c - 1))
                        for half in range(2):
                            cols = slice(half * 512, half * 512 + 512)
                            for k in range(4 * c, 4 * c + 4):
                                for a, w in ([(yl, woh)] if low else [(yh, woh), (yh, wol)]):
                                    ins = nc.tensor.matmul(OB[:, cols], a[:, k], w[:, k, cols],
                                                           start=(k == 0 and a is yh and w is woh), stop=(k == KD - 1 and low))
                    if c:
                        ins.then_inc(S["op"], 1)

                def body(t, j, b):
                    first = isinstance(b, int)
                    p = j % 2
                    us = units(j, first, p)
                    has_prev = not (isinstance(t, int) and t == 0)

                    def scores(u):
                        if band:
                            wait(pe, S["exp"], t * U + (u - 1))
                        else:
                            pe.wait_ge(S["cp"], t * 16 + 14)
                        unit_scores(nc, us[u], SC[bank(p, u)]).then_inc(S["sc"], 1)

                    def values(u):
                        pe.wait_ge(S["eva"], a_unit(t, u) + 1)
                        pe.wait_ge(S["evd"], d_unit(t, u) + 1)
                        if u == 0 and has_prev:
                            pe.wait_ge(S["xadd"], t)
                        ins = unit_pv(nc, us[u], pt_of(p, u), OB)
                        if u == U - 1:
                            ins.then_inc(S["pv"], 1)

                    def turn(srcs, n_d, n_a):
                        wait(pe, S["evd"], n_d)
                        wait(pe, S["eva"], n_a)
                        for g in range(MG):
                            at = (g % 3) * P + 512 * (g // 3)
                            ins = nc.tensor.transpose(TP[:, at:at + P], srcs(g), ident[:])
                        ins.then_inc(S["tp"], 1)

                    pe.wait_ge(s_ld[p], (t - p) * 8 * LOADS + 16 * LOADS)
                    turn(lambda g: tT[:, g], d_pre(t), a_pre(t))
                    if band:
                        scores(0)
                        if has_prev:
                            turn_outputs(t, o)
                        pe.wait_ge(s_ldk[p], (t - p) * 8 + 16)
                        if has_prev:
                            pe.wait_ge(S["kc"], t)
                        scores(1)
                        if has_prev:
                            project_half(t, 0)
                            project_half(t, 1)
                        for u in range(U):
                            pe.wait_ge(S["exp"], t * U + (u + 1))
                            pe.wait_ge(S["eva"], a_unit(t, u))
                            pe.wait_ge(S["evd"], d_unit(t, u))
                            unit_transposes(nc, us[u], se[bank(p, u)], TP, ident).then_inc(S["tp"], 1)
                            if u:
                                values(u - 1)
                            elif has_prev:
                                pe.wait_ge(S["vc"], t)
                            if u + 2 < U:
                                scores(u + 2)
                        values(U - 1)
                        return

                    def level(i):
                        m = 0 if i == 0 else 1 << (i - 1)
                        if i == 0:
                            wait(pe, S["exp"], t)
                        elif i == 1:
                            wait(pe, S["s"], t)
                        else:
                            pe.wait_ge(S["cp"], t * 16 + 2 * (i - 1))
                        if i:
                            pe.wait_ge(S["hst"], t * 8 + i)
                        if i > 1:
                            pe.wait_ge(S["hcp"], t * 7 + (i - 1))
                        for h in range(MG):
                            at = (h % 3) * P + 512 * (h // 3)
                            hs = slice(h * P, (h + 1) * P)
                            ins = nc.tensor.matmul(SC[i % 2][:, at:at + P], k_of(m, p)[:, hs], q_of(m, p)[:, hs],
                                                   start=True, stop=True)
                            if h % 3 == 2:
                                ins.then_inc(S["lv"], 1)
                    level(0)
                    level(1)
                    level(2)
                    if has_prev:
                        turn_outputs(t, o)
                    level(3)
                    if has_prev:
                        project_half(t, 0)
                    level(4)
                    level(5)
                    if has_prev:
                        project_half(t, 1)
                    level(6)
                    level(7)
                    scores(0)
                    pe.wait_ge(S["hst"], t * 8 + 8)
                    pe.wait_ge(S["hcp"], t * 7 + 7)
                    turn(lambda g: km[128][:, g * P:(g + 1) * P], d_mid(t), t * PER_A + PRE)
                    pe.wait_ge(S["cp"], t * 16 + 16)
                    if has_prev:
                        pe.wait_ge(S["xadd"], t)
                        pe.wait_ge(S["s"], t)
                    else:
                        pe.wait_ge(S["init"], N_INIT)
                    for h in range(MG):
                        hs = slice(h * P, (h + 1) * P)
                        nc.tensor.matmul(OB[:, hs], am[p][:, hs], inat[:, hs], start=True, stop=False)
                        ins = nc.tensor.matmul(OB[:, hs], qm[128][:, hs], st[:, hs], start=False, stop=True)
                    ins.then_inc(S["hv"], 1)
                    pe.wait_ge(S["evd"], d_mid(t) + 1)
                    pe.wait_ge(S["eva"], t * PER_A + (PRE + 1))
                    pe.wait_ge(S["exp"], t + 1)
                    unit_transposes(nc, us[0], se[0], TP, ident).then_inc(S["tp"], 1)
                    for h in range(MG):
                        at = (h % 3) * P + 512 * (h // 3)
                        hs = slice(h * P, (h + 1) * P)
                        ins = nc.tensor.matmul(SC[1][:, at:at + P], knat[:, hs], inat[:, hs], start=True, stop=True)
                    ins.then_inc(S["kv"], 1)
                    values(0)

                tiles(pe, body)
                turn_outputs(NT, o)
                project_half(NT, 0)
                project_half(NT, 1)
                turn_outputs(NT, o_s, sample=True)
                pe.wait_ge(S["xadd"], NT)
                project_half(NT + 1, 0)
                project_half(NT + 1, 1)

            @block.vector
            def _(dve):
                def outputs(t):
                    dve.wait_ge(S["pv"], t)
                    n = HA + HX if band else HX
                    nc.vector.reciprocal(rs[:, 0:n], tot[:, 0:n]).then_inc(S["rs"], 1)
                    dve.wait_ge(S["rs"], t)
                    for at, heads in ((0, 8), (8, 8)) if band else ((HA, HX),):
                        cs = slice(at * HD, (at + heads) * HD)
                        of = at if band else 0
                        ins = nc.vector.tensor_tensor(o[:, cs].rearrange("p (h d) -> p h d", d=HD),
                                                      OB[:, cs].rearrange("p (h d) -> p h d", d=HD),
                                                      rs[:, of:of + heads].unsqueeze(2).to_broadcast([P, heads, HD]), ALU.mult)
                    ins.then_inc(S["o"], 1)

                def outputs_copy(t):
                    dve.wait_ge(S["hv"], t + 1)
                    nc.vector.tensor_copy(o[:, 512:MIX], OB[:, 512:MIX]).then_inc(S["ocp"], 1)

                def outputs_mean(t):
                    dve.wait_ge(S["osq"], t + 1)
                    nc.vector.tensor_scalar(ms6[:, 0:MG], ssq[:, 0:MG], 1.0 / P, EPS, ALU.mult, ALU.add).then_inc(S["oms"], 1)

                def outputs_norm(t):
                    dve.wait_ge(S["ors"], t + 1)
                    for c in range(2):
                        hs, cs = slice(c * 4, 4 + c * 2), slice(c * 512, 512 + c * 256)
                        nc.vector.tensor_tensor(o[:, cs].rearrange("p (h d) -> p h d", d=P),
                                                (o if c else OB)[:, cs].rearrange("p (h d) -> p h d", d=P),
                                                rs6[:, hs].unsqueeze(2).to_broadcast([P, 4 - 2 * c, P]), ALU.mult)

                def gate(t, sample=False):
                    n = t + 1 if sample else t
                    dve.wait_ge(S["tp"], d_y(t) + (2 if sample else 1))
                    dve.wait_ge(S["ldg"], n * 16)
                    for c in range(2):
                        cs = slice(c * 512, (c + 1) * 512)
                        nc.vector.tensor_tensor(y[:, cs], TP[:, cs], gt[:, 4 * c:4 * c + 4].rearrange("p k n -> p (k n)"),
                                                ALU.mult).then_inc(S["evd" if c else "yg"], 1)

                def low_parts(n):
                    for c in range(2):
                        cs = slice(c * 512, (c + 1) * 512)
                        dve.wait_ge(S["yh"], n * 2 + (c - 1))
                        nc.vector.tensor_tensor(yl[:, 4 * c:4 * c + 4].rearrange("p k n -> p (k n)"), y[:, cs],
                                                yh[:, 4 * c:4 * c + 4].bitcast(F32).rearrange("p k n -> p (k n)"),
                                                ALU.subtract).then_inc(S["yl"], 1)

                def add(n, p):
                    dve.wait_ge(S["op"], n)
                    dve.wait_ge(s_ldx[p], (n - 1 - p) * 8 + 16)
                    for c in range(2):
                        ins = nc.vector.tensor_tensor(xt[p][:, c * 512:(c + 1) * 512], xt[p][:, c * 512:(c + 1) * 512],
                                                      OB[:, c * 512:(c + 1) * 512], ALU.add)
                    ins.then_inc(S["xadd"], 1)

                def final_mean(n):
                    dve.wait_ge(S["fsq"], n)
                    wait(dve, S["frs"], n - 1)
                    nc.vector.tensor_scalar(fm[:, 0:1], fs[:, 0:1], 1.0 / D, EPS, ALU.mult, ALU.add).then_inc(S["fms"], 1)

                def body(t, j, b):
                    first = isinstance(b, int)
                    p = j % 2
                    us = units(j, first, p)
                    has_prev = not (isinstance(t, int) and t == 0)

                    def low_min(u):
                        scored = counted(dve, t * U + (u + 1))
                        if band:
                            dve.wait_ge(S["bias"], 1)
                        dve.wait_ge(S["sc"], scored)
                        unit_min(nc, us[u], SC[bank(p, u)], se[bank(p, u)], mn[:, us[u].at]).then_inc(S["min"], 1)
                    if not band:
                        dve.wait_ge(s_ld[p], (t - p) * 8 * LOADS + 16 * LOADS)
                        nc.vector.tensor_tensor(qm[1][:], q[p][:], t1[p][:], ALU.mult).then_inc(S["hst"], 1)
                    elif has_prev:
                        outputs(t)
                    if band and has_prev:
                        i = (j - 1) % 4
                        nc.vector.tensor_copy(vprev[:, i], vcur[:, i]).then_inc(S["vc"], 1)
                        wait(dve, S["vc"], t - 1)
                    dve.wait_ge(S["tp"], d_pre(t) + 1)
                    dst = vcur[:, j] if band else inat[:]
                    nc.vector.tensor_copy(dst[:, 384:MIX], TP[:, 512:896]).then_inc(S["evd"], 1)
                    if band:
                        low_min(0)
                        if has_prev:
                            gate(t)
                            low_parts(t)
                        low_min(1)
                        if has_prev:
                            add(t, 1 - p)
                        for u in range(U):
                            dve.wait_ge(S["tp"], d_unit(t, u) + 1)
                            unit_evac_high(us[u], nc.vector.tensor_copy, pt_of(p, u), TP).then_inc(S["evd"], 1)
                            if u + 2 < U:
                                low_min(u + 2)
                    else:
                        def step(i):
                            m = 1 << (i - 1)
                            dve.wait_ge(S["hst"], t * 8 + i)
                            wait(dve, S["hcp"], t * 7 + (i - 1))
                            n = MIX // (2 * m)

                            def two(a, width=m):
                                return a[:].rearrange("p (n two m) -> p n two m", two=2, m=width)
                            tot_m = two(t_of(m, p), 1)
                            nc.vector.tensor_tensor(two(qm[2 * m])[:, :, 1], two(q_of(m, p))[:, :, 1],
                                                    tot_m[:, :, 0].to_broadcast([P, n, m]), ALU.mult)
                            nc.vector.tensor_tensor(two(km[2 * m])[:, :, 0], two(k_of(m, p))[:, :, 0],
                                                    tot_m[:, :, 1].to_broadcast([P, n, m]), ALU.mult)
                            nc.vector.tensor_tensor(tm[2 * m][:].unsqueeze(2), tot_m[:, :, 0], tot_m[:, :, 1], ALU.mult
                                                    ).then_inc(S["hst"], 1)

                        def place(i):
                            for c in range(2):
                                made = counted(dve, t * 16 + (2 * i + c + 1))
                                placed = counted(dve, t * 16 + (2 * i + c - 1))
                                dve.wait_ge(S["init"], N_INIT)
                                dve.wait_ge(S["lv"], made)
                                if i:
                                    dve.wait_ge(S["cp"], placed)
                                hs = slice(c * 384, c * 384 + 384)
                                nc.vector.copy_predicated(am[p][:, hs].rearrange("p (h n) -> p h n", n=P),
                                                          masks[:, i:i + 1].bitcast(U32).to_broadcast([P, 3, P]),
                                                          SC[i % 2][:, 512 * c:512 * c + 384].rearrange("p (h n) -> p h n", n=P)
                                                          ).then_inc(S["cp"], 1)
                        step(1)
                        place(0)
                        if has_prev:
                            outputs_norm(t - 1)
                            outputs(t)
                        step(2)
                        place(1)
                        if has_prev:
                            gate(t)
                        step(3)
                        place(2)
                        if has_prev:
                            low_parts(t)
                        for i in range(4, LEVELS):
                            step(i)
                            place(i - 1)
                        if has_prev:
                            add(t, 1 - p)
                        place(LEVELS - 1)
                        if has_prev:
                            final_mean(t)
                        low_min(0)
                        dve.wait_ge(S["tp"], d_mid(t) + 1)
                        nc.vector.tensor_copy(knat[:, 384:MIX], TP[:, 512:896]).then_inc(S["evd"], 1)
                        outputs_copy(t)
                        dve.wait_ge(S["tp"], d_unit(t, 0) + 1)
                        unit_evac_high(us[0], nc.vector.tensor_copy, pt[0], TP).then_inc(S["evd"], 1)
                        outputs_mean(t)
                        dve.wait_ge(S["kv"], t + 1)
                        for h in range(MG):
                            at = (h % 3) * P + 512 * (h // 3)
                            hs = slice(h * P, (h + 1) * P)
                            ins = nc.vector.scalar_tensor_tensor(out=st[:, hs], in0=st[:, hs], scalar=tm[128][:, h:h + 1],
                                                                 in1=SC[1][:, at:at + P], op0=ALU.mult, op1=ALU.add)
                        ins.then_inc(S["s"], 1)
                tiles(dve, body)
                if not band:
                    outputs_norm(NT - 1)
                outputs(NT)
                gate(NT)
                low_parts(NT)
                add(NT, 1)
                if not band:
                    final_mean(NT)
                gate(NT, sample=True)
                low_parts(NT + 1)
                add(NT + 1, 0)
                if not band:
                    final_mean(NT + 1)

            @block.scalar
            def _(act):
                def y_high(n, sample=False):
                    act.wait_ge(S["yg"], n)
                    for c in range(2):
                        if c:
                            act.wait_ge(S["evd"], d_y(NT) + 2 if sample else d_y(n) + 1)
                        nc.scalar.copy(yh[:, 4 * c:4 * c + 4].rearrange("p k n -> p (k n)"), y[:, c * 512:(c + 1) * 512]
                                       ).then_inc(S["yh"], 1)

                def final_square(n, p):
                    act.wait_ge(S["xadd"], n)
                    wait(act, S["fms"], n - 1)
                    nc.scalar.activation(y[:], xt[p][:], ACT.Square, accum_out=fs[:, 0:1]).then_inc(S["fsq"], 1)

                def final_scale(n, p):
                    act.wait_ge(S["frs"], n)
                    nc.scalar.mul(xt[p][:], xt[p][:], fr[:, 0:1]).then_inc(S["fsc"], 1)

                def out_square(t):
                    act.wait_ge(S["hv"], t + 1)
                    wait(act, S["fsq"], t)
                    for h in range(MG):
                        hs = slice(h * P, (h + 1) * P)
                        if h == 4:
                            act.wait_ge(S["ocp"], t + 1)
                        ins = nc.scalar.activation(y[:, hs], (OB if h < 4 else o)[:, hs], ACT.Square,
                                                   accum_out=ssq[:, h:h + 1])
                    ins.then_inc(S["osq"], 1)

                def body(t, j, b):
                    first = isinstance(b, int)
                    p = j % 2
                    us = units(j, first, p)
                    has_prev = not (isinstance(t, int) and t == 0)

                    def exp(u):
                        act.wait_ge(S["min"], t * U + (u + 1))
                        unit_exp(nc, us[u], SC[bank(p, u)], se[bank(p, u)], mn[:, us[u].at], tot[:, us[u].at]
                                 ).then_inc(S["exp"], 1)
                    act.wait_ge(S["tp"], d_pre(t) + 1)
                    if band:
                        wait(act, S["vc"], t - 1)
                    dst = vcur[:, j] if band else inat[:]
                    nc.scalar.copy(dst[:, 0:384], TP[:, 0:384]).then_inc(S["eva"], 1)
                    if band:
                        if has_prev:
                            i = (j - 1) % 4
                            nc.scalar.copy(kprev[:, :, i * P:(i + 1) * P], kcur[:, :, i * P:(i + 1) * P]).then_inc(S["kc"], 1)
                            y_high(t)
                        exp(0)
                        exp(1)
                        for u in range(U):
                            act.wait_ge(S["tp"], d_unit(t, u) + 1)
                            unit_evac_low(us[u], nc.scalar.copy, pt_of(p, u), TP).then_inc(S["eva"], 1)
                            if u + 2 < U:
                                exp(u + 2)
                    else:
                        act.wait_ge(s_ld[p], (t - p) * 8 * LOADS + 16 * LOADS)

                        def carry(i):
                            m = 1 << (i - 1)
                            act.wait_ge(S["hst"], t * 8 + i)
                            wait(act, S["hcp"], t * 7 + (i - 1))

                            def two(a):
                                return a[:].rearrange("p (n two m) -> p n two m", two=2, m=m)
                            nc.scalar.copy(two(qm[2 * m])[:, :, 0], two(q_of(m, p))[:, :, 0])
                            nc.scalar.copy(two(km[2 * m])[:, :, 1], two(k_of(m, p))[:, :, 1]).then_inc(S["hcp"], 1)
                        carry(1)
                        carry(2)
                        if has_prev:
                            y_high(t)
                        for i in range(3, LEVELS):
                            carry(i)
                        if has_prev:
                            final_square(t, 1 - p)
                        act.wait_ge(S["tp"], d_mid(t) + 1)
                        nc.scalar.copy(knat[:, 0:384], TP[:, 0:384]).then_inc(S["eva"], 1)
                        exp(0)
                        if has_prev:
                            final_scale(t, 1 - p)
                        act.wait_ge(S["tp"], d_unit(t, 0) + 1)
                        unit_evac_low(us[0], nc.scalar.copy, pt[0], TP).then_inc(S["eva"], 1)
                        out_square(t)
                tiles(act, body)
                y_high(NT)
                if not band:
                    final_square(NT, 1)
                    final_scale(NT, 1)
                y_high(NT + 1, sample=True)
                if not band:
                    final_square(NT + 1, 0)
                    final_scale(NT + 1, 0)


_INS = ['x_prompt', 'x_sample', 'cache_a_k', 'cache_a_v', 'state_b', 'cache_mem_k', 'cache_mem_v', 'mem_prompt',
        'ln_g', 'w_in', 'w_out', 'rel_bias_table', 'lower_bounds', 'hgrn_norm_g', 'mem_norm_g', 'w_mem_kv', 'final_g']
_OUTS = [(1, 2048, 1024), (8, 16, 1024), (1, 1, 512, 12, 64), (1, 1, 512, 12, 64), (1, 1, 6, 128, 128),
         (2, 1, 256, 4, 64), (2, 1, 256, 4, 64), (1, 8, 16, 12, 64), (1, 8, 16, 12, 64), (1, 8, 6, 128, 128)]


def kernel(**inputs):
    import numpy as _np
    import concourse.bacc as _bacc
    from concourse import mybir as _mybir
    from concourse.bass_utils import run_bass_kernel_spmd as _run

    nc = _bacc.Bacc("TRN2", target_bir_lowering=False, num_devices=1)
    arrays, args = {}, []
    for name in _INS:
        a = _np.ascontiguousarray(inputs[name])
        arrays[f"in_{name}_dram"] = a
        args.append(nc.dram_tensor(f"in_{name}_dram", a.shape, _mybir.dt.from_np(a.dtype), kind="ExternalInput").ap())
    for i, shape in enumerate(_OUTS):
        args.append(nc.dram_tensor(f"out_{i}_dram", shape, F32, kind="ExternalOutput").ap())
    hybrid_encoder(nc, *args)
    r = _run(nc, [arrays], core_ids=[0])
    return tuple(r.results[0][f"out_{i}_dram"] for i in range(len(_OUTS)))
```
